# Optimizing a Trainium2 kernel written in Bass

```python
import math
import jax, jax.numpy as jnp
from jax import lax
import numpy as np

D_MODEL = 2048
BATCH = 1
SEQ = 256
DEPTH = 2
DEC_BATCH = 8
DEC_SEQ = 8
PAST_LEN = 2048
PAGE_SIZE = 128

N_A_LAYERS = DEPTH // 2
N_B_LAYERS = DEPTH - N_A_LAYERS
HEAD_SIZE_A = 64
N_HEADS_A = D_MODEL // HEAD_SIZE_A
D_DECAY_LORA = max(32, int(round(1.8 * math.sqrt(D_MODEL) / 32)) * 32)
D_AAA_LORA = max(32, int(round(1.8 * math.sqrt(D_MODEL) / 32)) * 32)
HEAD_DIM_B = 128
N_HEADS_B = D_MODEL // HEAD_DIM_B
Q_BLOCK = 128
RMS_EPS = 1e-6
LNX_EPS = 64e-5

kernel_name = "rwkv7_yoco_stickbreaking_step"

def _rmsnorm(x, g):
    xf = x.astype(jnp.float32)
    y = xf * lax.rsqrt(jnp.mean(xf * xf, axis=-1, keepdims=True) + RMS_EPS)
    return (y * g.astype(jnp.float32)).astype(x.dtype)

def _wkv7_scan(S0, r, w, k, v, kk, a):
    def step(S, inp):
        r_t, w_t, k_t, v_t, kk_t, a_t = inp
        sa = jnp.einsum("bhvk,bhk->bhv", S, -kk_t)
        S = (S * w_t[:, :, None, :] + sa[..., None] * (kk_t * a_t)[:, :, None, :]
             + v_t[..., None] * k_t[:, :, None, :])
        o_t = jnp.einsum("bhvk,bhk->bhv", S, r_t)
        return S, o_t
    seq = tuple(jnp.moveaxis(t, 1, 0) for t in (r, w, k, v, kk, a))
    S, o = lax.scan(step, S0, seq)
    return jnp.moveaxis(o, 0, 1), S

def _rwkv7_mix(h, shift_prev, S0, mu, w_rkvg, w0, w1, w2, a0, a1, a2,
               k_k, k_a, r_k, lnx_g, lnx_b, w_o):
    B, T, D = h.shape
    f32 = jnp.float32
    H, N = N_HEADS_A, HEAD_SIZE_A
    h_prev = jnp.concatenate([shift_prev[:, None, :].astype(h.dtype), h[:, :-1]], axis=1)
    xs = h[None] + (h_prev - h)[None] * mu[:, None, None, :].astype(h.dtype)
    r, k, v, g = jnp.einsum("pbtd,pde->pbte", xs[:4], w_rkvg)
    w_raw = -jax.nn.softplus(-(w0 + jnp.tanh(xs[4] @ w1) @ w2).astype(f32)) - 0.5
    decay = jnp.exp(-jnp.exp(w_raw))
    a = jax.nn.sigmoid((a0 + (xs[5] @ a1) @ a2).astype(f32))
    heads = lambda t: t.astype(f32).reshape(B, T, H, N)
    r, k, v, decay, a = heads(r), heads(k), heads(v), heads(decay), heads(a)
    kk = k * k_k.astype(f32).reshape(H, N)
    kk = kk / jnp.maximum(jnp.sqrt(jnp.sum(kk * kk, axis=-1, keepdims=True)), 1e-12)
    k = k * (1.0 + (a - 1.0) * k_a.astype(f32).reshape(H, N))
    o, S = _wkv7_scan(S0.astype(f32), r, decay, k, v, kk, a)
    mean = jnp.mean(o, axis=-1, keepdims=True)
    var = jnp.mean(jnp.square(o - mean), axis=-1, keepdims=True)
    o = ((o - mean) * lax.rsqrt(var + LNX_EPS) * lnx_g.astype(f32).reshape(H, N)
         + lnx_b.astype(f32).reshape(H, N))
    o = o + jnp.sum(r * k * r_k.astype(f32), axis=-1, keepdims=True) * v
    o = o.reshape(B, T, D).astype(h.dtype) * jax.nn.silu(g)
    return o @ w_o, h[:, -1], S.astype(S0.dtype)

def _shared_kv(h, kv_norm, w_kv):
    B, T, _ = h.shape
    k, v = jnp.split(_rmsnorm(h, kv_norm) @ w_kv, 2, axis=-1)
    return (k.reshape(B, T, N_HEADS_B, HEAD_DIM_B), v.reshape(B, T, N_HEADS_B, HEAD_DIM_B))

def _stick_breaking(q, k, v, q_pos, k_pos, logit_bias):
    f32 = jnp.float32
    B, Tq, H, d = q.shape
    qb_size = Q_BLOCK if Tq % Q_BLOCK == 0 else Tq
    nb = Tq // qb_size
    scale = 1.0 / math.sqrt(d)
    kf, vf = k.astype(f32), v.astype(f32)
    bias = logit_bias.astype(f32)[None, :, None, None]
    qb = jnp.moveaxis(q.reshape(B, nb, qb_size, H, d), 1, 0)
    pb = q_pos.reshape(nb, qb_size)

    def block(args):
        q_i, p_i = args
        z = jnp.einsum("bqhd,bkhd->bhqk", q_i.astype(f32), kf) * scale + bias
        mask = (k_pos[None, :] < p_i[:, None])[None, None]
        log_keep = jnp.where(mask, jax.nn.log_sigmoid(-z), 0.0)
        log_rest = lax.cumsum(log_keep, axis=3, reverse=True) - log_keep
        att = jnp.where(mask, jnp.exp(jax.nn.log_sigmoid(z) + log_rest), 0.0)
        return jnp.einsum("bhqk,bkhd->bqhd", att, vf)

    o = lax.map(block, (qb, pb))
    return jnp.moveaxis(o, 0, 1).reshape(B, Tq, H, d).astype(q.dtype)

def _sb_mix(h, k, v, q_pos, k_pos, w_qg, logit_bias, w_o):
    B, T, D = h.shape
    q, g = jnp.split(h @ w_qg, 2, axis=-1)
    o = _stick_breaking(q.reshape(B, T, N_HEADS_B, HEAD_DIM_B), k, v, q_pos, k_pos, logit_bias)
    return (o.reshape(B, T, D) * jax.nn.silu(g)) @ w_o

def setup_inputs(seed: int = 0) -> dict:
    key = jax.random.key(seed)
    ks = jax.random.split(key, 32)
    f32 = jnp.float32
    D = D_MODEL
    nrm = lambda i, shape: jax.random.normal(ks[i], shape, f32)
    n_pages = PAST_LEN // PAGE_SIZE
    n_used = DEC_BATCH * n_pages
    n_pool = n_used + max(1, n_used // 4)
    page_table = jax.random.permutation(ks[6], n_pool)[:n_used].reshape(DEC_BATCH, n_pages).astype(jnp.int32)
    return {
        "x_prompt": nrm(0, (BATCH, SEQ, D)),
        "x_sample": nrm(1, (DEC_BATCH, DEC_SEQ, D)),
        "state_shift": nrm(2, (N_A_LAYERS, DEC_BATCH, D)),
        "state_wkv": 0.1 * nrm(3, (N_A_LAYERS, DEC_BATCH, N_HEADS_A, HEAD_SIZE_A, HEAD_SIZE_A)),
        "cache_k": nrm(4, (n_pool, PAGE_SIZE, N_HEADS_B, HEAD_DIM_B)),
        "cache_v": nrm(5, (n_pool, PAGE_SIZE, N_HEADS_B, HEAD_DIM_B)),
        "page_table": page_table,
        "a_norm": 1.0 + 0.02 * nrm(7, (N_A_LAYERS, D)),
        "a_mu": jax.random.uniform(ks[8], (N_A_LAYERS, 6, D), f32),
        "a_w_rkvg": nrm(9, (N_A_LAYERS, 4, D, D)) * D ** -0.5,
        "a_w0": jax.random.uniform(ks[10], (N_A_LAYERS, D), f32, minval=-3.0, maxval=1.0),
        "a_w1": nrm(11, (N_A_LAYERS, D, D_DECAY_LORA)) * D ** -0.5,
        "a_w2": nrm(12, (N_A_LAYERS, D_DECAY_LORA, D)) * 0.1 * D_DECAY_LORA ** -0.5,
        "a_a0": 0.1 * nrm(13, (N_A_LAYERS, D)),
        "a_a1": nrm(14, (N_A_LAYERS, D, D_AAA_LORA)) * D ** -0.5,
        "a_a2": nrm(15, (N_A_LAYERS, D_AAA_LORA, D)) * 0.1 * D_AAA_LORA ** -0.5,
        "a_k_k": 0.85 + 0.05 * nrm(16, (N_A_LAYERS, D)),
        "a_k_a": 1.0 + 0.05 * nrm(17, (N_A_LAYERS, D)),
        "a_r_k": 0.1 * nrm(18, (N_A_LAYERS, N_HEADS_A, HEAD_SIZE_A)),
        "a_lnx_g": 1.0 + 0.02 * nrm(19, (N_A_LAYERS, D)),
        "a_lnx_b": 0.02 * nrm(20, (N_A_LAYERS, D)),
        "a_w_o": nrm(21, (N_A_LAYERS, D, D)) * D ** -0.5,
        "kv_norm": 1.0 + 0.02 * nrm(22, (D,)),
        "w_kv": nrm(23, (D, 2 * D)) * D ** -0.5,
        "b_norm": 1.0 + 0.02 * nrm(24, (N_B_LAYERS, D)),
        "b_w_qg": nrm(25, (N_B_LAYERS, D, 2 * D)) * D ** -0.5,
        "b_logit_bias": jax.random.uniform(ks[28], (N_B_LAYERS, N_HEADS_B), f32, minval=-10.0, maxval=-4.0),
        "b_w_o": nrm(26, (N_B_LAYERS, D, D)) * D ** -0.5,
        "final_norm": 1.0 + 0.02 * nrm(27, (D,)),
    }

def reference(x_prompt, x_sample, state_shift, state_wkv, cache_k, cache_v, page_table,
              a_norm, a_mu, a_w_rkvg, a_w0, a_w1, a_w2, a_a0, a_a1, a_a2, a_k_k, a_k_a,
              a_r_k, a_lnx_g, a_lnx_b, a_w_o, kv_norm, w_kv, b_norm, b_w_qg, b_logit_bias,
              b_w_o, final_norm):
    B, T, D = x_prompt.shape
    Bs, Ts, _ = x_sample.shape
    n_pages = page_table.shape[1]
    past_len = n_pages * cache_k.shape[1]
    pos_prompt = jnp.arange(T, dtype=jnp.int32)
    k_pos_sample = jnp.arange(past_len + Ts, dtype=jnp.int32)
    q_pos_sample = past_len + jnp.arange(Ts, dtype=jnp.int32)

    h_p, h_s = x_prompt, x_sample
    shift_p, wkv_p, shift_s, wkv_s = [], [], [], []
    k_p = v_p = k_s_new = v_s_new = k_s_all = v_s_all = None
    for i in range(DEPTH):
        if i < N_A_LAYERS:
            w_args = (a_mu[i], a_w_rkvg[i], a_w0[i], a_w1[i], a_w2[i], a_a0[i], a_a1[i], a_a2[i],
                      a_k_k[i], a_k_a[i], a_r_k[i], a_lnx_g[i], a_lnx_b[i], a_w_o[i])
            out_p, sh_p, S_p = _rwkv7_mix(_rmsnorm(h_p, a_norm[i]),
                                          jnp.zeros((B, D), x_prompt.dtype),
                                          jnp.zeros((B,) + state_wkv.shape[2:], state_wkv.dtype),
                                          *w_args)
            out_s, sh_s, S_s = _rwkv7_mix(_rmsnorm(h_s, a_norm[i]), state_shift[i], state_wkv[i],
                                          *w_args)
            h_p = h_p + out_p
            h_s = h_s + out_s
            shift_p.append(sh_p); wkv_p.append(S_p)
            shift_s.append(sh_s); wkv_s.append(S_s)
        else:
            if i == N_A_LAYERS:
                k_p, v_p = _shared_kv(h_p, kv_norm, w_kv)
                k_s_new, v_s_new = _shared_kv(h_s, kv_norm, w_kv)
                k_past = cache_k[page_table].reshape(Bs, past_len, N_HEADS_B, HEAD_DIM_B)
                v_past = cache_v[page_table].reshape(Bs, past_len, N_HEADS_B, HEAD_DIM_B)
                k_s_all = jnp.concatenate([k_past.astype(k_s_new.dtype), k_s_new], axis=1)
                v_s_all = jnp.concatenate([v_past.astype(v_s_new.dtype), v_s_new], axis=1)
            j = i - N_A_LAYERS
            h_p = h_p + _sb_mix(_rmsnorm(h_p, b_norm[j]), k_p, v_p, pos_prompt, pos_prompt,
                                b_w_qg[j], b_logit_bias[j], b_w_o[j])
            h_s = h_s + _sb_mix(_rmsnorm(h_s, b_norm[j]), k_s_all, v_s_all, q_pos_sample,
                                k_pos_sample, b_w_qg[j], b_logit_bias[j], b_w_o[j])

    y_prompt = _rmsnorm(h_p, final_norm)
    y_sample = _rmsnorm(h_s, final_norm)
    new_shift_prompt = jnp.stack(shift_p)
    new_wkv_prompt = jnp.stack(wkv_p)
    new_shift_sample = jnp.stack(shift_s)
    new_wkv_sample = jnp.stack(wkv_s)
    return (y_prompt, y_sample, new_shift_prompt, new_wkv_prompt, k_p, v_p,
            new_shift_sample, new_wkv_sample, k_s_new, v_s_new)


_drawn_inputs = setup_inputs


def setup_inputs(seed=0):
    import zlib

    import numpy as np

    out = dict(_drawn_inputs(seed))
    spreads = {}
    factors = {'a_w1': 5.793,
     'a_w2': 5.987,
     'a_k_k': 3.556,
     'a_lnx_g': 6.903,
     'a_lnx_b': 6.741,
     'kv_norm': 2.827,
     'b_norm': 8.0,
     'final_norm': 2.828}
    for name, (base, spread) in spreads.items():
        noise = np.random.default_rng([zlib.crc32(name.encode()), seed]).standard_normal(out[name].shape)
        drawn = base * np.exp(spread * noise) if base else spread * noise
        out[name] = __import__('jax').numpy.asarray(drawn.astype(out[name].dtype))
    for name, factor in factors.items():
        out[name] = (out[name] * factor).astype(out[name].dtype)
    return out
```

```python
import math
from contextlib import ExitStack

import concourse.bass as bass
from concourse import mybir

F32 = mybir.dt.float32
F32R = mybir.dt.float32r
I32 = mybir.dt.int32
ALU = mybir.AluOpType
ACT = mybir.ActivationFunctionType

P = 128
D = 2048
NM = D // P
SEQ, NB, TS = 256, 8, 8
TOK = SEQ + NB * TS
LORA = 96
NHB, DH = 16, 128
PAGE, NPAGE = 128, 16
L = 64
NCH = SEQ // L
RMS_EPS, LNX_EPS = 1e-6, 64e-5
DECAY = math.exp(-0.5)
SCALE = 1.0 / math.sqrt(DH)

VECS = ["a_norm", "kv_norm", "b_norm", "final_norm", "mu0", "mu1", "mu2", "mu3", "mu4", "mu5",
        "w0", "a0", "k_k", "k_a", "r_k", "lnx_g", "lnx_b"]
VEC = {n: i for i, n in enumerate(VECS)}

PROJ = ["r", "k", "v", "g", "wo", "kk", "kv", "q", "g2", "bo"]
PB = {n: i for i, n in enumerate(PROJ)}
GATED = ("g", "g2")
RESIDUAL = ("wo", "bo")
SPILL = [n for n in PROJ if n not in RESIDUAL] + ["s", "a"]
SP_I = {n: i for i, n in enumerate(SPILL)}

QC = 4
GW = 512
LEAD = 4


class Core:
    pass


def weight_buffers(nc, ctx, c_):
    def sb(name, shape):
        return ctx.enter_context(nc.sbuf_tensor(c_.name(name), shape, F32))

    c_.wraw = sb("wraw", [P, 4, QC, GW])
    c_.stage = sb("stage", [P, 4, TOK])
    c_.sig = sb("sig", [P, 4, TOK])
    c_.xtmp = sb("xtmp", [P, 2, 4, TOK])
    c_.xsq = c_.xtmp[:, 0]
    c_.rs = sb("rs", [P, TOK])


def x_buffers(nc, ctx, c_):
    c_.xhi = ctx.enter_context(nc.sbuf_tensor(c_.name("xhi"), [P, NM, TOK], F32R))
    c_.xlo = ctx.enter_context(nc.sbuf_tensor(c_.name("xlo"), [P, NM, TOK], F32R))


def weight_chunk(c_, n, grp, q):
    w = c_.W[PROJ[n]].rearrange("(q k p) n -> q p k n", k=QC, p=P)
    return w[q][:, :, bass.ds(grp * GW, GW)]


def load_group(c_, sp, n, grp, prior):
    for q in range(4):
        if prior is not None:
            sp.wait_ge(c_.wlo_ready, 4 * prior + q + 1)
        sp.dma_start(c_.wraw[:, q], weight_chunk(c_, n, grp, q)).then_inc(c_.w_in[q], 16)


def store_group(c_, sp, n, grp, g_all, spilled):
    sp.wait_ge(c_.evacuated, 4 * g_all + 4 + LEAD)
    dst = c_.spill[SP_I[PROJ[n]]].rearrange("m p t -> p m t")[:, bass.ds(4 * grp, 4), :]
    sp.dma_start(dst, c_.stage[:]).then_inc(c_.stored, 16)


def sp_projection(c_, sp, n, nxt, first_store):
    spilled = PROJ[n] not in RESIDUAL
    prev_spilled = n > 0 and PROJ[n - 1] not in RESIDUAL and not first_store
    load_group(c_, sp, n, 1, 4 * n)
    if prev_spilled:
        store_group(c_, sp, n - 1, 3, 4 * n - 1, None)
    with sp.Fori(1, 3) as g:
        load_group(c_, sp, n, g + 1, 4 * n + g)
        if spilled:
            store_group(c_, sp, n, g - 1, 4 * n + g - 1, None)
    if nxt is not None:
        load_group(c_, sp, nxt, 0, 4 * n + 3)
    if spilled:
        store_group(c_, sp, n, 2, 4 * n + 2, None)


def pe_projection(c_, pe, n, x_base):
    with pe.Fori(0, 4) as grp:
        g_all = grp + 4 * n
        for q in range(4):
            s = q % 2
            pe.wait_ge(c_.wlo_ready, 4 * g_all + q + 1)
            pe.wait_ge(c_.x_ready, x_base + q + 1)
            for m in range(4):
                if q == 0:
                    pe.wait_ge(c_.evacuated, 4 * g_all + m - 3 + LEAD)
                for k in range(QC):
                    kc = QC * q + k
                    wh = c_.whi[:, s, k, m * P:(m + 1) * P]
                    wl = c_.wlo[:, s, k, m * P:(m + 1) * P]
                    out = c_.psP[:, m, 0:TOK]
                    pe.matmul(out, wh, c_.xhi[:, kc, :], start=(kc == 0), stop=False)
                    pe.matmul(out, wh, c_.xlo[:, kc, :], start=False, stop=False)
                    last = pe.matmul(out, wl, c_.xhi[:, kc, :], start=False, stop=(kc == NM - 1))
                if q == 3:
                    last.then_inc(c_.bank_full, 1)
            if q < 3:
                last.then_inc(c_.chunk_used, 1)


def wait_chunk_used(c_, eng, g_all, q):
    if q < 3:
        eng.wait_ge(c_.chunk_used, 3 * g_all + q + 1)
    else:
        eng.wait_ge(c_.bank_full, 4 * g_all + 4)


def act_split(c_, act, g_all, q):
    act.wait_ge(c_.w_in[q], 16 * g_all + 16)
    if isinstance(g_all, int) and g_all == 0 and q < 2:
        pass
    elif q == 0:
        act.wait_ge(c_.chunk_used, 3 * g_all)
    elif q == 1:
        act.wait_ge(c_.bank_full, 4 * g_all)
    else:
        act.wait_ge(c_.chunk_used, 3 * g_all + q - 1)
    act.activation(c_.whi[:, q % 2], c_.wraw[:, q], ACT.Copy).then_inc(c_.whi_ready, 1)


def dve_split(c_, dve, g_all, q):
    dve.wait_ge(c_.whi_ready, 4 * g_all + q + 1)
    dve.tensor_tensor(c_.wlo[:, q % 2], c_.wraw[:, q], c_.whi[:, q % 2],
                      ALU.subtract).then_inc(c_.wlo_ready, 1)


def act_gate(c_, act, n, g_all):
    if n is None or PROJ[n] not in GATED:
        return
    for m in range(4):
        act.wait_ge(c_.bank_full, 4 * g_all + m + 1)
        act.wait_ge(c_.evacuated, 4 * g_all + m - 3 + LEAD)
        act.activation(c_.sig[:, m], c_.psP[:, m, 0:TOK], ACT.Sigmoid).then_inc(c_.sig_ready, 1)


def dve_evacuate(c_, dve, n, g_all, grp):
    if n is None:
        return
    name = PROJ[n]
    for m in range(4):
        dve.wait_ge(c_.bank_full, 4 * g_all + m + 1)
        ps = c_.psP[:, m, 0:TOK]
        if name in RESIDUAL:
            r = c_.resT[:, bass.ds(4 * grp + m, 1), :].rearrange("p a t -> p (a t)")
            dve.tensor_tensor(r, ps, r, ALU.add).then_inc(c_.evacuated, 1)
            continue
        if m == 0:
            stores = [i for i in range(n) if PROJ[i] not in RESIDUAL]
            dve.wait_ge(c_.stored, 16 * (4 * len(stores) + grp) + 1)
        if name in GATED:
            before = 16 * sum(PROJ[i] in GATED for i in range(n))
            dve.wait_ge(c_.sig_ready, before + 4 * grp + m + 1)
            dve.tensor_tensor(c_.stage[:, m], ps, c_.sig[:, m], ALU.mult).then_inc(c_.evacuated, 1)
        else:
            dve.tensor_copy(c_.stage[:, m], ps).then_inc(c_.evacuated, 1)


def act_x_quarter(c_, act, j, q):
    act.wait_ge(c_.xtmp_ready, 4 * (j + 1))
    act.activation(c_.xhi[:, 4 * q:4 * q + 4], c_.xtmp[:, j % 2], ACT.Copy).then_inc(c_.xhi_ready, 1)


def dve_x_tmp(c_, dve, j, q, source):
    if j >= 2:
        dve.wait_ge(c_.x_ready, j - 1)
    for i in range(4):
        source(dve, c_.xtmp[:, j % 2, i], 4 * q + i).then_inc(c_.xtmp_ready, 1)


def dve_x_low(c_, dve, j, q):
    dve.wait_ge(c_.xhi_ready, j + 1)
    dve.tensor_tensor(c_.xlo[:, 4 * q:4 * q + 4], c_.xtmp[:, j % 2], c_.xhi[:, 4 * q:4 * q + 4],
                      ALU.subtract).then_inc(c_.x_ready, 1)


def dve_x_quarter(c_, dve, j, q, source):
    dve_x_tmp(c_, dve, j, q, source)
    dve_x_low(c_, dve, j, q)


def act_projection(c_, act, n, prev, roll=None, rolled=None):
    g0 = 4 * n

    def group(g_all, ended, ended_g, before_1=None, after=None):
        for q in range(4):
            if q == 1 and before_1 is not None:
                before_1()
            act_split(c_, act, g_all, q)
            if q == 0:
                act_gate(c_, act, ended, ended_g)
            if after is not None and q >= 1:
                after(q - 1)

    def last_quarter():
        wait_chunk_used(c_, act, g0 - 1, 3)
        act_x_quarter(c_, act, rolled + 3, 3)

    group(g0, prev, g0 - 1, before_1=last_quarter if rolled is not None else None)
    with act.Fori(1, 3) as grp:
        group(grp + g0, n, grp + g0 - 1)

    def roll_quarter(q):
        wait_chunk_used(c_, act, g0 + 3, q)
        act_x_quarter(c_, act, roll + q, q)

    group(g0 + 3, n, g0 + 2, after=roll_quarter if roll is not None else None)


def dve_projection(c_, dve, n, prev, roll=None, rolled=None, source=None, source_now=None):
    g0 = 4 * n
    for q in range(4):
        dve_split(c_, dve, g0, q)
        if q == 0:
            dve_evacuate(c_, dve, prev, g0 - 1, 3)
            if rolled is not None:
                dve_x_quarter(c_, dve, rolled + 3, 3, source_now)
    with dve.Fori(1, 3) as grp:
        for q in range(4):
            dve_split(c_, dve, grp + g0, q)
            if q == 0:
                dve_evacuate(c_, dve, n, grp + g0 - 1, grp - 1)
    for q in range(4):
        dve_split(c_, dve, g0 + 3, q)
        if q == 0:
            dve_evacuate(c_, dve, n, g0 + 2, 2)
        if roll is not None and q >= 1:
            dve_x_quarter(c_, dve, roll + q - 1, q - 1, source)


def norm_squares_act(c_, act, j):
    for m in range(NM):
        if m >= 2:
            act.wait_ge(c_.sq_summed, NM * j + m - 1)
        act.activation(c_.xsq[:, m % 2], c_.resT[:, m], ACT.Square).then_inc(c_.sq_ready, 1)


def norm_sum_pe(c_, pe, j):
    for m in range(NM):
        pe.wait_ge(c_.sq_ready, NM * j + m + 1)
        pe.matmul(c_.psN[:, 0:TOK], c_.ones[:], c_.xsq[:, m % 2], start=(m == 0),
                  stop=(m == NM - 1)).then_inc(c_.sq_summed, 1)


def norm_rsqrt_act(c_, act, j):
    act.wait_ge(c_.sq_summed, NM * (j + 1))
    act.activation(c_.rs[:], c_.psN[:, 0:TOK], ACT.Ln, bias=c_.consts[:, 0:1],
                   scale=1.0 / D).then_inc(c_.ln_ready, 1)
    act.wait_ge(c_.ln_ready, j + 1)
    act.activation(c_.rs[:], c_.rs[:], ACT.Exp, scale=-0.5).then_inc(c_.rs_ready, 1)


def normed(c_, gain):
    def source(dve, out, m):
        v = VEC[gain] * NM + m
        return dve.scalar_tensor_tensor(out=out, in0=c_.resT[:, m], scalar=c_.vec[:, v:v + 1],
                                        in1=c_.rs[:], op0=ALU.mult, op1=ALU.mult)
    return source


def mixed(c_, p):
    def source(dve, out, m):
        v = VEC[f"mu{p}"] * NM + m
        return dve.scalar_tensor_tensor(out=out, in0=c_.delta[:, m], scalar=c_.vec[:, v:v + 1],
                                        in1=c_.hT[:, m], op0=ALU.mult, op1=ALU.add)
    return source


def opening(nc, c_, a):
    with ExitStack() as ctx:
        def sb(name, shape, dt=F32):
            return ctx.enter_context(nc.sbuf_tensor(name, shape, dt))

        def sem(name):
            return ctx.enter_context(nc.semaphore(name))

        xnat = sb("xnat", [P, 3, D])
        shnat = sb("shnat", [NB, D])
        vnat = sb("vnat", [P, 3, P])
        shT = sb("shT", [P, NM, NB])
        lastT = sb("lastT", [P, NB + 1, NM])
        lastN = sb("lastN", [P, 2, P])
        w1 = sb("w1s", [P, 2, NM, LORA])
        w2 = sb("w2s", [LORA, 2, D])
        low = sb("low", [LORA, 2, TOK])
        psT = ctx.enter_context(nc.psum_tensor("psT", [P, 4, 512], F32))
        psN = c_.psN = ctx.enter_context(nc.psum_tensor(c_.name("psN"), [P, 512], F32))
        psL = ctx.enter_context(nc.psum_tensor("psL", [P, 2, 512], F32))
        psV = ctx.enter_context(nc.psum_tensor("psV", [P, 512], F32))
        x_in, v_in, sh_in, lora_in = sem("x_in"), sem("v_in"), sem("sh_in"), sem("lora_in")
        ident_made, const_made = sem("ident_made"), sem("const_made")
        vec_turned, x_turned, sh_turned = sem("vec_turned"), sem("x_turned"), sem("sh_turned")
        x_out, vec_ready, sh_ready = sem("x_out"), sem("vec_ready"), sem("sh_ready")
        h_ready, delta_ready = sem("h_ready"), sem("delta_ready")
        low_ready, up_summed, up_out = sem("low_ready"), sem("up_summed"), sem("up_out")
        last_ready, last_turned, last_out, last_stored = (sem("last_ready"), sem("last_turned"),
                                                          sem("last_out"), sem("last_stored"))
        mix_ready, mix_used, up_stored = sem("mix_ready"), sem("mix_used"), sem("up_stored")
        block = ctx.enter_context(nc.Block())

        @block.sync
        def _(sp):
            for n, name in enumerate(VECS):
                src = a[name].rearrange("(m p) -> m p", p=P)
                sp.dma_start(vnat[16 * (n % 8):16 * (n % 8) + 16, n // 8], src).then_inc(v_in, 16)
            for t in range(2):
                sp.dma_start(xnat[:, t], a["x_prompt"][0, t * P:(t + 1) * P]).then_inc(x_in, 16)
            sp.dma_start(xnat[0:64, 2], a["x_sample"].rearrange("b t d -> (b t) d")).then_inc(x_in, 16)
            sp.dma_start(shnat[:], a["state_shift"][0]).then_inc(sh_in, 16)
            for j, (d1, d2) in enumerate((("a_w1", "a_w2"), ("a_a1", "a_a2"))):
                sp.dma_start(w1[:, j], a[d1][0].rearrange("(m p) n -> p m n", p=P)).then_inc(lora_in, 16)
                sp.dma_start(w2[:, j], a[d2][0]).then_inc(lora_in, 16)
            load_group(c_, sp, 0, 0, None)
            sp.wait_ge(last_out, 2)
            sp.dma_start(a["o_shift_s"][0].rearrange("b (m p) -> (b m) p", p=P),
                         lastN[:, 0]).then_inc(last_stored, 16)
            sp.dma_start(a["o_shift_p"][0, 0].rearrange("(m p) -> m p", p=P),
                         lastN[0:NM, 1]).then_inc(last_stored, 16)
            for j, name in enumerate(("s", "a")):
                for g in range(4):
                    sp.wait_ge(up_out, 16 * j + 4 * g + 4)
                    sp.dma_start(c_.spill[SP_I[name]].rearrange("m p t -> p m t")[:, 4 * g:4 * g + 4],
                                 c_.stage[:]).then_inc(up_stored, 16)
            sp.wait_ge(up_stored, 16 * 8)
            sp.wait_ge(last_stored, 32)

        @block.gpsimd
        def _(pool):
            pool.memset(c_.ident[:], 0.0).then_inc(ident_made, 1)
            pool.wait_ge(ident_made, 1)
            pool.affine_select(out=c_.ident[:], in_=c_.ident[:], compare_op=ALU.not_equal, fill=1.0,
                               base=0, pattern=[[-1, P]], channel_multiplier=1).then_inc(ident_made, 1)

        @block.vector
        def _(dve):
            dve.memset(c_.ones[:], 1.0).then_inc(const_made, 1)
            dve.memset(c_.consts[:, 0:1], RMS_EPS).then_inc(const_made, 1)
            dve.memset(c_.consts[:, 1:2], LNX_EPS).then_inc(const_made, 1)
            dve.memset(c_.consts[:, 2:3], 10.0 * math.log(2.0)).then_inc(const_made, 1)
            dve.wait_ge(vec_turned, 3)
            dve.tensor_copy(c_.vec[:, 0:NM * len(VECS)], psV[:, 0:NM * len(VECS)]).then_inc(vec_ready, 1)
            dve.wait_ge(sh_turned, 1)
            dve.tensor_copy(shT[:], psV[:, 384:512].rearrange("p (m b) -> p m b", m=NM)).then_inc(sh_ready, 1)
            dve.wait_ge(vec_ready, 1)
            dve.wait_ge(c_.rs_ready, 1)
            src = normed(c_, "a_norm")
            for m in range(NM):
                src(dve, c_.hT[:, m], m).then_inc(h_ready, 1)
            dve.wait_ge(h_ready, NM)
            dve.wait_ge(sh_ready, 1)
            h, dl = c_.hT, c_.delta
            dve.tensor_tensor(dl[:, :, 1:SEQ], h[:, :, 0:SEQ - 1], h[:, :, 1:SEQ],
                              ALU.subtract).then_inc(delta_ready, 1)
            dve.tensor_scalar(dl[:, :, 0:1], h[:, :, 0:1], -1.0, None, ALU.mult).then_inc(delta_ready, 1)
            for b in range(NB):
                t0 = SEQ + b * TS
                dve.tensor_tensor(dl[:, :, t0 + 1:t0 + TS], h[:, :, t0:t0 + TS - 1],
                                  h[:, :, t0 + 1:t0 + TS], ALU.subtract).then_inc(delta_ready, 1)
                dve.tensor_tensor(dl[:, :, t0:t0 + 1], shT[:, :, b:b + 1], h[:, :, t0:t0 + 1],
                                  ALU.subtract).then_inc(delta_ready, 1)
                dve.tensor_copy(lastT[:, b], h[:, :, t0 + TS - 1]).then_inc(last_ready, 1)
            dve.tensor_copy(lastT[:, NB], h[:, :, SEQ - 1]).then_inc(last_ready, 1)
            dve.wait_ge(last_turned, 1)
            dve.tensor_copy(lastN[:, 0], psN[:, 384:512]).then_inc(last_out, 1)
            dve.wait_ge(last_turned, 2)
            dve.tensor_copy(lastN[0:NM, 1], psN[0:NM, 384:512]).then_inc(last_out, 1)
            dve.wait_ge(delta_ready, 2 + 2 * NB)
            for j in range(2):
                source = mixed(c_, 4 + j)
                for m in range(NM):
                    k = NM * j + m
                    if k >= 8:
                        dve.wait_ge(mix_used, k - 7)
                    source(dve, c_.xtmp[:, (k // 4) % 2, k % 4], m).then_inc(mix_ready, 1)

        @block.scalar
        def _(act):
            act.preload_act_table_set("natural_log_exp_and_others")
            for m in range(NM):
                act.wait_ge(x_turned, m + 1)
                act.activation(c_.resT[:, m], psT[:, m % 4, 0:TOK], ACT.Copy).then_inc(x_out, 1)
            act.wait_ge(x_out, NM)
            norm_squares_act(c_, act, 0)
            act.wait_ge(const_made, 4)
            norm_rsqrt_act(c_, act, 0)
            act.preload_act_table(ACT.Sigmoid)
            for j in range(2):
                act.wait_ge(mix_used, NM * (j + 1))
                act.activation(low[:, j], psL[0:LORA, j, 0:TOK],
                               ACT.Tanh if j == 0 else ACT.Copy).then_inc(low_ready, 1)
            act.wait_ge(vec_ready, 1)
            for j in range(2):
                for m in range(NM):
                    k = NM * j + m
                    act.wait_ge(up_summed, k + 1)
                    if k >= 4 and k % 4 == 0:
                        act.wait_ge(up_stored, 16 * (k // 4))
                    v = VEC[("w0", "a0")[j]] * NM + m
                    act.activation(c_.stage[:, m % 4], psT[:, m % 4, 0:TOK], ACT.Sigmoid,
                                   bias=c_.vec[:, v:v + 1]).then_inc(up_out, 1)

        @block.tensor
        def _(pe):
            pe.wait_ge(ident_made, 2)
            pe.wait_ge(v_in, 16 * len(VECS))
            pe.wait_ge(const_made, 4)
            for t in range(3):
                w = min(P, NM * len(VECS) - P * t)
                pe.transpose(psV[:, P * t:P * t + w], vnat[0:w, t], c_.ident[0:w, 0:w]).then_inc(vec_turned, 1)
            pe.wait_ge(sh_in, 16)
            pe.wait_ge(vec_ready, 1)
            for m in range(NM):
                last = pe.transpose(psV[:, 384 + NB * m:384 + NB * m + NB], shnat[:, m * P:(m + 1) * P],
                                    c_.ident[0:NB, 0:NB])
            last.then_inc(sh_turned, 1)
            pe.wait_ge(x_in, 48)
            for m in range(NM):
                if m >= 4:
                    pe.wait_ge(x_out, m - 3)
                for t in range(3):
                    w = (P, P, NB * TS)[t]
                    last = pe.transpose(psT[:, m % 4, t * P:t * P + w], xnat[0:w, t, m * P:(m + 1) * P],
                                        c_.ident[0:w, 0:w])
                last.then_inc(x_turned, 1)
            norm_sum_pe(c_, pe, 0)
            pe.wait_ge(last_ready, NB + 1)
            pe.wait_ge(c_.rs_ready, 1)
            pe.transpose(psN[:, 384:512], lastT[:, 0:NB].rearrange("p b m -> p (b m)"),
                         c_.ident[:]).then_inc(last_turned, 1)
            pe.wait_ge(last_out, 1)
            pe.transpose(psN[0:NM, 384:512], lastT[:, NB], c_.ident[:]).then_inc(last_turned, 1)
            pe.wait_ge(lora_in, 64)
            for j in range(2):
                for m in range(NM):
                    pe.wait_ge(mix_ready, NM * j + m + 1)
                    k = NM * j + m
                    last = pe.matmul(psL[0:LORA, j, 0:TOK], w1[:, j, m], c_.xtmp[:, (k // 4) % 2, k % 4],
                                     start=(m == 0), stop=(m == NM - 1))
                    last.then_inc(mix_used, 1)
            for j in range(2):
                pe.wait_ge(low_ready, j + 1)
                for m in range(NM):
                    k = NM * j + m
                    if k >= 4:
                        pe.wait_ge(up_out, k - 3)
                    pe.matmul(psT[:, m % 4, 0:TOK], w2[:, j, m * P:(m + 1) * P], low[:, j],
                              start=True, stop=True).then_inc(up_summed, 1)


def split_buffers(nc, ctx, c_):
    c_.whi = ctx.enter_context(nc.sbuf_tensor(c_.name("whi"), [P, 2, QC, GW], F32R))
    c_.wlo = ctx.enter_context(nc.sbuf_tensor(c_.name("wlo"), [P, 2, QC, GW], F32R))
    c_.psP = ctx.enter_context(nc.psum_tensor(c_.name("psP"), [P, 4, 512], F32))


def mixing_projections(nc, c_, a):
    with ExitStack() as ctx:
        split_buffers(nc, ctx, c_)
        block = ctx.enter_context(nc.Block())

        @block.sync
        def _(sp):
            for n in range(4):
                sp_projection(c_, sp, n, n + 1 if n < 3 else None, first_store=(n == 0))
            store_group(c_, sp, 3, 3, 15, None)
            sp.wait_ge(c_.stored, 16 * 16 + 1)

        @block.tensor
        def _(pe):
            for n in range(4):
                pe_projection(c_, pe, n, 4 * n)

        @block.scalar
        def _(act):
            for q in range(4):
                act_x_quarter(c_, act, q, q)
            for n in range(4):
                act_projection(c_, act, n, n - 1 if n else None, roll=4 * n + 4 if n < 3 else None,
                               rolled=4 * n if n else None)
            act_gate(c_, act, 3, 15)

        @block.vector
        def _(dve):
            dve.sem_inc(c_.evacuated, LEAD)
            dve.sem_inc(c_.stored, 1)
            for q in range(4):
                dve_x_quarter(c_, dve, q, q, mixed(c_, 0))
            for n in range(4):
                dve_projection(c_, dve, n, n - 1 if n else None, roll=4 * n + 4 if n < 3 else None,
                               rolled=4 * n if n else None, source=mixed(c_, n + 1) if n < 3 else None,
                               source_now=mixed(c_, n))
            dve_evacuate(c_, dve, 3, 15, 3)


class Marks:

    def __init__(self, sem, names):
        self.sem, self.names, self.n, self.seen = sem, {x: i for i, x in enumerate(names)}, len(names), []

    def wait(self, eng, name, it):
        eng.wait_ge(self.sem, it * self.n + (self.names[name] + 1))

    def done(self, ins, name):
        assert self.names[name] == len(self.seen), (name, len(self.seen))
        self.seen.append(name)
        ins.then_inc(self.sem, 1)


NT = 2
HS = 64
CH = NCH + 1

DVE_R = ["cs", "kk0", "ssm", "kk", "Az", "ka", "Bz", "ka1", "k2", "Kz", "D", "F", "Dt", "AK",
         "W", "Wt", "RB", "RK", "Y", "Yt", "Z4", "Z2", "X",
         "U0", "SA0", "ST0", "SP1", "U1", "SA1", "ST1", "SP2", "U2", "SA2", "ST2",
         "SP3", "U3", "SA3", "ST3", "U4", "SA4", "Bx", "Kx",
         "bonus", "cen", "on", "ong", "onb", "oy", "y", "xl"]
ACT_R = ["Pc", "Pi", "Pm", "sq", "ln", "rn", "Vn", "Bn", "Kn", "D2", "D2t", "D4", "D4t", "E", "Et",
         "E2", "E2t", "S0T", "E4t", "O0", "O1", "O2", "O3", "O4", "SN", "SF", "csq", "lnv", "rstd",
         "xh"]
POOL_R = ["csm", "Rz", "rk1", "rk2", "BpP", "BpS", "KpP", "KpS", "ID", "W1", "IDt", "W1t", "AzM",
          "dP"]
PE_R = ["ss", "bon", "abT", "ab", "Vn", "Bn", "Kn", "D2", "D2t", "akT", "D3", "D3t", "D4", "D4t",
        "rbT", "rkT", "Y", "Yt", "E", "Et", "S0T", "E2", "E2t", "E4t", "Z4", "Z2", "X",
        "U0", "SA0", "S0", "O0", "U1", "SA1", "S1", "O1", "U2", "SA2", "S2", "O2",
        "U3", "SA3", "S3", "O3", "U4", "SA4", "O4", "SN", "SF", "mean", "var"]
TAKEN = {"ss": ("v", "ssm"), "bon": ("v", "bonus"), "abT": ("v", "F"), "ab": ("v", "Dt"),
         "Vn": ("a", "Vn"), "Bn": ("a", "Bn"), "Kn": ("a", "Kn"), "D2": ("a", "D2"),
         "D2t": ("a", "D2t"), "akT": ("v", "AK"), "D3": ("v", "W"), "D3t": ("v", "Wt"),
         "D4": ("a", "D4"), "D4t": ("a", "D4t"), "rbT": ("v", "RB"), "rkT": ("v", "RK"),
         "Y": ("v", "Y"), "Yt": ("v", "Yt"), "E": ("a", "E"), "Et": ("a", "Et"),
         "S0T": ("a", "S0T"), "E2": ("a", "E2"), "E2t": ("a", "E2t"), "E4t": ("a", "E4t"),
         "Z4": ("v", "Z4"), "Z2": ("v", "Z2"), "X": ("v", "X"), "SN": ("a", "SN"),
         "SF": ("a", "SF"), "mean": ("v", "cen"), "var": ("a", "lnv")}
for _c in range(CH):
    TAKEN |= {f"U{_c}": ("v", f"U{_c}"), f"SA{_c}": ("v", f"SA{_c}"), f"O{_c}": ("a", f"O{_c}"),
              f"S{_c}": ("v", f"ST{_c}")}
TURNS = [x for x in PE_R if x != "bon"]
SETS = 3


def recurrence(nc, c_, a):
    with ExitStack() as ctx:
        def sb(name, shape, dt=F32):
            return ctx.enter_context(nc.sbuf_tensor("rw_" + name, shape, dt))

        def sem(name):
            return ctx.enter_context(nc.semaphore("rw_" + name))

        def big(name):
            return sb(name, [P, NT, TOK])

        ins = {x: big("in_" + x) for x in ("r", "k", "v", "s", "a", "g")}
        R_, K_, V_, S_, A_, G_ = (ins[x] for x in ("r", "k", "v", "s", "a", "g"))
        T = {x: big(x) for x in
             ("cs", "csm", "Pc", "Pi", "Pm", "kk0", "sq", "rn", "kk", "Az", "Bz", "Kz", "Rz",
              "k2", "rk", "Bp", "Kp", "D", "F", "Dt", "AK", "RB", "RK", "Vn", "Bn", "Kn", "D2",
              "D2t", "D4", "D4t", "W1", "W1t", "Y", "Yt", "Et")}
        T["E2"], T["E2t"], T["E4t"], T["Z4"], T["Z2"] = T["D2"], T["D2t"], T["D4"], T["W1"], T["W1t"]
        T["X"] = T["Z4"]
        T["OT"], T["E"] = T["Pm"], T["csm"]
        T["W"], T["Wt"] = T["W1"], T["W1t"]
        T["ka1"] = T["k2"]
        S0n = sb("S0n", [P, NT, NB, HS])
        S0T = sb("S0T", [P, NT, NB, HS])
        AzM = sb("AzM", [P, NT, NB, HS])
        dP = sb("dP", [P, NT, NB, HS])
        Bx = sb("Bx", [P, NT, NB, HS])
        Kx = sb("Kx", [P, NT, NB, HS])
        SN = AzM
        ST = [sb(f"ST{i}", [P, NT, HS]) for i in range(2)]
        SPr = sb("SPr", [P, NT, HS])
        U = sb("U", [P, NT, HS])
        SA = [sb(f"SA{i}", [P, NT, HS]) for i in range(2)]
        SF = sb("SF", [P, NT, HS])
        blk, blkm = sb("blk", [P, P]), sb("blkm", [P, P])
        I2 = sb("I2", [P, HS])
        mS, mI, mD, mDt, mF = (sb(x, [P, TOK]) for x in ("mS", "mI", "mD", "mDt", "mF"))
        keep = sb("keep", [P, TOK])
        mB = sb("mB", [P, NB, HS])
        mJ = sb("mJ", [P, NB])
        ps = [ctx.enter_context(nc.psum_tensor(f"rw_ps{i}", [P, NT, 512], F32)) for i in range(SETS)]
        psB = ctx.enter_context(nc.psum_tensor("rw_psB", [P, NT, 512], F32))
        s_in = {x: sem("in_" + x) for x in ins}
        s0_in, masks, wkv_stored, wkvp_stored = sem("s0_in"), sem("masks"), sem("wkv_stored"), sem("wkvp_stored")
        v, t, g, s = (Marks(sem(x), y) for x, y in (("vector", DVE_R), ("tensor", PE_R),
                                                   ("pool", POOL_R), ("scalar", ACT_R)))
        who = {"v": v, "a": s}

        passed = {x: sem("passed_" + x) for x in ("pe", "sp")}

        def pass_point(eng, x):
            eng.sem_inc(passed[x], 1)

        def step_ps(name):
            return psB if name == "bon" else ps[TURNS.index(name) % SETS]

        def full(x):
            return x[:, :, 0:TOK]

        def rows(mask):
            return mask[:].unsqueeze(1).to_broadcast([P, NT, TOK])

        def prm(name, i):
            w = c_.vec[:, bass.ds(VEC[name] * NM + NT * i, NT)]
            return w.unsqueeze(2).to_broadcast([P, NT, TOK])

        def chunk(x, c):
            return x[:, :, c * L:(c + 1) * L]

        def prompt_chunks(x):
            return x[:, :, 0:SEQ].rearrange("p t (c l) -> p t c l", l=L)

        def sample_blocks(x):
            return x[:, :, SEQ:TOK].rearrange("p t (b l) -> p t b l", l=TS)

        block = ctx.enter_context(nc.Block())

        @block.sync
        def _(sp):
            def load(i, prior):
                for x, (eng, last) in (("s", (g, "csm")), ("k", (v, "k2")), ("a", (v, "ka1")),
                                       ("r", (g, "rk1"))):
                    if prior is not None:
                        eng.wait(sp, last, prior)
                        pass_point(sp, "sp")
                    sp.dma_start(ins[x][:], c_.spill[SP_I[x]].rearrange("m p t -> p m t")
                                 [:, bass.ds(NT * i, NT), :]).then_inc(s_in[x], 16)
                if prior is not None:
                    t.wait(sp, "S0T", prior)
                pass_point(sp, "sp")
                for m in range(NT):
                    src = a["state_wkv"][0].rearrange("b (m h) v k -> m (h v) b k", h=2)
                    sp.dma_start(S0n[:, m], src[bass.ds(NT * i + m, 1), :, :, :]
                                 .rearrange("m p b k -> (m p) b k")).then_inc(s0_in, 16)
                if prior is not None:
                    v.wait(sp, "y", prior)
                for x in ("v", "g"):
                    pass_point(sp, "sp")
                    sp.dma_start(ins[x][:], c_.spill[SP_I[x]].rearrange("m p t -> p m t")
                                 [:, bass.ds(NT * i, NT), :]).then_inc(s_in[x], 16)

            def store(i):
                s.wait(sp, "SF", i)
                pass_point(sp, "sp")
                dst_s = a["o_wkv_s"][0].rearrange("b (m h) v k -> m (h v) b k", h=2)
                dst_p = a["o_wkv_p"][0, 0].rearrange("(m h) v k -> m (h v) k", h=2)
                for m in range(NT):
                    sp.dma_start(dst_s[bass.ds(NT * i + m, 1), :, :, :].rearrange("m p b k -> (m p) b k"),
                                 SN[:, m]).then_inc(wkv_stored, 16)
                    sp.dma_start(dst_p[bass.ds(NT * i + m, 1), :, :].rearrange("m p k -> (m p) k"),
                                 SF[:, m]).then_inc(wkvp_stored, 16)

            load(0, None)
            with sp.Fori(0, NM // NT - 1) as i:
                store(i)
                load(i + 1, i)
            store(NM // NT - 1)
            sp.wait_ge(wkv_stored, 16 * NM)
            sp.wait_ge(wkvp_stored, 16 * NM)

        @block.gpsimd
        def _(pool):
            n = [0]

            def made(ins_):
                n[0] += 1
                ins_.then_inc(masks, 1)
                pool.wait_ge(masks, n[0])

            def tri(m, c0, cols, op, sign):
                for h in range(2):
                    view = m[64 * h:64 * h + 64, c0:c0 + cols]
                    made(pool.affine_select(out=view, in_=view, compare_op=op, fill=0.0, base=0,
                                            pattern=[[sign, cols]], channel_multiplier=-sign))

            def blocks(m, c0, cols):
                for h in range(2):
                    view = m[64 * h:64 * h + 64, c0:c0 + cols].rearrange("p (b u) -> p b u", u=TS)
                    made(pool.affine_select(out=view, in_=view, compare_op=ALU.is_ge, fill=0.0, base=0,
                                            pattern=[[-TS, cols // TS], [0, TS]], channel_multiplier=1))
                    made(pool.affine_select(out=view, in_=view, compare_op=ALU.is_ge, fill=0.0,
                                            base=TS - 1, pattern=[[TS, cols // TS], [0, TS]],
                                            channel_multiplier=-1))

            made(pool.memset(blk[:], 0.0))
            made(pool.memset(blkm[:], 0.0))
            for h in range(2):
                made(pool.memset(blk[64 * h:64 * h + 64, 64 * h:64 * h + 64], 1.0))
                made(pool.memset(blkm[64 * h:64 * h + 64, 64 * h:64 * h + 64], 1.0 / HS))
                made(pool.tensor_copy(I2[64 * h:64 * h + 64, :],
                                      c_.ident[64 * h:64 * h + 64, 64 * h:64 * h + 64]))
            for m in (mS, mI, mD, mDt):
                made(pool.memset(m[:], 1.0))
            for c in range(CH):
                tri(mS, c * L, L, ALU.is_gt, 1)
                tri(mD, c * L, L, ALU.is_gt, 1)
                tri(mI, c * L, L, ALU.is_ge, 1)
                tri(mDt, c * L, L, ALU.is_gt, -1)
                blocks(mD, c * L, L)
                blocks(mDt, c * L, L)
            blocks(mS, SEQ, L)
            blocks(mI, SEQ, L)
            made(pool.tensor_tensor(mF[:], mS[:], mD[:], ALU.subtract))
            made(pool.memset(keep[:], 1.0))
            made(pool.memset(keep[:, 0:SEQ].rearrange("p (c l) -> p c l", l=L)[:, :, 0:1], 0.0))
            made(pool.memset(keep[:, SEQ:TOK].rearrange("p (c l) -> p c l", l=TS)[:, :, 0:1], 0.0))
            made(pool.memset(mB[:], 0.0))
            for b in range(NB):
                made(pool.memset(mB[:, b, TS * b:TS * b + TS], 1.0))
            made(pool.memset(mJ[:], 1.0))
            for h in range(2):
                view = mJ[64 * h:64 * h + 64, :]
                made(pool.affine_select(out=view, in_=view, compare_op=ALU.is_ge, fill=0.0, base=0,
                                        pattern=[[-TS, NB]], channel_multiplier=1))
                made(pool.affine_select(out=view, in_=view, compare_op=ALU.is_ge, fill=0.0,
                                        base=TS - 1, pattern=[[TS, NB]], channel_multiplier=-1))
            c_.n_masks = n[0]

            def tt(name, out, x, y, op, i):
                g.done(pool.tensor_tensor(out, x, y, op), name)

            with pool.Fori(0, NM // NT) as i:
                v.wait(pool, "cs", i)
                tt("csm", full(T["csm"]), full(T["cs"]), full(S_), ALU.subtract, i)
                s.wait(pool, "Pc", i)
                pool.wait_ge(s_in["r"], 16 * i + 16)
                tt("Rz", full(T["Rz"]), full(R_), full(T["Pc"]), ALU.mult, i)
                v.wait(pool, "k2", i)
                tt("rk1", full(T["rk"]), full(R_), full(T["k2"]), ALU.mult, i)
                g.wait(pool, "rk1", i)
                tt("rk2", full(T["rk"]), full(T["rk"]), prm("r_k", i), ALU.mult, i)
                for x, z in (("Bp", "Bz"), ("Kp", "Kz")):
                    v.wait(pool, z, i)
                    tt(x + "P", prompt_chunks(T[x]), prompt_chunks(T[z]),
                       prompt_chunks(T["Pc"])[:, :, :, L - 1:L].to_broadcast([P, NT, NCH, L]), ALU.mult, i)
                    tt(x + "S", sample_blocks(T[x]), sample_blocks(T[z]),
                       sample_blocks(T["Pc"])[:, :, :, TS - 1:TS].to_broadcast([P, NT, NB, TS]), ALU.mult, i)
                idb = I2[:].unsqueeze(1).to_broadcast([P, CH, HS])
                for x, d, d2 in (("", "D", "D2"), ("t", "Dt", "D2t")):
                    v.wait(pool, d, i)
                    w4 = T["W1" + x][:].rearrange("p t (c l) -> p (t c) l", l=L)
                    d4 = T[d][:].rearrange("p t (c l) -> p (t c) l", l=L)
                    tt("ID" + x, w4, d4, I2[:].unsqueeze(1).to_broadcast([P, NT * CH, HS]), ALU.add, i)
                    s.wait(pool, d2, i)
                    g.wait(pool, "ID" + x, i)
                    tt("W1" + x, full(T["W1" + x]), full(T["W1" + x]), full(T[d2]), ALU.add, i)
                tt("AzM", AzM[:], T["Az"][:, :, SEQ:TOK].unsqueeze(2).to_broadcast([P, NT, NB, HS]),
                   mB[:].unsqueeze(1).to_broadcast([P, NT, NB, HS]), ALU.mult, i)
                tt("dP", dP[:], sample_blocks(T["Pc"])[:, :, :, TS - 1:TS].to_broadcast([P, NT, NB, HS]),
                   I2[:].unsqueeze(1).unsqueeze(1).to_broadcast([P, NT, NB, HS]), ALU.mult, i)

        @block.scalar
        def _(act):
            act.preload_act_table_set("natural_log_exp_and_others")
            act.wait_ge(masks, c_.n_masks)

            def af(name, out, in_, fn=ACT.Copy, **kw):
                s.done(act.activation(out, in_, fn, **kw), name)

            def take(name, i, out=None, n=CH):
                t.wait(act, name, i)
                dst = T[name] if out is None else out
                af(name, dst[:, :, 0:n * L], step_ps(name)[:, :, 0:n * L])

            with act.Fori(0, NM // NT) as i:
                v.wait(act, "cs", i)
                af("Pc", full(T["Pc"]), full(T["cs"]), ACT.Exp, scale=-DECAY)
                af("Pi", full(T["Pi"]), full(T["cs"]), ACT.Exp, scale=DECAY)
                g.wait(act, "csm", i)
                af("Pm", full(T["Pm"]), full(T["csm"]), ACT.Exp, scale=-DECAY)
                v.wait(act, "kk0", i)
                af("sq", full(T["sq"]), full(T["kk0"]), ACT.Square)
                v.wait(act, "ssm", i)
                af("ln", full(T["rn"]), full(T["rn"]), ACT.Ln, scale=float(2 ** 20))
                s.wait(act, "ln", i)
                af("rn", full(T["rn"]), full(T["rn"]), ACT.Exp, scale=-0.5, bias=c_.consts[:, 2:3])
                take("Vn", i)
                take("Bn", i)
                take("Kn", i)
                take("D2", i)
                take("D2t", i)
                take("D4", i)
                take("D4t", i)
                take("E", i, n=NCH)
                take("Et", i, n=NCH)
                take("E2", i, n=NCH)
                take("E2t", i, n=NCH)
                t.wait(act, "S0T", i)
                af("S0T", S0T[:], step_ps("S0T")[:, :, :].rearrange("p t (b k) -> p t b k", k=HS))
                take("E4t", i, n=NCH)
                for c in range(CH):
                    t.wait(act, f"O{c}", i)
                    af(f"O{c}", chunk(T["OT"], c), step_ps(f"O{c}")[:, :, 0:L])
                t.wait(act, "SN", i)
                af("SN", SN[:], step_ps("SN")[:, :, :].rearrange("p t (b k) -> p t b k", k=HS))
                t.wait(act, "SF", i)
                af("SF", SF[:], step_ps("SF")[:, :, 0:HS])
                v.wait(act, "cen", i)
                af("csq", full(T["sq"]), full(T["cs"]), ACT.Square)
                t.wait(act, "var", i)
                af("lnv", full(T["rn"]), full(step_ps("var")), ACT.Ln, bias=c_.consts[:, 1:2])
                s.wait(act, "lnv", i)
                af("rstd", full(T["rn"]), full(T["rn"]), ACT.Exp, scale=-0.5)
                v.wait(act, "y", i)
                af("xh", c_.xhi[:, bass.ds(NT * i, NT), :], full(T["kk"]))

        @block.vector
        def _(dve):
            dve.wait_ge(masks, c_.n_masks)

            def tt(name, out, x, y, op=ALU.mult):
                v.done(dve.tensor_tensor(out, x, y, op), name)

            def stt(name, out, x, scalar, y, op0, op1):
                v.done(dve.scalar_tensor_tensor(out=out, in0=x, scalar=scalar, in1=y, op0=op0, op1=op1),
                       name)

            def masked(name, step, mask, i):
                t.wait(dve, step, i)
                tt(name, full(T[name]), full(step_ps(step)), rows(mask))

            def plus(name, step, base, i, n=CH):
                t.wait(dve, step, i)
                tt(name, T[name][:, :, 0:n * L], step_ps(step)[:, :, 0:n * L],
                   T[base][:, :, 0:n * L], ALU.add)

            with dve.Fori(0, NM // NT) as i:
                dve.wait_ge(s_in["s"], 16 * i + 16)
                for m in range(NT):
                    ins_ = dve.tensor_tensor_scan(out=T["cs"][:, m], data0=keep[:], data1=S_[:, m],
                                                  initial=0.0, op0=ALU.mult, op1=ALU.add)
                v.done(ins_, "cs")
                dve.wait_ge(s_in["k"], 16 * i + 16)
                tt("kk0", full(T["kk0"]), full(K_), prm("k_k", i))
                t.wait(dve, "ss", i)
                v.done(dve.tensor_scalar(full(T["rn"]), full(step_ps("ss")), 1e-24, None, ALU.max), "ssm")
                s.wait(dve, "rn", i)
                tt("kk", full(T["kk"]), full(T["kk0"]), full(T["rn"]))
                v.wait(dve, "kk", i)
                stt("Az", full(T["Az"]), full(T["kk"]), -1.0, full(T["Pm"]), ALU.mult, ALU.mult)
                dve.wait_ge(s_in["a"], 16 * i + 16)
                tt("ka", full(T["kk0"]), full(T["kk"]), full(A_))
                v.wait(dve, "ka", i)
                tt("Bz", full(T["Bz"]), full(T["kk0"]), full(T["Pi"]))
                stt("ka1", full(T["ka1"]), full(A_), -1.0, prm("k_a", i), ALU.add, ALU.mult)
                v.wait(dve, "ka1", i)
                stt("k2", full(T["k2"]), full(T["ka1"]), 1.0, full(K_), ALU.add, ALU.mult)
                v.wait(dve, "k2", i)
                tt("Kz", full(T["Kz"]), full(T["k2"]), full(T["Pi"]))
                masked("D", "abT", mD, i)
                tt("F", full(T["F"]), full(step_ps("abT")), rows(mF))
                masked("Dt", "ab", mDt, i)
                masked("AK", "akT", mS, i)
                g.wait(dve, "W1", i)
                plus("W", "D3", "W1", i)
                g.wait(dve, "W1t", i)
                plus("Wt", "D3t", "W1t", i)
                masked("RB", "rbT", mI, i)
                masked("RK", "rkT", mI, i)
                plus("Y", "Y", "W", i)
                plus("Yt", "Yt", "Wt", i)
                plus("Z4", "Z4", "Y", i, NCH)
                plus("Z2", "Z2", "Z4", i, NCH)
                plus("X", "X", "Z2", i, NCH)
                for c in range(NCH):
                    if c > 0:
                        v.wait(dve, f"ST{c - 1}", i)
                        tt(f"SP{c}", SPr[:], ST[(c - 1) % 2][:],
                           T["Pc"][:, :, c * L + L - 1:c * L + L].to_broadcast([P, NT, HS]))
                    t.wait(dve, f"U{c}", i)
                    v.done(dve.tensor_copy(U[:], step_ps(f"U{c}")[:, :, 0:HS]), f"U{c}")
                    t.wait(dve, f"SA{c}", i)
                    v.done(dve.tensor_copy(SA[c % 2][:], step_ps(f"SA{c}")[:, :, 0:HS]), f"SA{c}")
                    t.wait(dve, f"S{c}", i)
                    if c > 0:
                        v.wait(dve, f"SP{c}", i)
                        tt(f"ST{c}", ST[c % 2][:], step_ps(f"S{c}")[:, :, 0:HS], SPr[:], ALU.add)
                    else:
                        v.done(dve.tensor_copy(ST[0][:], step_ps("S0")[:, :, 0:HS]), "ST0")
                t.wait(dve, "U4", i)
                v.done(dve.tensor_copy(U[:], step_ps("U4")[:, :, 0:HS]), "U4")
                t.wait(dve, "SA4", i)
                v.done(dve.tensor_copy(SA[0][:], step_ps("SA4")[:, :, 0:HS]), "SA4")
                mj = mJ[:].unsqueeze(2).unsqueeze(1).to_broadcast([P, NT, NB, HS])
                for name, out, src in (("Bx", Bx, "Bn"), ("Kx", Kx, "Kn")):
                    tt(name, out[:], T[src][:, :, SEQ:TOK].unsqueeze(2).to_broadcast([P, NT, NB, HS]), mj)
                t.wait(dve, "bon", i)
                dve.wait_ge(s_in["v"], 16 * i + 16)
                tt("bonus", full(T["k2"]), full(psB), full(V_))
                t.wait(dve, "mean", i)
                tt("cen", full(T["cs"]), full(T["OT"]), full(step_ps("mean")), ALU.subtract)
                s.wait(dve, "rstd", i)
                tt("on", full(T["OT"]), full(T["cs"]), full(T["rn"]))
                v.wait(dve, "on", i)
                tt("ong", full(T["OT"]), full(T["OT"]), prm("lnx_g", i))
                v.wait(dve, "ong", i)
                tt("onb", full(T["OT"]), full(T["OT"]), prm("lnx_b", i), ALU.add)
                v.wait(dve, "onb", i)
                tt("oy", full(T["OT"]), full(T["OT"]), full(T["k2"]), ALU.add)
                v.wait(dve, "oy", i)
                dve.wait_ge(s_in["g"], 16 * i + 16)
                tt("y", full(T["kk"]), full(T["OT"]), full(G_))
                s.wait(dve, "xh", i)
                tt("xl", c_.xlo[:, bass.ds(NT * i, NT), :], full(T["kk"]),
                   c_.xhi[:, bass.ds(NT * i, NT), :], ALU.subtract)

        @block.tensor
        def _(pe):
            pe.wait_ge(masks, c_.n_masks)

            def need(marks, name, i):
                marks.wait(pe, name, i)
                pass_point(pe, "pe")

            def begin(name, i):
                if name != "bon":
                    k = TURNS.index(name)
                    if k >= SETS:
                        eng, mark = TAKEN[TURNS[k - SETS]]
                        who[eng].wait(pe, mark, i)
                pass_point(pe, "pe")
                return step_ps(name)

            def products(name, lhs, rhs, i, n=CH, ident=False):
                out = begin(name, i)
                for m in range(NT):
                    for c in range(n):
                        for h in range(2):
                            r = slice(64 * h, 64 * h + 64)
                            cc = slice(c * L, c * L + L)
                            last = pe.matmul(out[r, m, cc], lhs[r, m, cc],
                                             I2[r, :] if ident else rhs[r, m, cc], start=True, stop=True)
                t.done(last, name)

            def heads(name, i, groups, cols=HS):
                out = begin(name, i)
                for m in range(NT):
                    for h in range(2):
                        r = slice(64 * h, 64 * h + 64)
                        for j, (lhs, rhs, c0, w) in enumerate(groups):
                            last = pe.matmul(out[r, m, c0:c0 + w], lhs(r, m), rhs(r, m), start=(j == 0),
                                             stop=(j == len(groups) - 1))
                t.done(last, name)

            def at(x, c):
                return lambda r, m: x[r, m, c * L:(c + 1) * L]

            def of(x):
                return lambda r, m: x[r, m]

            def over_channels(name, mat, x, i):
                out = begin(name, i)
                for m in range(NT):
                    last = pe.matmul(out[:, m, 0:TOK], mat[:], x[:, m], start=True, stop=True)
                t.done(last, name)

            Tn = T
            with pe.Fori(0, NM // NT) as i:
                need(s, "sq", i)
                over_channels("ss", blk, T["sq"], i)
                need(g, "rk2", i)
                over_channels("bon", blk, T["rk"], i)
                need(v, "Bz", i)
                products("abT", T["Bz"], T["Az"], i)
                products("ab", T["Az"], T["Bz"], i)
                pe.wait_ge(s_in["v"], 16 * i + 16)
                products("Vn", V_, None, i, ident=True)
                need(g, "KpS", i)
                products("Bn", T["Bp"], None, i, ident=True)
                products("Kn", T["Kp"], None, i, ident=True)
                need(v, "Dt", i)
                products("D2", T["Dt"], T["D"], i)
                products("D2t", T["D"], T["Dt"], i)
                need(v, "Kz", i)
                products("akT", T["Kz"], T["Az"], i)
                need(s, "D2t", i)
                products("D3", T["D2t"], T["D"], i)
                products("D3t", T["D2"], T["Dt"], i)
                products("D4", T["D2t"], T["D2"], i)
                products("D4t", T["D2"], T["D2t"], i)
                products("rbT", T["Bz"], T["Rz"], i)
                products("rkT", T["Kz"], T["Rz"], i)
                need(s, "D4t", i)
                need(v, "Wt", i)
                products("Y", T["D4t"], T["W"], i)
                products("Yt", T["D4"], T["Wt"], i)
                need(v, "Yt", i)
                products("E", T["Yt"], T["F"], i, NCH)
                products("Et", T["F"], T["Yt"], i, NCH)
                pe.wait_ge(s0_in, 16 * NT * i + 16 * NT)
                out = begin("S0T", i)
                for m in range(NT):
                    for b in range(NB):
                        for h in range(2):
                            r = slice(64 * h, 64 * h + 64)
                            last = pe.matmul(out[r, m, b * HS:(b + 1) * HS], S0n[r, m, b], I2[r, :],
                                             start=True, stop=True)
                t.done(last, "S0T")
                need(s, "Et", i)
                products("E2", T["Et"], T["E"], i, NCH)
                products("E2t", T["E"], T["Et"], i, NCH)
                need(s, "E2t", i)
                products("E4t", T["E2"], T["E2t"], i, NCH)
                need(s, "E4t", i)
                need(v, "Y", i)
                products("Z4", T["E4t"], T["Y"], i, NCH)
                need(v, "Z4", i)
                products("Z2", T["E2t"], T["Z4"], i, NCH)
                need(v, "Z2", i)
                products("X", T["Et"], T["Z2"], i, NCH)
                need(s, "Kn", i)
                for c in range(NCH):
                    old, new = ST[(c - 1) % 2], SA[c % 2]
                    before = c > 0
                    if before:
                        need(v, f"ST{c - 1}", i)
                    heads(f"U{c}", i, ([(at(T["Az"], c), of(old), 0, HS)] if before else [])
                          + [(at(T["AK"], c), at(T["Vn"], c), 0, HS)])
                    need(v, f"U{c}", i)
                    if c == 0:
                        need(v, "X", i)
                    heads(f"SA{c}", i, [(at(T["X"], c), of(U), 0, HS)])
                    need(v, f"SA{c}", i)
                    heads(f"S{c}", i, [(at(T["Bn"], c), of(new), 0, HS),
                                       (at(T["Kn"], c), at(T["Vn"], c), 0, HS)])
                    heads(f"O{c}", i, ([(of(old), at(T["Rz"], c), 0, L)] if before else [])
                          + [(of(new), at(T["RB"], c), 0, L), (at(T["Vn"], c), at(T["RK"], c), 0, L)])
                need(g, "AzM", i)
                need(s, "S0T", i)

                def nth(x, b):
                    return lambda r, m: x[r, m, b]

                heads("U4", i, [(at(T["AK"], 4), at(T["Vn"], 4), 0, HS)]
                      + [(nth(AzM, b), nth(S0T, b), 0, HS) for b in range(NB)])
                need(v, "U4", i)
                heads("SA4", i, [(at(T["Y"], 4), of(U), 0, HS)])
                need(v, "SA4", i)
                heads("O4", i, [(of(SA[0]), at(T["RB"], 4), 0, L), (at(T["Vn"], 4), at(T["RK"], 4), 0, L)]
                      + [(nth(S0T, b), (lambda b: lambda r, m: T["Rz"][r, m, SEQ + TS * b:SEQ + TS * b + TS])(b),
                          TS * b, TS) for b in range(NB)])
                need(v, "Kx", i)
                need(g, "dP", i)

                def wide(x):
                    return lambda r, m: x[r, m].rearrange("p b k -> p (b k)")

                heads("SN", i, [(of(SA[0]), wide(Bx), 0, NB * HS), (at(T["Vn"], 4), wide(Kx), 0, NB * HS)]
                      + [(nth(S0T, b), nth(dP, b), b * HS, HS) for b in range(NB)])
                need(v, "ST3", i)
                heads("SF", i, [(of(ST[1]), lambda r, m: I2[r, :], 0, HS)])
                need(s, "O4", i)
                over_channels("mean", blkm, T["OT"], i)
                need(s, "csq", i)
                over_channels("var", blkm, T["sq"], i)


def middle(nc, c_, a):
    with ExitStack() as ctx:
        split_buffers(nc, ctx, c_)
        c_.psN = ctx.enter_context(nc.psum_tensor(c_.name("psN"), [P, 512], F32))
        res_stored = ctx.enter_context(nc.semaphore("res_stored"))
        wo, kk, kv, q, g2 = (PB[x] for x in ("wo", "kk", "kv", "q", "g2"))
        block = ctx.enter_context(nc.Block())

        @block.sync
        def _(sp):
            load_group(c_, sp, wo, 0, None)
            for n in (wo, kk, kv, q, g2):
                sp_projection(c_, sp, n, n + 1 if n < g2 else None, first_store=(n == wo))
                if n == kk:
                    sp.dma_start(c_.res_spill.rearrange("m p t -> p m t"), c_.resT[:]).then_inc(res_stored, 16)
            store_group(c_, sp, g2, 3, 4 * g2 + 3, None)
            sp.wait_ge(res_stored, 16)
            sp.wait_ge(c_.stored, 16 * 32 + 1)

        @block.tensor
        def _(pe):
            pe_projection(c_, pe, wo, 12)
            norm_sum_pe(c_, pe, 1)
            pe_projection(c_, pe, kk, 16)
            pe_projection(c_, pe, kv, 16)
            pe_projection(c_, pe, q, 20)
            pe_projection(c_, pe, g2, 20)

        @block.scalar
        def _(act):
            act_projection(c_, act, wo, None)
            act.wait_ge(c_.evacuated, 4 * (4 * wo + 4) + LEAD)
            norm_squares_act(c_, act, 1)
            norm_rsqrt_act(c_, act, 1)
            for x in range(4):
                act_x_quarter(c_, act, 16 + x, x)
            act.preload_act_table(ACT.Sigmoid)
            act_projection(c_, act, kk, None)
            act_projection(c_, act, kv, kk, roll=20)
            act_projection(c_, act, q, kv, rolled=20)
            act_projection(c_, act, g2, q)
            act_gate(c_, act, g2, 4 * g2 + 3)

        @block.vector
        def _(dve):
            dve_projection(c_, dve, wo, None)
            dve_evacuate(c_, dve, wo, 4 * wo + 3, 3)
            dve.wait_ge(c_.rs_ready, 2)
            for x in range(4):
                dve_x_quarter(c_, dve, 16 + x, x, normed(c_, "kv_norm"))
            dve_projection(c_, dve, kk, None)
            dve_projection(c_, dve, kv, kk, roll=20, source=normed(c_, "b_norm"))
            dve_projection(c_, dve, q, kv, rolled=20, source_now=normed(c_, "b_norm"))
            dve_projection(c_, dve, g2, q)
            dve_evacuate(c_, dve, g2, 4 * g2 + 3, 3)


MASKED = -1e30
HG = 4
ZW = P + SEQ

DVE_P = ["z", "sp", "rc", "arg", "y", "qs", "knl"]
ACT_P = ["abs", "exp", "ln", "kn", "vn", "att", "attT", "gs", "knh"]
PE_P = ["z", "kn", "vn", "attT", "o"]


def prompt_attention(nc, c_, a):
    with ExitStack() as ctx:
        def sb(name, shape, dt=F32):
            return ctx.enter_context(nc.sbuf_tensor("pa_" + name, shape, dt))

        def sem(name):
            return ctx.enter_context(nc.semaphore("pa_" + name))

        ins = {x: sb("in_" + x, [P, HG, TOK]) for x in ("q", "kk", "kv", "g2")}
        Q, K, V, G = (ins[x] for x in ("q", "kk", "kv", "g2"))
        kn, vn = sb("kn", [P, HG, 3, P]), sb("vn", [P, HG, 3, P])
        z, w, sp_, rc, att, attT = (sb(x, [P, HG, ZW]) for x in ("z", "w", "sp", "rc", "att", "attT"))
        mask, onesz = sb("mask", [P, ZW]), sb("onesz", [P, SEQ])
        zadd = sb("zadd", [P, HG, ZW])
        bcol, bdiag, brow = sb("bcol", [NHB, 1]), sb("bdiag", [NHB, NHB]), sb("brow", [P, NHB])
        spread = sb("spread", [NHB, P])
        psA = ctx.enter_context(nc.psum_tensor("pa_psA", [P, HG, 512], F32))
        psB = ctx.enter_context(nc.psum_tensor("pa_psB", [P, HG, 512], F32))
        s_in = {x: sem("in_" + x) for x in ins}
        b_in, made, bias_made, kv_stored, b_mm = (sem("b_in"), sem("made"), sem("bias_made"),
                                                  sem("kv_stored"), sem("b_mm"))
        v, t, s = (Marks(sem(x), y) for x, y in (("vector", DVE_P), ("tensor", PE_P), ("scalar", ACT_P)))
        passed, zadd_ready = sem("passed"), sem("zadd_ready")
        n_made = [0]

        block = ctx.enter_context(nc.Block())

        @block.sync
        def _(sp):
            sp.dma_start(bcol[:], a["b_logit_bias"][0].rearrange("(h o) -> h o", o=1)).then_inc(b_in, 16)

            def load(i, prior):
                for x, (m, last) in (("q", (v, "qs")), ("kk", (v, "knl")), ("kv", (t, "vn")), ("g2", (v, "y"))):
                    if prior is not None:
                        if x == "g2":
                            s.wait(sp, "gs", prior)
                            sp.sem_inc(passed, 1)
                        m.wait(sp, last, prior)
                        sp.sem_inc(passed, 1)
                    sp.dma_start(ins[x][:], c_.spill[SP_I[x]].rearrange("m p t -> p m t")
                                 [:, bass.ds(HG * i, HG), :]).then_inc(s_in[x], 16)

            def store(i):
                for x, buf, mark in (("k", kn, "kn"), ("v", vn, "vn")):
                    s.wait(sp, mark, i)
                    sp.sem_inc(passed, 1)
                    for tt in range(2):
                        dst = a[f"o_{x}_p"][0, tt * P:(tt + 1) * P]
                        sp.dma_start(dst[:, bass.ds(HG * i, HG), :], buf[:, :, tt]).then_inc(kv_stored, 16)
                    dst = a[f"o_{x}_s"].rearrange("b t h d -> (b t) h d")
                    sp.dma_start(dst[:, bass.ds(HG * i, HG), :], buf[0:NB * TS, :, 2]).then_inc(kv_stored, 16)

            sp.sem_inc(kv_stored, 1)
            load(0, None)
            with sp.Fori(0, NHB // HG - 1) as i:
                store(i)
                load(i + 1, i)
            store(NHB // HG - 1)
            sp.wait_ge(kv_stored, 16 * 6 * (NHB // HG) + 1)

        @block.gpsimd
        def _(pool):
            def step(ins_):
                n_made[0] += 1
                ins_.then_inc(made, 1)
                pool.wait_ge(made, n_made[0])

            step(pool.memset(mask[:], 0.0))
            step(pool.memset(onesz[:], 1.0))
            step(pool.memset(spread[:], 1.0))
            step(pool.affine_select(out=mask[:, 0:P], in_=mask[:, 0:P], compare_op=ALU.is_gt, fill=MASKED,
                                    base=0, pattern=[[-1, P]], channel_multiplier=1))
            step(pool.affine_select(out=mask[:, P:ZW], in_=mask[:, P:ZW], compare_op=ALU.is_gt, fill=MASKED,
                                    base=P, pattern=[[-1, SEQ]], channel_multiplier=1))
            step(pool.affine_select(out=spread[:], in_=spread[:], compare_op=ALU.is_ge, fill=0.0,
                                    base=0, pattern=[[1, P]], channel_multiplier=-TS))
            step(pool.affine_select(out=spread[:], in_=spread[:], compare_op=ALU.is_ge, fill=0.0,
                                    base=TS - 1, pattern=[[-1, P]], channel_multiplier=TS))

            pool.wait_ge(bias_made, 3)
            def add_mask(i):
                pool.tensor_tensor(zadd[:], mask[:].unsqueeze(1).to_broadcast([P, HG, ZW]),
                                   brow[:, bass.ds(HG * i, HG)].unsqueeze(2).to_broadcast([P, HG, ZW]),
                                   ALU.add).then_inc(zadd_ready, 1)

            add_mask(0)
            with pool.Fori(1, NHB // HG) as i:
                v.wait(pool, "z", i - 1)
                add_mask(i)

        @block.scalar
        def _(act):
            act.preload_act_table_set("natural_log_exp_and_others")
            with act.Fori(0, NHB // HG) as i:
                v.wait(act, "z", i)
                s.done(act.activation(w[:], z[:], ACT.Abs), "abs")
                s.wait(act, "abs", i)
                s.done(act.activation(w[:], w[:], ACT.Exp, scale=-1.0), "exp")
                s.wait(act, "exp", i)
                s.done(act.activation(w[:], w[:], ACT.Ln, bias=c_.ones[:, 0:1]), "ln")
                for x, buf in (("kn", kn), ("vn", vn)):
                    t.wait(act, x, i)
                    act.wait_ge(kv_stored, 16 * 6 * i + 1)
                    for tt in range(3):
                        n = P if tt < 2 else NB * TS
                        last = act.activation(buf[0:n, :, tt], psB[0:n, :, tt * P:(tt + 1) * P], ACT.Copy)
                    s.done(last, x)
                v.wait(act, "arg", i)
                s.done(act.activation(att[:], z[:], ACT.Exp), "att")
                t.wait(act, "attT", i)
                s.done(act.activation(attT[:], psA[:, :, 0:ZW], ACT.Copy), "attT")
                act.wait_ge(s_in["g2"], 16 * i + 16)
                s.done(act.activation(c_.gS[:, bass.ds(HG * i, HG), :], G[:, :, SEQ:TOK], ACT.Copy), "gs")
                act.wait_ge(s_in["kk"], 16 * i + 16)
                s.done(act.activation(c_.kNh[:, bass.ds(HG * i, HG), :], K[:, :, SEQ:TOK], ACT.Copy), "knh")

        @block.vector
        def _(dve):
            dve.wait_ge(b_in, 16)
            dve.tensor_scalar(bdiag[:], c_.ident[0:NHB, 0:NHB], bcol[:, 0:1], None, ALU.mult).then_inc(bias_made, 1)
            dve.wait_ge(b_mm, 1)
            dve.tensor_copy(brow[:], psA[:, 0, 0:NHB]).then_inc(bias_made, 1)
            dve.tensor_copy(c_.biasQ[:], psA[:, 0, NHB:NHB + 1]).then_inc(bias_made, 1)
            dve.wait_ge(made, n_made[0])
            with dve.Fori(0, NHB // HG) as i:
                t.wait(dve, "z", i)
                dve.wait_ge(zadd_ready, i + 1)
                v.done(dve.scalar_tensor_tensor(out=z[:], in0=psA[:, :, 0:ZW], scalar=SCALE, in1=zadd[:],
                                                op0=ALU.mult, op1=ALU.add), "z")
                s.wait(dve, "ln", i)
                v.done(dve.scalar_tensor_tensor(out=sp_[:], in0=z[:], scalar=0.0, in1=w[:], op0=ALU.max,
                                                op1=ALU.add), "sp")
                v.wait(dve, "sp", i)
                for h in range(HG):
                    dve.tensor_tensor_scan(out=rc[:, h, P - 1::-1], data0=onesz[:, 0:P],
                                           data1=sp_[:, h, P - 1::-1], initial=0.0, op0=ALU.mult, op1=ALU.add)
                    last = dve.tensor_tensor_scan(out=rc[:, h, ZW - 1:P - 1:-1], data0=onesz[:],
                                                  data1=sp_[:, h, ZW - 1:P - 1:-1], initial=0.0,
                                                  op0=ALU.mult, op1=ALU.add)
                v.done(last, "rc")
                v.wait(dve, "rc", i)
                v.done(dve.tensor_tensor(z[:], z[:], rc[:], ALU.subtract), "arg")
                t.wait(dve, "o", i)
                dve.wait_ge(s_in["g2"], 16 * i + 16)
                v.done(dve.tensor_tensor(c_.yT[:, bass.ds(HG * i, HG), 0:SEQ], psB[:, :, 0:SEQ],
                                         G[:, :, 0:SEQ], ALU.mult), "y")
                dve.wait_ge(s_in["q"], 16 * i + 16)
                v.done(dve.tensor_scalar(c_.qS[:, bass.ds(HG * i, HG), :], Q[:, :, SEQ:TOK], SCALE, None,
                                         ALU.mult), "qs")
                s.wait(dve, "knh", i)
                v.done(dve.tensor_tensor(c_.kNl[:, bass.ds(HG * i, HG), :], K[:, :, SEQ:TOK],
                                         c_.kNh[:, bass.ds(HG * i, HG), :], ALU.subtract), "knl")

        @block.tensor
        def _(pe):
            pe.wait_ge(made, n_made[0])
            pe.wait_ge(bias_made, 1)
            pe.matmul(psA[:, 0, 0:NHB], c_.ones[0:NHB, :], bdiag[:], start=True, stop=True)
            pe.matmul(psA[:, 0, NHB:NHB + 1], spread[:], bcol[:], start=True, stop=True).then_inc(b_mm, 1)
            pe.wait_ge(bias_made, 3)

            def rows(name, src, i):
                for h in range(HG):
                    for tt in range(3):
                        n = P if tt < 2 else NB * TS
                        last = pe.transpose(psB[0:n, h, tt * P:(tt + 1) * P], src[:, h, tt * P:tt * P + n],
                                            c_.ident[:])
                t.done(last, name)

            with pe.Fori(0, NHB // HG) as i:
                pe.wait_ge(s_in["q"], 16 * i + 16)
                pe.wait_ge(s_in["kk"], 16 * i + 16)
                for h in range(HG):
                    pe.matmul(psA[:, h, 0:P], Q[:, h, 0:P], K[:, h, 0:P], start=True, stop=True)
                    last = pe.matmul(psA[:, h, P:ZW], Q[:, h, P:SEQ], K[:, h, 0:SEQ], start=True, stop=True)
                t.done(last, "z")
                rows("kn", K, i)
                pe.wait_ge(s_in["kv"], 16 * i + 16)
                s.wait(pe, "kn", i)
                rows("vn", V, i)
                s.wait(pe, "att", i)
                for h in range(HG):
                    for j, c0 in enumerate((0, P, 2 * P)):
                        last = pe.transpose(psA[:, h, c0:c0 + P], att[:, h, c0:c0 + P], c_.ident[:])
                t.done(last, "attT")
                s.wait(pe, "vn", i)
                s.wait(pe, "attT", i)
                for h in range(HG):
                    pe.matmul(psB[:, h, 0:P], vn[:, h, 0], attT[:, h, 0:P], start=True, stop=True)
                    pe.matmul(psB[:, h, P:SEQ], vn[:, h, 0], attT[:, h, P:2 * P], start=True, stop=False)
                    last = pe.matmul(psB[:, h, P:SEQ], vn[:, h, 1], attT[:, h, 2 * P:ZW], start=False, stop=True)
                t.done(last, "o")


def closing(nc, c_, a):
    with ExitStack() as ctx:
        weight_buffers(nc, ctx, c_)
        split_buffers(nc, ctx, c_)
        yn = ctx.enter_context(nc.sbuf_tensor("yn", [P, 3, D], F32))
        c_.psN = ctx.enter_context(nc.psum_tensor(c_.name("psN"), [P, 512], F32))
        psT = ctx.enter_context(nc.psum_tensor("out_ps", [P, 3, 512], F32))
        res_in, turned, out_ready, y_stored = (ctx.enter_context(nc.semaphore(x)) for x in
                                               ("res_in", "turned", "out_ready", "y_stored"))
        y_ready = ctx.enter_context(nc.semaphore("y_ready"))
        bo = PB["bo"]
        block = ctx.enter_context(nc.Block())

        @block.sync
        def _(sp):
            load_group(c_, sp, bo, 0, None)
            sp.wait_ge(c_.x_ready, 28)
            sp.dma_start(c_.resT[:], c_.res_spill.rearrange("m p t -> p m t")).then_inc(res_in, 16)
            sp_projection(c_, sp, bo, None, first_store=True)
            sp.wait_ge(out_ready, NM)
            for tt in range(2):
                sp.dma_start(a["o_y_p"][0, tt * P:(tt + 1) * P], yn[:, tt]).then_inc(y_stored, 16)
            sp.dma_start(a["o_y_s"].rearrange("b t d -> (b t) d"), yn[0:NB * TS, 2]).then_inc(y_stored, 16)
            sp.wait_ge(y_stored, 48)

        @block.tensor
        def _(pe):
            pe_projection(c_, pe, bo, 24)
            norm_sum_pe(c_, pe, 2)
            for m in range(NM):
                pe.wait_ge(y_ready, m + 1)
                if m >= 3:
                    pe.wait_ge(out_ready, m - 2)
                for tt in range(3):
                    n = P if tt < 2 else NB * TS
                    last = pe.transpose(psT[0:n, m % 3, tt * P:(tt + 1) * P], c_.yT[:, m, tt * P:tt * P + n],
                                        c_.ident[:])
                last.then_inc(turned, 1)

        @block.scalar
        def _(act):
            for q in range(4):
                act.activation(c_.xhi[:, 4 * q:4 * q + 4], c_.yT[:, 4 * q:4 * q + 4], ACT.Copy).then_inc(c_.xhi_ready, 1)
            act_projection(c_, act, bo, None)
            act.wait_ge(c_.evacuated, 4 * (4 * bo + 4) + LEAD)
            norm_squares_act(c_, act, 2)
            norm_rsqrt_act(c_, act, 2)
            for m in range(NM):
                act.wait_ge(turned, m + 1)
                act.activation(yn[:, 0:2, m * P:(m + 1) * P],
                               psT[:, m % 3, 0:2 * P].rearrange("p (t c) -> p t c", t=2), ACT.Copy)
                act.activation(yn[0:64, 2, m * P:(m + 1) * P], psT[0:64, m % 3, 2 * P:3 * P],
                               ACT.Copy).then_inc(out_ready, 1)

        @block.vector
        def _(dve):
            for q in range(4):
                dve.wait_ge(c_.xhi_ready, 24 + q + 1)
                dve.tensor_tensor(c_.xlo[:, 4 * q:4 * q + 4], c_.yT[:, 4 * q:4 * q + 4],
                                  c_.xhi[:, 4 * q:4 * q + 4], ALU.subtract).then_inc(c_.x_ready, 1)
            dve.wait_ge(res_in, 16)
            dve_projection(c_, dve, bo, None)
            dve_evacuate(c_, dve, bo, 4 * bo + 3, 3)
            dve.wait_ge(c_.rs_ready, 3)
            src = normed(c_, "final_norm")
            for m in range(NM):
                src(dve, c_.yT[:, m], m).then_inc(y_ready, 1)


KB = 4
NBLK = NPAGE // KB
BK = KB * PAGE
NQ = NBLK * 4
NEW = NB * TS
LAG = 5


def sample_attention(nc, c_, a):
    with ExitStack() as ctx:
        def sb(name, shape, dt=F32):
            return ctx.enter_context(nc.sbuf_tensor("sa_" + name, shape, dt))

        def sem(name):
            return ctx.enter_context(nc.semaphore("sa_" + name))

        kraw, vraw = sb("kraw", [P, 4, KB, 512]), sb("vraw", [P, 4, KB, 512])
        vhi, vlo = sb("vhi", [P, 2, KB, 512], F32R), sb("vlo", [P, 2, KB, 512], F32R)
        khi, klo = sb("khi", [P, 2, BK], F32R), sb("klo", [P, 2, BK], F32R)
        qp = sb("qp", [P, 2, 8 * 136], F32R)
        z, w, sps, rc, att = (sb(x, [P, BK]) for x in ("z", "w", "sps", "rc", "att"))
        moved = sb("moved", [P, BK])
        carry, onesz = sb("carry", [P, 1]), sb("onesz", [P, BK])
        st, st_new = sb("st", [P, KB, 2, P], F32R), sb("st_new", [NEW, 2, P], F32R)
        osb = sb("osb", [P, 4, 512])
        vn_raw = sb("vn_raw", [NEW, D])
        vn_hi, vn_lo = sb("vn_hi", [NEW, D], F32R), sb("vn_lo", [NEW, D], F32R)
        mask, mask8 = sb("mask", [P, NB, NEW]), sb("mask8", [P, TS])
        spread, tri = sb("spread", [TS, P]), sb("tri", [TS, TS])
        I2 = sb("I2", [P, 64])
        pt = sb("pt", [1, NB * NPAGE], I32)
        psO = ctx.enter_context(nc.psum_tensor("sa_psO", [P, 4, 512], F32))
        psS = ctx.enter_context(nc.psum_tensor("sa_psS", [P, 2, 512], F32))
        psT = ctx.enter_context(nc.psum_tensor("sa_psT", [P, 2, 512], F32))

        k_in, v_in = [sem(f"k_in{q}") for q in range(4)], [sem(f"v_in{q}") for q in range(4)]
        pt_in, vn_in, made, mask_mm, mask_out = (sem(x) for x in ("pt_in", "vn_in", "made", "mask_mm", "mask_out"))
        vn_hi_ready, vn_lo_ready = sem("vn_hi_ready"), sem("vn_lo_ready")
        keys_turned, keys_hi, keys_lo, keys_scored = (sem(x) for x in ("keys_turned", "keys_hi", "keys_lo", "keys_scored"))
        qp_hi, qp_lo = sem("qp_hi"), sem("qp_lo")
        new_scored = sem("new_scored")
        half_moved, z_ready = sem("half_moved"), sem("z_ready")
        abs_ready, exp_ready, ln_ready, sp_ready = (sem(x) for x in ("abs", "exp", "ln", "sp"))
        rc_ready, carry_ready, arg_ready, att_ready = (sem(x) for x in ("rc", "carry", "arg", "att"))
        new_z = sem("new_z")
        att_turned, st_hi, st_lo = sem("att_turned"), sem("st_hi"), sem("st_lo")
        v_hi, v_lo, values_used = sem("v_hi"), sem("v_lo"), sem("values_used")
        o_copied, final_summed, final_out = sem("o_copied"), sem("final_summed"), sem("final_out")
        passed_sp, passed_pe = sem("passed_sp"), sem("passed_pe")
        n_made = [0]

        def chain(b, c, k=1):
            return 5 * k * b + k * c

        def clocks(b, n, old):
            return ([(old, n + NQ)] if old is not None and n + NQ <= 22 else []) + ([(b, n)] if b is not None else [])

        def sequence(slot):
            def run(eng):
                for n in range(NQ):
                    slot(0, n, None)
                with eng.Fori(1, NB) as b:
                    for n in range(NQ):
                        slot(b, n, b - 1)
                for n in range(NQ, NQ + 7):
                    slot(None, n - NQ, NB - 1)
            return run

        def step_kind(m):
            out = set()
            if m == 2:
                out |= {"new_scores"}
            if m == 3:
                out |= {"att0"}
            for s in range(NBLK):
                if m == 4 * s + 3:
                    out |= {f"zA{s + 1}"}
                if m == 4 * s + 4:
                    out |= {f"zB{s + 1}"}
                if m == 4 * s + 5:
                    out |= {f"att{s + 1}"}
            if m in (20, 22):
                out |= {f"final{(m - 20) // 2}"}
            if 18 <= m <= 21:
                out |= {f"copy{m - 18}"}
            return out

        block = ctx.enter_context(nc.Block())

        @block.sync
        def _(sp):
            sp.dma_start(pt[:], a["page_table"].rearrange("(o b) n -> o (b n)", o=1)).then_inc(pt_in, 16)
            sp.dma_start(vn_raw[:], a["o_v_s"].rearrange("b t h d -> (b t) (h d)")).then_inc(vn_in, 16)
            sp.wait_ge(pt_in, 16)

            def load(ring, name, arrived, b, n):
                s, gg = n // 4, n % 4
                sp.sem_inc(passed_sp, 1)
                for pg in range(KB):
                    col = KB * (NBLK - 1 - s) + pg
                    page = sp.value_load(pt[0:1, bass.ds(NPAGE * b + col, 1)])
                    src = a[name][bass.ds(page, 1), :, 4 * gg:4 * gg + 4, :].rearrange("o s h d -> (o s) (h d)")
                    sp.dma_start(ring[:, gg, pg], src).then_inc(arrived[gg], 16)

            def slot(b, n, old):
                if b is not None:
                    if not (isinstance(b, int) and 4 * n < 16):
                        sp.wait_ge(keys_turned, 64 * b + 4 * n - 12)
                    load(kraw, "cache_k", k_in, b, n)
                vb, p = (b, n - 4) if n >= 4 else (old, n + 12)
                if vb is not None:
                    if not (isinstance(vb, int) and vb == 0 and p < 4):
                        sp.wait_ge(v_lo, 32 * vb + 2 * p - 6)
                    load(vraw, "cache_v", v_in, vb, p)

            for n in range(NQ):
                slot(0, n, None)
            with sp.Fori(1, NB) as b:
                for n in range(NQ):
                    slot(b, n, b - 1)
            for n in range(4):
                slot(None, n, NB - 1)

        @block.gpsimd
        def _(pool):
            def step(ins_):
                n_made[0] += 1
                ins_.then_inc(made, 1)
                pool.wait_ge(made, n_made[0])

            step(pool.memset(onesz[:], 1.0))
            for g in range(2):
                step(pool.memset(qp[:, g].bitcast(F32), 0.0))
                step(pool.tensor_copy(I2[64 * g:64 * g + 64, :], c_.ident[64 * g:64 * g + 64, 64 * g:64 * g + 64]))
            step(pool.memset(tri[:], 0.0))
            step(pool.affine_select(out=tri[:], in_=tri[:], compare_op=ALU.is_gt, fill=MASKED, base=0,
                                    pattern=[[-1, TS]], channel_multiplier=1))
            step(pool.memset(spread[:], 0.0))
            step(pool.affine_select(out=spread[:].rearrange("q (h r) -> q h r", r=TS),
                                    in_=spread[:].rearrange("q (h r) -> q h r", r=TS),
                                    compare_op=ALU.not_equal, fill=1.0, base=0,
                                    pattern=[[0, NHB], [1, TS]], channel_multiplier=-1))
            step(pool.memset(mask[:], MASKED))
            pool.wait_ge(mask_out, 1)
            for b in range(NB):
                step(pool.tensor_copy(mask[:, b, TS * b:TS * b + TS], mask8[:]))

            def slot(b, n, old):
                vb, p = (b, n - 4) if n >= 4 else (old, n + 12)
                if vb is None:
                    return
                for hf in range(2):
                    pool.wait_ge(v_hi, 32 * vb + 2 * p + hf + 1)
                    r = slice(2 * hf, 2 * hf + 2)
                    pool.tensor_tensor(vlo[:, p % 2, r], vraw[:, p % 4, r], vhi[:, p % 2, r],
                                       ALU.subtract).then_inc(v_lo, 1)

            for n in range(NQ):
                slot(0, n, None)
            with pool.Fori(1, NB) as b:
                for n in range(NQ):
                    slot(b, n, b - 1)
            for n in range(4):
                slot(None, n, NB - 1)

        def half_source(b, c, half, rows):
            if c == 0:
                return psT[rows, plan[window_of(b)]["new_scores"], NEW * half:NEW * half + NEW]
            return psS[rows, half, :]

        def width(c):
            return NEW if c == 0 else BK

        plan = turn_plan(step_kind)

        def bank(b, x):
            return plan[window_of(b)]["key", x]

        def qp_view(g, part):
            return qp[:, g].rearrange("p (i x) -> p i x", x=136)[:, :, 64 * part:64 * part + TS]

        @block.scalar
        def _(act):
            act.preload_act_table_set("natural_log_exp_and_others")
            act.wait_ge(vn_in, 16)
            act.activation(vn_hi[:], vn_raw[:], ACT.Copy).then_inc(vn_hi_ready, 1)
            act.wait_ge(made, 5)

            def keys(b, x):
                act.wait_ge(keys_turned, 64 * b + x + 1)
                if not (isinstance(b, int) and x < 2):
                    act.wait_ge(keys_scored, 64 * b + x - 1)
                act.activation(khi[:, x % 2], psT[:, bank(b, x)], ACT.Copy).then_inc(keys_hi, 1)

            def move(b, c, half):
                if c == 0:
                    act.wait_ge(new_scored, b + 1)
                else:
                    act.wait_ge(keys_scored, 64 * b + 16 * (c - 1) + 8 * half + 8)
                if c > 0 or not (isinstance(b, int) and b == 0):
                    act.wait_ge(z_ready, chain(b, c, 2) - 1 + half)
                dst, src = (slice(0, 64), slice(64, 128)) if half == 0 else (slice(64, 128), slice(0, 64))
                act.activation(moved[dst, 0:width(c)], half_source(b, c, half, src),
                               ACT.Copy).then_inc(half_moved, 1)

            def chain_step(b, c, name):
                n = slice(0, width(c))
                if name == "abs":
                    act.wait_ge(z_ready if c else new_z, chain(b, c, 2) + 2 if c else b + 1)
                    act.activation(w[:, n], z[:, n], ACT.Abs).then_inc(abs_ready, 1)
                elif name == "exp":
                    act.wait_ge(abs_ready, chain(b, c) + 1)
                    act.activation(w[:, n], w[:, n], ACT.Exp, scale=-1.0).then_inc(exp_ready, 1)
                elif name == "ln":
                    act.wait_ge(exp_ready, chain(b, c) + 1)
                    act.activation(w[:, n], w[:, n], ACT.Ln, bias=c_.ones[:, 0:1]).then_inc(ln_ready, 1)

            def slot(b, n, old):
                now = clocks(b, n, old)
                steps = [(bb, x) for bb, m in now for x in sorted(step_kind(m))]
                for bb, x in steps:
                    if x[:3] == "att":
                        c = int(x[3])
                        act.wait_ge(arg_ready, chain(bb, c) + 1)
                        if c or not (isinstance(bb, int) and bb == 0):
                            act.wait_ge(att_turned, chain(bb, c))
                        act.activation(att[:, 0:width(c)], z[:, 0:width(c)], ACT.Exp).then_inc(att_ready, 1)
                for bb, x in steps:
                    if x[0] == "z":
                        move(bb, int(x[2]), 0 if x[1] == "A" else 1)
                chains = [(bb, int(x[2])) for bb, x in steps if x[:2] == "zB"]
                new = [bb for bb, x in steps if x == "new_scores"]
                if b is not None and n == 0:
                    if old is not None:
                        act.wait_ge(keys_scored, 64 * b)
                    for g in range(2):
                        ins_ = act.activation(qp_view(g, 0), c_.qS[:, 8 * g:8 * g + 8, bass.ds(TS * b, TS)], ACT.Copy)
                    ins_.then_inc(qp_hi, 1)
                for j in range(4):
                    if b is not None:
                        keys(b, 4 * n + j)
                    for bb, c in chains:
                        if j < 3:
                            chain_step(bb, c, ("abs", "exp", "ln")[j])
                    for bb in new:
                        if j == 1:
                            move(bb, 0, 0)
                            move(bb, 0, 1)
                        if j == 2:
                            chain_step(bb, 0, "abs")
                        if j == 3:
                            chain_step(bb, 0, "exp")
                            chain_step(bb, 0, "ln")
                    if j == 1:
                        for bb, x in steps:
                            if x[:3] == "att":
                                c = int(x[3])
                                act.wait_ge(att_turned, chain(bb, c) + 1)
                                if c == 0:
                                    if not isinstance(bb, int):
                                        act.wait_ge(values_used, 16 * bb - 12)
                                    dst = st_new[:, :, 0:64]
                                    src = psT[0:NEW, plan[window_of(b)][x], 0:P].rearrange("k (g r) -> k g r", g=2)
                                else:
                                    if c > 1 or not isinstance(bb, int):
                                        act.wait_ge(values_used, 16 * bb + 4 * c - 4)
                                    dst = st[:, :, :, 0:64]
                                    src = psT[:, plan[window_of(b)][x], :].rearrange("k (t g r) -> k t g r", t=KB, g=2)
                                act.activation(dst, src, ACT.Copy).then_inc(st_hi, 1)
                    if j in (1, 2):
                        vb, p = (b, n - 4) if n >= 4 else (old, n + 12)
                        if vb is not None:
                            act.wait_ge(v_in[p % 4], 64 * (4 * vb + p // 4 + 1))
                            if j == 1 and not (isinstance(vb, int) and vb == 0 and p < 2):
                                act.wait_ge(values_used, 16 * vb + p - 1)
                            r = slice(2 * (j - 1), 2 * j)
                            act.activation(vhi[:, p % 2, r], vraw[:, p % 4, r], ACT.Copy).then_inc(v_hi, 1)

            sequence(slot)(act)

        @block.vector
        def _(dve):
            dve.wait_ge(mask_mm, 1)
            dve.tensor_copy(mask8[:], psT[:, 0, 0:TS]).then_inc(mask_out, 1)
            dve.wait_ge(vn_hi_ready, 1)
            dve.tensor_tensor(vn_lo[:], vn_raw[:], vn_hi[:], ALU.subtract).then_inc(vn_lo_ready, 1)
            dve.wait_ge(made, n_made[0])

            def keys(b, x):
                dve.wait_ge(keys_hi, 64 * b + x + 1)
                dve.tensor_tensor(klo[:, x % 2], psT[:, bank(b, x)], khi[:, x % 2],
                                  ALU.subtract).then_inc(keys_lo, 1)

            def z_half(b, c, half):
                dve.wait_ge(half_moved, chain(b, c, 2) + (half + 1 if c else 2))
                if c > 0 or not (isinstance(b, int) and b == 0):
                    dve.wait_ge(att_ready, chain(b, c))
                r = slice(64 * half, 64 * half + 64)
                dve.scalar_tensor_tensor(out=z[r, 0:width(c)], in0=half_source(b, c, half, r),
                                         scalar=c_.biasQ[r, 0:1], in1=moved[r, 0:width(c)], op0=ALU.add,
                                         op1=ALU.add).then_inc(z_ready, 1)

            def chain_rest(b, c):
                n = slice(0, width(c))
                dve.wait_ge(ln_ready, chain(b, c) + 1)
                dve.scalar_tensor_tensor(out=sps[:, n], in0=z[:, n], scalar=0.0, in1=w[:, n], op0=ALU.max,
                                         op1=ALU.add).then_inc(sp_ready, 1)
                dve.wait_ge(sp_ready, chain(b, c) + 1)
                last = width(c) - 1
                if c:
                    dve.wait_ge(carry_ready, chain(b, c))
                dve.tensor_tensor_scan(out=rc[:, last::-1], data0=onesz[:, n], data1=sps[:, last::-1],
                                       initial=0.0 if c == 0 else carry[:, 0:1], op0=ALU.mult,
                                       op1=ALU.add).then_inc(rc_ready, 1)
                dve.wait_ge(rc_ready, chain(b, c) + 1)
                dve.tensor_copy(carry[:], rc[:, 0:1]).then_inc(carry_ready, 1)
                dve.tensor_tensor(z[:, n], z[:, n], rc[:, n], ALU.subtract).then_inc(arg_ready, 1)

            def slot(b, n, old):
                steps = [(bb, x) for bb, m in clocks(b, n, old) for x in sorted(step_kind(m))]
                for bb, x in steps:
                    if x[0] == "z":
                        z_half(bb, int(x[2]), 0 if x[1] == "A" else 1)
                    if x[:4] == "copy":
                        gg = int(x[4])
                        dve.wait_ge(values_used, 16 * bb + 12 + gg + 1)
                        dve.tensor_copy(osb[:, gg], psO[:, gg]).then_inc(o_copied, 1)
                if b is not None and n == 0:
                    dve.wait_ge(qp_hi, b + 1)
                    for g in range(2):
                        ins_ = dve.tensor_tensor(qp_view(g, 1), c_.qS[:, 8 * g:8 * g + 8, bass.ds(TS * b, TS)],
                                                 qp_view(g, 0), ALU.subtract)
                    ins_.then_inc(qp_lo, 1)
                for j in range(4):
                    if b is not None:
                        keys(b, 4 * n + j)
                    if j != 1:
                        continue
                    for bb, x in steps:
                        if x == "new_scores":
                            z_half(bb, 0, 0)
                            z_half(bb, 0, 1)
                            dve.wait_ge(z_ready, chain(bb, 0, 2) + 2)
                            dve.tensor_tensor(z[:, 0:NEW], z[:, 0:NEW],
                                              mask[:, bass.ds(bb, 1), :].rearrange("p o k -> p (o k)"),
                                              ALU.add).then_inc(new_z, 1)
                        if x[:3] == "att":
                            c = int(x[3])
                            dve.wait_ge(st_hi, chain(bb, c) + 1)
                            if c == 0:
                                src = psT[0:NEW, plan[window_of(b)][x], 0:P].rearrange("k (g r) -> k g r", g=2)
                                dve.tensor_tensor(st_new[:, :, 64:128], src, st_new[:, :, 0:64],
                                                  ALU.subtract).then_inc(st_lo, 1)
                            else:
                                src = psT[:, plan[window_of(b)][x], :].rearrange("k (t g r) -> k t g r", t=KB, g=2)
                                dve.tensor_tensor(st[:, :, :, 64:128], src, st[:, :, :, 0:64],
                                                  ALU.subtract).then_inc(st_lo, 1)
                        if x[:5] == "final":
                            f = int(x[5])
                            dve.wait_ge(final_summed, 2 * bb + f + 1)
                            h = slice(8 * f, 8 * f + 8)
                            dve.tensor_tensor(c_.yT[:, h, bass.ds(SEQ + TS * bb, TS)],
                                              psT[:, plan[window_of(b)][x], 0:64].rearrange("p (h q) -> p h q", h=8),
                                              c_.gS[:, h, bass.ds(TS * bb, TS)], ALU.mult).then_inc(final_out, 1)
                for bb, x in steps:
                    if x == "new_scores":
                        chain_rest(bb, 0)
                    if x[:2] == "zB":
                        chain_rest(bb, int(x[2]))

            sequence(slot)(dve)

        @block.tensor
        def _(pe):
            pe.wait_ge(made, 9)
            pe.matmul(psT[:, 0, 0:TS], spread[:], tri[:], start=True, stop=True).then_inc(mask_mm, 1)
            pe.wait_ge(mask_out, 1)
            pe.wait_ge(made, n_made[0])
            pe.wait_ge(vn_lo_ready, 1)
            user = [None, None]
            turn = [1]

            def take_bank(sem_, per, k, b):
                t = turn[0] % 2
                turn[0] += 1
                if user[t] is not None:
                    s_, per_, k_, b_ = user[t]
                    pe.wait_ge(s_, per_ * b_ + k_)
                user[t] = (sem_, per, k, b)
                return t

            def turn_keys(b, x):
                gg, j = (x // 4) % 4, x % 4
                if j == 0:
                    pe.wait_ge(k_in[gg], 64 * (4 * b + x // 16 + 1))
                t = take_bank(keys_lo, 64, x + 1, b)
                assert t == bank(b, x)
                for pg in range(KB):
                    last = pe.transpose(psT[:, t, pg * P:(pg + 1) * P], kraw[:, gg, pg, j * P:(j + 1) * P],
                                        c_.ident[:])
                last.then_inc(keys_turned, 1)

            def score(b, x):
                s, gg, j = x // 16, (x // 4) % 4, x % 4
                half, i = gg // 2, 4 * (gg % 2) + j
                pe.wait_ge(keys_lo, 64 * b + x + 1)
                if x == 0:
                    pe.wait_ge(qp_lo, b + 1)
                if i == 0:
                    c = s + 1
                    if s > 0 or not (isinstance(b, int) and b == 0):
                        pe.wait_ge(z_ready, chain(b, c, 2) + half - 1 if s > 0 else 10 * b - 1 + half)
                lhs = qp[:, half, i * P:(i + 1) * P]
                pe.matmul(psS[:, half, :], lhs, khi[:, x % 2], start=(i == 0), stop=False)
                pe.matmul(psS[:, half, :], lhs, klo[:, x % 2], start=False, stop=(i == 7)).then_inc(keys_scored, 1)

            def extra(b, bb, x):
                if x == "new_scores":
                    t = take_bank(new_z, 1, 1, bb)
                    assert t == plan[window_of(b)][x]
                    for half in range(2):
                        for i in range(8):
                            lhs = qp[:, half, i * P:(i + 1) * P]
                            out = psT[:, t, NEW * half:NEW * half + NEW]
                            pe.matmul(out, lhs, c_.kNh[:, 8 * half + i], start=(i == 0), stop=False)
                            last = pe.matmul(out, lhs, c_.kNl[:, 8 * half + i], start=False, stop=(i == 7))
                    last.then_inc(new_scored, 1)
                elif x[:3] == "att":
                    c = int(x[3])
                    t = take_bank(st_lo, 5, c + 1, bb)
                    assert t == plan[window_of(b)][x]
                    pe.wait_ge(att_ready, chain(bb, c) + 1)
                    if c == 0:
                        pe.sem_inc(passed_pe, 1)
                        last = pe.transpose(psT[0:NEW, t, 0:P], att[:, 0:NEW], c_.ident[:])
                    else:
                        for pg in range(KB):
                            last = pe.transpose(psT[:, t, pg * P:(pg + 1) * P], att[:, pg * P:(pg + 1) * P],
                                                c_.ident[:])
                    last.then_inc(att_turned, 1)
                elif x[:5] == "final":
                    f = int(x[5])
                    t = take_bank(final_out, 2, f + 1, bb)
                    assert t == plan[window_of(b)][x]
                    pe.wait_ge(o_copied, 4 * bb + 2 * f + 2)
                    for i in range(8):
                        h = 8 * f + i
                        last = pe.matmul(psT[:, t, i * TS:(i + 1) * TS], osb[:, h // 4, (h % 4) * P:(h % 4 + 1) * P],
                                         I2[:, i * TS:(i + 1) * TS], start=True, stop=True)
                    last.then_inc(final_summed, 1)

            def values(b, p):
                gg, c = p % 4, p // 4 + 1
                half = gg // 2
                if p < 4:
                    pe.wait_ge(st_lo, chain(b, 0) + 1)
                    if not (isinstance(b, int) and b == 0):
                        pe.wait_ge(o_copied, 4 * b - 3 + gg)
                    for j, x in enumerate((vn_hi, vn_lo)):
                        pe.matmul(psO[:, gg], st_new[:, half, :], x[:, 512 * gg:512 * gg + 512],
                                  start=(j == 0), stop=False)
                pe.wait_ge(st_lo, chain(b, c) + 1)
                pe.wait_ge(v_lo, 32 * b + 2 * p + 2)
                for pg in range(KB):
                    for j, x in enumerate((vhi, vlo)):
                        last = pe.matmul(psO[:, gg], st[:, pg, half, :], x[:, p % 2, pg], start=False,
                                         stop=(p >= 12 and pg == KB - 1 and j == 1))
                last.then_inc(values_used, 1)

            def slot(b, n, old):
                steps = [(bb, x) for bb, m in clocks(b, n, old) for x in sorted(step_kind(m))]
                if b is not None:
                    turn_keys(b, 4 * n)
                    turn_keys(b, 4 * n + 1)
                    score(b, 4 * n)
                for bb, x in steps:
                    extra(b, bb, x)
                if b is not None:
                    turn_keys(b, 4 * n + 2)
                    score(b, 4 * n + 1)
                    turn_keys(b, 4 * n + 3)
                    score(b, 4 * n + 2)
                vb, p = (b, n - LAG) if n >= LAG else (old, n + NQ - LAG)
                if vb is not None and p < NQ:
                    values(vb, p)
                if b is not None:
                    score(b, 4 * n + 3)

            for n in range(NQ):
                slot(0, n, None)
            with pe.Fori(1, NB) as b:
                user[:] = [(s_, per, k, b - 1) for s_, per, k, _ in user]
                for n in range(NQ):
                    slot(b, n, b - 1)
            user[:] = [(s_, per, k, NB - 1) for s_, per, k, _ in user]
            for n in range(7):
                slot(None, n, NB - 1)


def turn_plan(step_kind):
    plans = {}
    for window, start in (("first", 1), ("loop", 0), ("rest", 0)):
        plan, t = {}, start
        for n in range(NQ):
            if window != "rest":
                plan["key", 4 * n], plan["key", 4 * n + 1] = t % 2, (t + 1) % 2
                t += 2
            for m in {"first": (n,), "loop": (n + NQ, n), "rest": (n + NQ,)}[window]:
                for x in sorted(step_kind(m)):
                    if x == "new_scores" or x[:3] == "att" or x[:5] == "final":
                        plan[x] = t % 2
                        t += 1
            if window != "rest":
                plan["key", 4 * n + 2], plan["key", 4 * n + 3] = t % 2, (t + 1) % 2
                t += 2
        assert window == "rest" or t % 2 == 0
        plans[window] = plan
    return plans


def window_of(b):
    return "rest" if b is None else "first" if isinstance(b, int) else "loop"


def program(nc, a):
    c_ = Core()
    with ExitStack() as ctx:
        def sb(name, shape, dt=F32):
            return ctx.enter_context(nc.sbuf_tensor(name, shape, dt))

        def sem(name):
            return ctx.enter_context(nc.semaphore(name))

        used = set()

        def name(x):
            while x in used:
                x += "_"
            used.add(x)
            return x

        c_.name = name
        c_.W = {"r": a["a_w_rkvg"][0, 0], "k": a["a_w_rkvg"][0, 1], "v": a["a_w_rkvg"][0, 2],
                "g": a["a_w_rkvg"][0, 3], "wo": a["a_w_o"][0], "kk": a["w_kv"][:, 0:D],
                "kv": a["w_kv"][:, D:2 * D], "q": a["b_w_qg"][0][:, 0:D],
                "g2": a["b_w_qg"][0][:, D:2 * D], "bo": a["b_w_o"][0]}
        c_.spill = nc.dram_tensor("spill", [len(SPILL), NM, P, TOK], F32, kind="Internal").ap()
        c_.res_spill = nc.dram_tensor("res_spill", [NM, P, TOK], F32, kind="Internal").ap()
        c_.ident = sb("ident", [P, P])
        c_.ones = sb("ones", [P, P])
        c_.consts = sb("consts", [P, 4])
        c_.vec = sb("vec", [P, 3 * P])
        c_.resT = sb("resT", [P, NM, TOK])
        c_.wlo_ready = sem("wlo_ready")
        c_.whi_ready = sem("whi_ready")
        c_.evacuated = sem("evacuated")
        c_.stored = sem("stored")
        c_.bank_full = sem("bank_full")
        c_.chunk_used = sem("chunk_used")
        c_.sig_ready = sem("sig_ready")
        c_.xtmp_ready = sem("xtmp_ready")
        c_.xhi_ready = sem("xhi_ready")
        c_.x_ready = sem("x_ready")
        c_.sq_ready = sem("sq_ready")
        c_.sq_summed = sem("sq_summed")
        c_.ln_ready = sem("ln_ready")
        c_.rs_ready = sem("rs_ready")
        c_.w_in = [sem(f"w_in{q}") for q in range(4)]
        with ExitStack() as ch:
            weight_buffers(nc, ch, c_)
            c_.hT = ch.enter_context(nc.sbuf_tensor("hT", [P, NM, TOK], F32))
            c_.delta = ch.enter_context(nc.sbuf_tensor("delta", [P, NM, TOK], F32))
            opening(nc, c_, a)
            x_buffers(nc, ch, c_)
            mixing_projections(nc, c_, a)
        with ExitStack() as cx:
            x_buffers(nc, cx, c_)
            recurrence(nc, c_, a)
            weight_buffers(nc, cx, c_)
            middle(nc, c_, a)
        c_.yT = c_.resT
        with ExitStack() as ca:
            c_.qS = ca.enter_context(nc.sbuf_tensor("qS", [P, NHB, NB * TS], F32))
            c_.gS = ca.enter_context(nc.sbuf_tensor("gS", [P, NHB, NB * TS], F32))
            c_.kNh = ca.enter_context(nc.sbuf_tensor("kNh", [P, NHB, NB * TS], F32R))
            c_.kNl = ca.enter_context(nc.sbuf_tensor("kNl", [P, NHB, NB * TS], F32R))
            c_.biasQ = ca.enter_context(nc.sbuf_tensor("biasQ", [P, 1], F32))
            prompt_attention(nc, c_, a)
            sample_attention(nc, c_, a)
        x_buffers(nc, ctx, c_)
        closing(nc, c_, a)


OUTS = (("o_y_p", (1, SEQ, D)), ("o_y_s", (NB, TS, D)), ("o_shift_p", (1, 1, D)),
        ("o_wkv_p", (1, 1, D // HS, HS, HS)), ("o_k_p", (1, SEQ, NHB, DH)), ("o_v_p", (1, SEQ, NHB, DH)),
        ("o_shift_s", (1, NB, D)), ("o_wkv_s", (1, NB, D // HS, HS, HS)),
        ("o_k_s", (NB, TS, NHB, DH)), ("o_v_s", (NB, TS, NHB, DH)))


def vector_views(a):
    for i in range(6):
        a[f"mu{i}"] = a["a_mu"][0, i]
    for x in ("w0", "a0", "k_k", "k_a", "lnx_g", "lnx_b"):
        a[x] = a["a_" + x][0]
    for x in ("a_norm", "b_norm"):
        a[x] = a[x][0]
    a["r_k"] = a["a_r_k"][0].rearrange("h n -> (h n)")


def kernel(**inputs):
    import numpy as np
    import concourse.bacc as bacc
    from concourse.bass_utils import run_bass_kernel_spmd

    nc = bacc.Bacc("TRN2", target_bir_lowering=False, num_devices=1)
    a, arrays = {}, {}
    for name, value in inputs.items():
        arrays["in_" + name] = np.ascontiguousarray(value)
        a[name] = nc.dram_tensor("in_" + name, arrays["in_" + name].shape,
                                 mybir.dt.from_np(arrays["in_" + name].dtype), kind="ExternalInput").ap()
    for name, shape in OUTS:
        a[name] = nc.dram_tensor(name, shape, F32, kind="ExternalOutput").ap()
    vector_views(a)
    program(nc, a)
    r = run_bass_kernel_spmd(nc, [arrays], core_ids=[0])
    return tuple(r.results[0][name] for name, _ in OUTS)
```

```python
import math
from contextlib import ExitStack

import concourse.bass as bass
from concourse import mybir

F32 = mybir.dt.float32
F32R = mybir.dt.float32r
I32 = mybir.dt.int32
ALU = mybir.AluOpType
ACT = mybir.ActivationFunctionType

P = 128
D = 2048
NM = D // P
SEQ, NB, TS = 256, 8, 8
TOK = SEQ + NB * TS
LORA = 96
NHB, DH = 16, 128
PAGE, NPAGE = 128, 16
L = 64
NCH = SEQ // L
RMS_EPS, LNX_EPS = 1e-6, 64e-5
DECAY = math.exp(-0.5)
SCALE = 1.0 / math.sqrt(DH)

VECS = ["a_norm", "kv_norm", "b_norm", "final_norm", "mu0", "mu1", "mu2", "mu3", "mu4", "mu5",
        "w0", "a0", "k_k", "k_a", "r_k", "lnx_g", "lnx_b"]
VEC = {n: i for i, n in enumerate(VECS)}

PROJ = ["r", "k", "v", "g", "wo", "kk", "kv", "q", "g2", "bo"]
PB = {n: i for i, n in enumerate(PROJ)}
GATED = ("g", "g2")
RESIDUAL = ("wo", "bo")
SPILL = [n for n in PROJ if n not in RESIDUAL] + ["s", "a"]
SP_I = {n: i for i, n in enumerate(SPILL)}

QC = 4
GW = 512
LEAD = 4


class Core:
    pass


def weight_buffers(nc, ctx, c_):
    def sb(name, shape):
        return ctx.enter_context(nc.sbuf_tensor(c_.name(name), shape, F32))

    c_.wraw = sb("wraw", [P, 4, QC, GW])
    c_.stage = sb("stage", [P, 4, TOK])
    c_.sig = sb("sig", [P, 4, TOK])
    c_.xtmp = sb("xtmp", [P, 2, 4, TOK])
    c_.xsq = c_.xtmp[:, 0]
    c_.rs = sb("rs", [P, TOK])


def x_buffers(nc, ctx, c_):
    c_.xhi = ctx.enter_context(nc.sbuf_tensor(c_.name("xhi"), [P, NM, TOK], F32R))
    c_.xlo = ctx.enter_context(nc.sbuf_tensor(c_.name("xlo"), [P, NM, TOK], F32R))


def weight_chunk(c_, n, grp, q):
    w = c_.W[PROJ[n]].rearrange("(q k p) n -> q p k n", k=QC, p=P)
    return w[q][:, :, bass.ds(grp * GW, GW)]


def load_group(c_, sp, n, grp, prior):
    for q in range(4):
        if prior is not None:
            sp.wait_ge(c_.wlo_ready, 4 * prior + q + 1)
        sp.dma_start(c_.wraw[:, q], weight_chunk(c_, n, grp, q)).then_inc(c_.w_in[q], 16)


def store_group(c_, sp, n, grp, g_all, spilled):
    sp.wait_ge(c_.evacuated, 4 * g_all + 4 + LEAD)
    dst = c_.spill[SP_I[PROJ[n]]].rearrange("m p t -> p m t")[:, bass.ds(4 * grp, 4), :]
    sp.dma_start(dst, c_.stage[:]).then_inc(c_.stored, 16)


def sp_projection(c_, sp, n, nxt, first_store):
    spilled = PROJ[n] not in RESIDUAL
    prev_spilled = n > 0 and PROJ[n - 1] not in RESIDUAL and not first_store
    load_group(c_, sp, n, 1, 4 * n)
    if prev_spilled:
        store_group(c_, sp, n - 1, 3, 4 * n - 1, None)
    with sp.Fori(1, 3) as g:
        load_group(c_, sp, n, g + 1, 4 * n + g)
        if spilled:
            store_group(c_, sp, n, g - 1, 4 * n + g - 1, None)
    if nxt is not None:
        load_group(c_, sp, nxt, 0, 4 * n + 3)
    if spilled:
        store_group(c_, sp, n, 2, 4 * n + 2, None)


def pe_projection(c_, pe, n, x_base):
    with pe.Fori(0, 4) as grp:
        g_all = grp + 4 * n
        for q in range(4):
            s = q % 2
            pe.wait_ge(c_.wlo_ready, 4 * g_all + q + 1)
            pe.wait_ge(c_.x_ready, x_base + q + 1)
            for m in range(4):
                if q == 0:
                    pe.wait_ge(c_.evacuated, 4 * g_all + m - 3 + LEAD)
                for k in range(QC):
                    kc = QC * q + k
                    wh = c_.whi[:, s, k, m * P:(m + 1) * P]
                    wl = c_.wlo[:, s, k, m * P:(m + 1) * P]
                    out = c_.psP[:, m, 0:TOK]
                    pe.matmul(out, wh, c_.xhi[:, kc, :], start=(kc == 0), stop=False)
                    pe.matmul(out, wh, c_.xlo[:, kc, :], start=False, stop=False)
                    last = pe.matmul(out, wl, c_.xhi[:, kc, :], start=False, stop=(kc == NM - 1))
                if q == 3:
                    last.then_inc(c_.bank_full, 1)
            if q < 3:
                last.then_inc(c_.chunk_used, 1)


def wait_chunk_used(c_, eng, g_all, q):
    if q < 3:
        eng.wait_ge(c_.chunk_used, 3 * g_all + q + 1)
    else:
        eng.wait_ge(c_.bank_full, 4 * g_all + 4)


def act_split(c_, act, g_all, q):
    act.wait_ge(c_.w_in[q], 16 * g_all + 16)
    if isinstance(g_all, int) and g_all == 0 and q < 2:
        pass
    elif q == 0:
        act.wait_ge(c_.chunk_used, 3 * g_all)
    elif q == 1:
        act.wait_ge(c_.bank_full, 4 * g_all)
    else:
        act.wait_ge(c_.chunk_used, 3 * g_all + q - 1)
    act.activation(c_.whi[:, q % 2], c_.wraw[:, q], ACT.Copy).then_inc(c_.whi_ready, 1)


def dve_split(c_, dve, g_all, q):
    dve.wait_ge(c_.whi_ready, 4 * g_all + q + 1)
    dve.tensor_tensor(c_.wlo[:, q % 2], c_.wraw[:, q], c_.whi[:, q % 2],
                      ALU.subtract).then_inc(c_.wlo_ready, 1)


def act_gate(c_, act, n, g_all):
    if n is None or PROJ[n] not in GATED:
        return
    for m in range(4):
        act.wait_ge(c_.bank_full, 4 * g_all + m + 1)
        act.wait_ge(c_.evacuated, 4 * g_all + m - 3 + LEAD)
        act.activation(c_.sig[:, m], c_.psP[:, m, 0:TOK], ACT.Sigmoid).then_inc(c_.sig_ready, 1)


def dve_evacuate(c_, dve, n, g_all, grp):
    if n is None:
        return
    name = PROJ[n]
    for m in range(4):
        dve.wait_ge(c_.bank_full, 4 * g_all + m + 1)
        ps = c_.psP[:, m, 0:TOK]
        if name in RESIDUAL:
            r = c_.resT[:, bass.ds(4 * grp + m, 1), :].rearrange("p a t -> p (a t)")
            dve.tensor_tensor(r, ps, r, ALU.add).then_inc(c_.evacuated, 1)
            continue
        if m == 0:
            stores = [i for i in range(n) if PROJ[i] not in RESIDUAL]
            dve.wait_ge(c_.stored, 16 * (4 * len(stores) + grp) + 1)
        if name in GATED:
            before = 16 * sum(PROJ[i] in GATED for i in range(n))
            dve.wait_ge(c_.sig_ready, before + 4 * grp + m + 1)
            dve.tensor_tensor(c_.stage[:, m], ps, c_.sig[:, m], ALU.mult).then_inc(c_.evacuated, 1)
        else:
            dve.tensor_copy(c_.stage[:, m], ps).then_inc(c_.evacuated, 1)


def act_x_quarter(c_, act, j, q):
    act.wait_ge(c_.xtmp_ready, 4 * (j + 1))
    act.activation(c_.xhi[:, 4 * q:4 * q + 4], c_.xtmp[:, j % 2], ACT.Copy).then_inc(c_.xhi_ready, 1)


def dve_x_tmp(c_, dve, j, q, source):
    if j >= 2:
        dve.wait_ge(c_.x_ready, j - 1)
    for i in range(4):
        source(dve, c_.xtmp[:, j % 2, i], 4 * q + i).then_inc(c_.xtmp_ready, 1)


def dve_x_low(c_, dve, j, q):
    dve.wait_ge(c_.xhi_ready, j + 1)
    dve.tensor_tensor(c_.xlo[:, 4 * q:4 * q + 4], c_.xtmp[:, j % 2], c_.xhi[:, 4 * q:4 * q + 4],
                      ALU.subtract).then_inc(c_.x_ready, 1)


def dve_x_quarter(c_, dve, j, q, source):
    dve_x_tmp(c_, dve, j, q, source)
    dve_x_low(c_, dve, j, q)


def act_projection(c_, act, n, prev, roll=None, rolled=None):
    g0 = 4 * n

    def group(g_all, ended, ended_g, before_1=None, after=None):
        for q in range(4):
            if q == 1 and before_1 is not None:
                before_1()
            act_split(c_, act, g_all, q)
            if q == 0:
                act_gate(c_, act, ended, ended_g)
            if after is not None and q >= 1:
                after(q - 1)

    def last_quarter():
        wait_chunk_used(c_, act, g0 - 1, 3)
        act_x_quarter(c_, act, rolled + 3, 3)

    group(g0, prev, g0 - 1, before_1=last_quarter if rolled is not None else None)
    with act.Fori(1, 3) as grp:
        group(grp + g0, n, grp + g0 - 1)

    def roll_quarter(q):
        wait_chunk_used(c_, act, g0 + 3, q)
        act_x_quarter(c_, act, roll + q, q)

    group(g0 + 3, n, g0 + 2, after=roll_quarter if roll is not None else None)


def dve_projection(c_, dve, n, prev, roll=None, rolled=None, source=None, source_now=None):
    g0 = 4 * n
    for q in range(4):
        dve_split(c_, dve, g0, q)
        if q == 0:
            dve_evacuate(c_, dve, prev, g0 - 1, 3)
            if rolled is not None:
                dve_x_quarter(c_, dve, rolled + 3, 3, source_now)
    with dve.Fori(1, 3) as grp:
        for q in range(4):
            dve_split(c_, dve, grp + g0, q)
            if q == 0:
                dve_evacuate(c_, dve, n, grp + g0 - 1, grp - 1)
    for q in range(4):
        dve_split(c_, dve, g0 + 3, q)
        if q == 0:
            dve_evacuate(c_, dve, n, g0 + 2, 2)
        if roll is not None and q >= 1:
            dve_x_quarter(c_, dve, roll + q - 1, q - 1, source)


def norm_squares_act(c_, act, j):
    for m in range(NM):
        if m >= 2:
            act.wait_ge(c_.sq_summed, NM * j + m - 1)
        act.activation(c_.xsq[:, m % 2], c_.resT[:, m], ACT.Square).then_inc(c_.sq_ready, 1)


def norm_sum_pe(c_, pe, j):
    for m in range(NM):
        pe.wait_ge(c_.sq_ready, NM * j + m + 1)
        pe.matmul(c_.psN[:, 0:TOK], c_.ones[:], c_.xsq[:, m % 2], start=(m == 0),
                  stop=(m == NM - 1)).then_inc(c_.sq_summed, 1)


def norm_rsqrt_act(c_, act, j):
    act.wait_ge(c_.sq_summed, NM * (j + 1))
    act.activation(c_.rs[:], c_.psN[:, 0:TOK], ACT.Ln, bias=c_.consts[:, 0:1],
                   scale=1.0 / D).then_inc(c_.ln_ready, 1)
    act.wait_ge(c_.ln_ready, j + 1)
    act.activation(c_.rs[:], c_.rs[:], ACT.Exp, scale=-0.5).then_inc(c_.rs_ready, 1)


def normed(c_, gain):
    def source(dve, out, m):
        v = VEC[gain] * NM + m
        return dve.scalar_tensor_tensor(out=out, in0=c_.resT[:, m], scalar=c_.vec[:, v:v + 1],
                                        in1=c_.rs[:], op0=ALU.mult, op1=ALU.mult)
    return source


def mixed(c_, p):
    def source(dve, out, m):
        v = VEC[f"mu{p}"] * NM + m
        return dve.scalar_tensor_tensor(out=out, in0=c_.delta[:, m], scalar=c_.vec[:, v:v + 1],
                                        in1=c_.hT[:, m], op0=ALU.mult, op1=ALU.add)
    return source


def opening(nc, c_, a):
    with ExitStack() as ctx:
        def sb(name, shape, dt=F32):
            return ctx.enter_context(nc.sbuf_tensor(name, shape, dt))

        def sem(name):
            return ctx.enter_context(nc.semaphore(name))

        xnat = sb("xnat", [P, 3, D])
        shnat = sb("shnat", [NB, D])
        vnat = sb("vnat", [P, 3, P])
        shT = sb("shT", [P, NM, NB])
        lastT = sb("lastT", [P, NB + 1, NM])
        lastN = sb("lastN", [P, 2, P])
        w1 = sb("w1s", [P, 2, NM, LORA])
        w2 = sb("w2s", [LORA, 2, D])
        low = sb("low", [LORA, 2, TOK])
        psT = ctx.enter_context(nc.psum_tensor("psT", [P, 4, 512], F32))
        psN = c_.psN = ctx.enter_context(nc.psum_tensor(c_.name("psN"), [P, 512], F32))
        psL = ctx.enter_context(nc.psum_tensor("psL", [P, 2, 512], F32))
        psV = ctx.enter_context(nc.psum_tensor("psV", [P, 512], F32))
        x_in, v_in, sh_in, lora_in = sem("x_in"), sem("v_in"), sem("sh_in"), sem("lora_in")
        ident_made, const_made = sem("ident_made"), sem("const_made")
        vec_turned, x_turned, sh_turned = sem("vec_turned"), sem("x_turned"), sem("sh_turned")
        x_out, vec_ready, sh_ready = sem("x_out"), sem("vec_ready"), sem("sh_ready")
        h_ready, delta_ready = sem("h_ready"), sem("delta_ready")
        low_ready, up_summed, up_out = sem("low_ready"), sem("up_summed"), sem("up_out")
        last_ready, last_turned, last_out, last_stored = (sem("last_ready"), sem("last_turned"),
                                                          sem("last_out"), sem("last_stored"))
        mix_ready, mix_used, up_stored = sem("mix_ready"), sem("mix_used"), sem("up_stored")
        block = ctx.enter_context(nc.Block())

        @block.sync
        def _(sp):
            for n, name in enumerate(VECS):
                src = a[name].rearrange("(m p) -> m p", p=P)
                sp.dma_start(vnat[16 * (n % 8):16 * (n % 8) + 16, n // 8], src).then_inc(v_in, 16)
            for t in range(2):
                sp.dma_start(xnat[:, t], a["x_prompt"][0, t * P:(t + 1) * P]).then_inc(x_in, 16)
            sp.dma_start(xnat[0:64, 2], a["x_sample"].rearrange("b t d -> (b t) d")).then_inc(x_in, 16)
            sp.dma_start(shnat[:], a["state_shift"][0]).then_inc(sh_in, 16)
            for j, (d1, d2) in enumerate((("a_w1", "a_w2"), ("a_a1", "a_a2"))):
                sp.dma_start(w1[:, j], a[d1][0].rearrange("(m p) n -> p m n", p=P)).then_inc(lora_in, 16)
                sp.dma_start(w2[:, j], a[d2][0]).then_inc(lora_in, 16)
            load_group(c_, sp, 0, 0, None)
            sp.wait_ge(last_out, 2)
            sp.dma_start(a["o_shift_s"][0].rearrange("b (m p) -> (b m) p", p=P),
                         lastN[:, 0]).then_inc(last_stored, 16)
            sp.dma_start(a["o_shift_p"][0, 0].rearrange("(m p) -> m p", p=P),
                         lastN[0:NM, 1]).then_inc(last_stored, 16)
            for j, name in enumerate(("s", "a")):
                for g in range(4):
                    sp.wait_ge(up_out, 16 * j + 4 * g + 4)
                    sp.dma_start(c_.spill[SP_I[name]].rearrange("m p t -> p m t")[:, 4 * g:4 * g + 4],
                                 c_.stage[:]).then_inc(up_stored, 16)
            sp.wait_ge(up_stored, 16 * 8)
            sp.wait_ge(last_stored, 32)

        @block.gpsimd
        def _(pool):
            pool.memset(c_.ident[:], 0.0).then_inc(ident_made, 1)
            pool.wait_ge(ident_made, 1)
            pool.affine_select(out=c_.ident[:], in_=c_.ident[:], compare_op=ALU.not_equal, fill=1.0,
                               base=0, pattern=[[-1, P]], channel_multiplier=1).then_inc(ident_made, 1)

        @block.vector
        def _(dve):
            dve.memset(c_.ones[:], 1.0).then_inc(const_made, 1)
            dve.memset(c_.consts[:, 0:1], RMS_EPS).then_inc(const_made, 1)
            dve.memset(c_.consts[:, 1:2], LNX_EPS).then_inc(const_made, 1)
            dve.memset(c_.consts[:, 2:3], 10.0 * math.log(2.0)).then_inc(const_made, 1)
            dve.wait_ge(vec_turned, 3)
            dve.tensor_copy(c_.vec[:, 0:NM * len(VECS)], psV[:, 0:NM * len(VECS)]).then_inc(vec_ready, 1)
            dve.wait_ge(sh_turned, 1)
            dve.tensor_copy(shT[:], psV[:, 384:512].rearrange("p (m b) -> p m b", m=NM)).then_inc(sh_ready, 1)
            dve.wait_ge(vec_ready, 1)
            dve.wait_ge(c_.rs_ready, 1)
            src = normed(c_, "a_norm")
            for m in range(NM):
                src(dve, c_.hT[:, m], m).then_inc(h_ready, 1)
            dve.wait_ge(h_ready, NM)
            dve.wait_ge(sh_ready, 1)
            h, dl = c_.hT, c_.delta
            dve.tensor_tensor(dl[:, :, 1:SEQ], h[:, :, 0:SEQ - 1], h[:, :, 1:SEQ],
                              ALU.subtract).then_inc(delta_ready, 1)
            dve.tensor_scalar(dl[:, :, 0:1], h[:, :, 0:1], -1.0, None, ALU.mult).then_inc(delta_ready, 1)
            for b in range(NB):
                t0 = SEQ + b * TS
                dve.tensor_tensor(dl[:, :, t0 + 1:t0 + TS], h[:, :, t0:t0 + TS - 1],
                                  h[:, :, t0 + 1:t0 + TS], ALU.subtract).then_inc(delta_ready, 1)
                dve.tensor_tensor(dl[:, :, t0:t0 + 1], shT[:, :, b:b + 1], h[:, :, t0:t0 + 1],
                                  ALU.subtract).then_inc(delta_ready, 1)
                dve.tensor_copy(lastT[:, b], h[:, :, t0 + TS - 1]).then_inc(last_ready, 1)
            dve.tensor_copy(lastT[:, NB], h[:, :, SEQ - 1]).then_inc(last_ready, 1)
            dve.wait_ge(last_turned, 1)
            dve.tensor_copy(lastN[:, 0], psN[:, 384:512]).then_inc(last_out, 1)
            dve.wait_ge(last_turned, 2)
            dve.tensor_copy(lastN[0:NM, 1], psN[0:NM, 384:512]).then_inc(last_out, 1)
            dve.wait_ge(delta_ready, 2 + 2 * NB)
            for j in range(2):
                source = mixed(c_, 4 + j)
                for m in range(NM):
                    k = NM * j + m
                    if k >= 8:
                        dve.wait_ge(mix_used, k - 7)
                    source(dve, c_.xtmp[:, (k // 4) % 2, k % 4], m).then_inc(mix_ready, 1)

        @block.scalar
        def _(act):
            act.preload_act_table_set("natural_log_exp_and_others")
            for m in range(NM):
                act.wait_ge(x_turned, m + 1)
                act.activation(c_.resT[:, m], psT[:, m % 4, 0:TOK], ACT.Copy).then_inc(x_out, 1)
            act.wait_ge(x_out, NM)
            norm_squares_act(c_, act, 0)
            act.wait_ge(const_made, 4)
            norm_rsqrt_act(c_, act, 0)
            act.preload_act_table(ACT.Sigmoid)
            for j in range(2):
                act.wait_ge(mix_used, NM * (j + 1))
                act.activation(low[:, j], psL[0:LORA, j, 0:TOK],
                               ACT.Tanh if j == 0 else ACT.Copy).then_inc(low_ready, 1)
            act.wait_ge(vec_ready, 1)
            for j in range(2):
                for m in range(NM):
                    k = NM * j + m
                    act.wait_ge(up_summed, k + 1)
                    if k >= 4 and k % 4 == 0:
                        act.wait_ge(up_stored, 16 * (k // 4))
                    v = VEC[("w0", "a0")[j]] * NM + m
                    act.activation(c_.stage[:, m % 4], psT[:, m % 4, 0:TOK], ACT.Sigmoid,
                                   bias=c_.vec[:, v:v + 1]).then_inc(up_out, 1)

        @block.tensor
        def _(pe):
            pe.wait_ge(ident_made, 2)
            pe.wait_ge(v_in, 16 * len(VECS))
            pe.wait_ge(const_made, 4)
            for t in range(3):
                w = min(P, NM * len(VECS) - P * t)
                pe.transpose(psV[:, P * t:P * t + w], vnat[0:w, t], c_.ident[0:w, 0:w]).then_inc(vec_turned, 1)
            pe.wait_ge(sh_in, 16)
            pe.wait_ge(vec_ready, 1)
            for m in range(NM):
                last = pe.transpose(psV[:, 384 + NB * m:384 + NB * m + NB], shnat[:, m * P:(m + 1) * P],
                                    c_.ident[0:NB, 0:NB])
            last.then_inc(sh_turned, 1)
            pe.wait_ge(x_in, 48)
            for m in range(NM):
                if m >= 4:
                    pe.wait_ge(x_out, m - 3)
                for t in range(3):
                    w = (P, P, NB * TS)[t]
                    last = pe.transpose(psT[:, m % 4, t * P:t * P + w], xnat[0:w, t, m * P:(m + 1) * P],
                                        c_.ident[0:w, 0:w])
                last.then_inc(x_turned, 1)
            norm_sum_pe(c_, pe, 0)
            pe.wait_ge(last_ready, NB + 1)
            pe.wait_ge(c_.rs_ready, 1)
            pe.transpose(psN[:, 384:512], lastT[:, 0:NB].rearrange("p b m -> p (b m)"),
                         c_.ident[:]).then_inc(last_turned, 1)
            pe.wait_ge(last_out, 1)
            pe.transpose(psN[0:NM, 384:512], lastT[:, NB], c_.ident[:]).then_inc(last_turned, 1)
            pe.wait_ge(lora_in, 64)
            for j in range(2):
                for m in range(NM):
                    pe.wait_ge(mix_ready, NM * j + m + 1)
                    k = NM * j + m
                    last = pe.matmul(psL[0:LORA, j, 0:TOK], w1[:, j, m], c_.xtmp[:, (k // 4) % 2, k % 4],
                                     start=(m == 0), stop=(m == NM - 1))
                    last.then_inc(mix_used, 1)
            for j in range(2):
                pe.wait_ge(low_ready, j + 1)
                for m in range(NM):
                    k = NM * j + m
                    if k >= 4:
                        pe.wait_ge(up_out, k - 3)
                    pe.matmul(psT[:, m % 4, 0:TOK], w2[:, j, m * P:(m + 1) * P], low[:, j],
                              start=True, stop=True).then_inc(up_summed, 1)


def split_buffers(nc, ctx, c_):
    c_.whi = ctx.enter_context(nc.sbuf_tensor(c_.name("whi"), [P, 2, QC, GW], F32R))
    c_.wlo = ctx.enter_context(nc.sbuf_tensor(c_.name("wlo"), [P, 2, QC, GW], F32R))
    c_.psP = ctx.enter_context(nc.psum_tensor(c_.name("psP"), [P, 4, 512], F32))


def mixing_projections(nc, c_, a):
    with ExitStack() as ctx:
        split_buffers(nc, ctx, c_)
        block = ctx.enter_context(nc.Block())

        @block.sync
        def _(sp):
            for n in range(4):
                sp_projection(c_, sp, n, n + 1 if n < 3 else None, first_store=(n == 0))
            store_group(c_, sp, 3, 3, 15, None)
            sp.wait_ge(c_.stored, 16 * 16 + 1)

        @block.tensor
        def _(pe):
            for n in range(4):
                pe_projection(c_, pe, n, 4 * n)

        @block.scalar
        def _(act):
            for q in range(4):
                act_x_quarter(c_, act, q, q)
            for n in range(4):
                act_projection(c_, act, n, n - 1 if n else None, roll=4 * n + 4 if n < 3 else None,
                               rolled=4 * n if n else None)
            act_gate(c_, act, 3, 15)

        @block.vector
        def _(dve):
            dve.sem_inc(c_.evacuated, LEAD)
            dve.sem_inc(c_.stored, 1)
            for q in range(4):
                dve_x_quarter(c_, dve, q, q, mixed(c_, 0))
            for n in range(4):
                dve_projection(c_, dve, n, n - 1 if n else None, roll=4 * n + 4 if n < 3 else None,
                               rolled=4 * n if n else None, source=mixed(c_, n + 1) if n < 3 else None,
                               source_now=mixed(c_, n))
            dve_evacuate(c_, dve, 3, 15, 3)


class Marks:

    def __init__(self, sem, names):
        self.sem, self.names, self.n, self.seen = sem, {x: i for i, x in enumerate(names)}, len(names), 0

    def wait(self, eng, name, it):
        eng.wait_ge(self.sem, it * self.n + (self.names[name] + 1))

    def done(self, ins, name):
        assert self.names[name] == self.seen % self.n, name
        self.seen += 1
        ins.then_inc(self.sem, 1)


HS = 64
CH = NCH + 1
LANES = 2
ITS = NM // LANES

PREPARE = """
v.cs v.kk0 a.Pc g.csm a.sq t.ss a.Pi a.Pm v.ssm a.ln a.rn g.Rz v.ka1 v.k2 v.rk v.Kz v.kk v.Az v.ka
v.Bz t.abT v.D v.F t.ab v.Dt t.akT v.AK g.ID g.IDt g.BpP g.BpS t.Vn a.Vn t.D2 a.D2 t.D2t a.D2t g.W1
g.W1t t.D3 v.W t.D3t v.Wt t.D4 a.D4 t.D4t a.D4t g.KpP g.KpS t.Y v.Y t.Yt v.Yt t.rbT v.RB t.E a.E
t.Et a.Et t.rkT v.RK g.AzM g.dP t.E2 a.E2 t.E2t a.E2t t.Z1 v.Z1 t.Bn a.Bn t.E4t a.E4t t.Z2 v.Z2
t.Kn a.Kn t.bon t.S0T a.S0T t.X v.X""".split()
RUN = """
t.U0 v.U0 t.U4 v.U4 t.SA0 v.SA0 t.SA4 v.SA4 g.Bx g.Kx t.S0 v.ST0 t.O0 a.O0 v.SP1 t.U1 v.U1 t.O4
a.O4 t.SA1 v.SA1 t.S1 v.ST1 t.O1 a.O1 v.SP2 t.SN a.SN t.U2 v.U2 t.SA2 v.SA2 t.S2 v.ST2 t.O2 a.O2
v.SP3 v.bonus t.U3 v.U3 t.SA3 v.SA3 t.S3 v.ST3 t.O3 a.O3 t.SF a.SF t.mean v.cen a.csq t.var a.lnv
a.rstd v.on v.ong v.oy v.y a.xh v.xl""".split()


def steps_of(engine):
    return [x[2:] for x in PREPARE + RUN if x[0] == engine]


def places(order):
    cost = [2 if x[0] == "t" else 1 for x in order]
    return {x: sum(cost[:k]) / sum(cost) for k, x in enumerate(order)}


AT = places(PREPARE) | places(RUN)


def side_by_side(*streams):
    ahead = [[next(x, None), x] for x in streams]
    while any(place is not None for place, _ in ahead):
        pick = min((x for x in ahead if x[0] is not None), key=lambda x: x[0])
        pick[0] = next(pick[1], None)


TAKEN = {"ss": ("v", "ssm"), "bon": ("v", "bonus"), "abT": ("v", "F"), "ab": ("v", "Dt"),
         "Vn": ("a", "Vn"), "Bn": ("a", "Bn"), "Kn": ("a", "Kn"), "D2": ("a", "D2"),
         "D2t": ("a", "D2t"), "akT": ("v", "AK"), "D3": ("v", "W"), "D3t": ("v", "Wt"),
         "D4": ("a", "D4"), "D4t": ("a", "D4t"), "rbT": ("v", "RB"), "rkT": ("v", "RK"),
         "Y": ("v", "Y"), "Yt": ("v", "Yt"), "E": ("a", "E"), "Et": ("a", "Et"),
         "S0T": ("a", "S0T"), "E2": ("a", "E2"), "E2t": ("a", "E2t"), "E4t": ("a", "E4t"),
         "Z1": ("v", "Z1"), "Z2": ("v", "Z2"), "X": ("v", "X"), "SN": ("a", "SN"),
         "SF": ("a", "SF"), "mean": ("v", "cen"), "var": ("a", "lnv")}
for _c in range(CH):
    TAKEN |= {f"U{_c}": ("v", f"U{_c}"), f"SA{_c}": ("v", f"SA{_c}"), f"O{_c}": ("a", f"O{_c}"),
              f"S{_c}": ("v", f"ST{_c}")}
TURNS = [x for x in steps_of("t") if x != "bon"]
SETS = 3


class Lane:

    def __init__(self, nc, ctx, k):
        self.k = k

        def sb(name, shape):
            return ctx.enter_context(nc.sbuf_tensor(f"rw{k}_{name}", shape, F32))

        def sem(name):
            return ctx.enter_context(nc.semaphore(f"rw{k}_{name}"))

        self.ins = {x: sb("in_" + x, [P, TOK]) for x in ("r", "k", "v", "s", "a", "g")}
        T = self.T = {x: sb(x, [P, TOK]) for x in
                      ("cs", "csm", "Pc", "Pi", "Pm", "kk0", "sq", "rn", "kk", "Az", "Bz", "Kz", "Rz",
                       "k2", "rk", "Bp", "Kp", "D", "F", "Dt", "AK", "RB", "RK", "Vn", "Bn", "Kn",
                       "D2", "D2t", "D4", "D4t", "W1", "W1t", "Y", "Yt", "Et")}
        T["E2"], T["E2t"], T["E4t"], T["Z1"], T["Z2"] = T["D2"], T["D2t"], T["D4"], T["W1"], T["W1t"]
        T["X"], T["OT"], T["E"] = T["W1"], T["Pm"], T["csm"]
        T["W"], T["Wt"] = T["W1"], T["W1t"]
        self.S0n, self.S0T, self.AzM, self.dP, self.Bx, self.Kx = (
            sb(x, [P, NB, HS]) for x in ("S0n", "S0T", "AzM", "dP", "Bx", "Kx"))
        self.SN = self.AzM
        self.ST, self.SA = [sb(f"ST{j}", [P, HS]) for j in range(2)], [sb(f"SA{j}", [P, HS]) for j in range(2)]
        self.SPr, self.U, self.SF, self.U4, self.SA4 = (sb(x, [P, HS]) for x in ("SPr", "U", "SF", "U4", "SA4"))
        self.ps = [ctx.enter_context(nc.psum_tensor(f"rw{k}_ps{j}", [P, 512], F32)) for j in range(SETS)]
        self.psB = ctx.enter_context(nc.psum_tensor(f"rw{k}_psB", [P, 512], F32))
        self.s_in = {x: sem("in_" + x) for x in self.ins}
        self.s0_in, self.wkv_stored, self.wkvp_stored = sem("s0_in"), sem("wkv_stored"), sem("wkvp_stored")
        self.t, self.v, self.a, self.g = (Marks(sem(x), steps_of(x)) for x in "tvag")
        self.who = {"v": self.v, "a": self.a}

    def bank(self, name):
        return self.psB if name == "bon" else self.ps[TURNS.index(name) % SETS]

    def tile(self, i):
        return LANES * i + self.k


def two_lanes(eng, lanes, prepare, run):
    one, two = lanes
    side_by_side(prepare(one, 0))
    with eng.Fori(0, ITS - 1) as i:
        side_by_side(run(one, i), prepare(two, i))
        side_by_side(run(two, i), prepare(one, i + 1))
    side_by_side(run(one, ITS - 1), prepare(two, ITS - 1))
    side_by_side(run(two, ITS - 1))


def recurrence(nc, c_, a):
    with ExitStack() as ctx:
        def sb(name, shape, dt=F32):
            return ctx.enter_context(nc.sbuf_tensor("rw_" + name, shape, dt))

        def sem(name):
            return ctx.enter_context(nc.semaphore("rw_" + name))

        lanes = [Lane(nc, ctx, k) for k in range(LANES)]
        blk, blkm = sb("blk", [P, P]), sb("blkm", [P, P])
        I2 = sb("I2", [P, HS])
        mS, mI, mD, mDt, mF = (sb(x, [P, TOK]) for x in ("mS", "mI", "mD", "mDt", "mF"))
        keep = sb("keep", [P, TOK])
        mB = sb("mB", [P, NB, HS])
        mJ = sb("mJ", [P, NB])
        masks = sem("masks")
        passed = {x: sem("passed_" + x) for x in ("pe", "sp")}

        def pass_point(eng, x):
            eng.sem_inc(passed[x], 1)

        def scalar(name, tile):
            return c_.vec[:, bass.ds(VEC[name] * NM + tile, 1)]

        def prompt_chunks(x):
            return x[:, 0:SEQ].rearrange("p (c l) -> p c l", l=L)

        def sample_blocks(x):
            return x[:, SEQ:TOK].rearrange("p (b l) -> p b l", l=TS)

        def wide(x):
            return x[:].rearrange("p b k -> p (b k)")

        block = ctx.enter_context(nc.Block())

        @block.sync
        def _(sp):
            def load(l, i, x):
                sp.dma_start(l.ins[x][:], c_.spill[SP_I[x]].rearrange("m p t -> p m t")
                             [:, bass.ds(l.tile(i), 1), :].rearrange("p m t -> p (m t)")).then_inc(l.s_in[x], 16)

            def load_early(l, i, prior):
                for x, eng, last in (("s", l.g, "csm"), ("k", l.v, "k2"), ("a", l.v, "ka"), ("r", l.v, "rk")):
                    if prior is not None:
                        eng.wait(sp, last, prior)
                        pass_point(sp, "sp")
                        if x == "r":
                            l.g.wait(sp, "Rz", prior)
                            pass_point(sp, "sp")
                    load(l, i, x)
                if prior is not None:
                    l.t.wait(sp, "S0T", prior)
                    pass_point(sp, "sp")
                src = a["state_wkv"][0].rearrange("b (m h) v k -> m (h v) b k", h=2)
                sp.dma_start(l.S0n[:], src[bass.ds(l.tile(i), 1), :, :, :]
                             .rearrange("m p b k -> (m p) b k")).then_inc(l.s0_in, 16)

            def load_late(l, i, prior):
                if prior is not None:
                    l.v.wait(sp, "y", prior)
                    pass_point(sp, "sp")
                for x in ("v", "g"):
                    load(l, i, x)

            def store(l, i):
                l.a.wait(sp, "SF", i)
                pass_point(sp, "sp")
                dst_s = a["o_wkv_s"][0].rearrange("b (m h) v k -> m (h v) b k", h=2)
                dst_p = a["o_wkv_p"][0, 0].rearrange("(m h) v k -> m (h v) k", h=2)
                sp.dma_start(dst_s[bass.ds(l.tile(i), 1), :, :, :].rearrange("m p b k -> (m p) b k"),
                             l.SN[:]).then_inc(l.wkv_stored, 16)
                sp.dma_start(dst_p[bass.ds(l.tile(i), 1), :, :].rearrange("m p k -> (m p) k"),
                             l.SF[:]).then_inc(l.wkvp_stored, 16)

            for l in lanes:
                load_early(l, 0, None)
                load_late(l, 0, None)
            with sp.Fori(0, ITS - 1) as i:
                for l in lanes:
                    load_early(l, i + 1, i)
                    store(l, i)
                    load_late(l, i + 1, i)
            for l in lanes:
                store(l, ITS - 1)
            for l in lanes:
                sp.wait_ge(l.wkv_stored, 16 * ITS)
                sp.wait_ge(l.wkvp_stored, 16 * ITS)

        @block.gpsimd
        def _(pool):
            n = [0]

            def made(ins_):
                n[0] += 1
                ins_.then_inc(masks, 1)
                pool.wait_ge(masks, n[0])

            def tri(m, c0, cols, op, sign):
                for h in range(2):
                    view = m[64 * h:64 * h + 64, c0:c0 + cols]
                    made(pool.affine_select(out=view, in_=view, compare_op=op, fill=0.0, base=0,
                                            pattern=[[sign, cols]], channel_multiplier=-sign))

            def blocks(m, c0, cols):
                for h in range(2):
                    view = m[64 * h:64 * h + 64, c0:c0 + cols].rearrange("p (b u) -> p b u", u=TS)
                    made(pool.affine_select(out=view, in_=view, compare_op=ALU.is_ge, fill=0.0, base=0,
                                            pattern=[[-TS, cols // TS], [0, TS]], channel_multiplier=1))
                    made(pool.affine_select(out=view, in_=view, compare_op=ALU.is_ge, fill=0.0,
                                            base=TS - 1, pattern=[[TS, cols // TS], [0, TS]],
                                            channel_multiplier=-1))

            made(pool.memset(blk[:], 0.0))
            made(pool.memset(blkm[:], 0.0))
            for h in range(2):
                made(pool.memset(blk[64 * h:64 * h + 64, 64 * h:64 * h + 64], 1.0))
                made(pool.memset(blkm[64 * h:64 * h + 64, 64 * h:64 * h + 64], 1.0 / HS))
                made(pool.tensor_copy(I2[64 * h:64 * h + 64, :],
                                      c_.ident[64 * h:64 * h + 64, 64 * h:64 * h + 64]))
            for m in (mS, mI, mD, mDt):
                made(pool.memset(m[:], 1.0))
            for c in range(CH):
                tri(mS, c * L, L, ALU.is_gt, 1)
                tri(mD, c * L, L, ALU.is_gt, 1)
                tri(mI, c * L, L, ALU.is_ge, 1)
                tri(mDt, c * L, L, ALU.is_gt, -1)
                blocks(mD, c * L, L)
                blocks(mDt, c * L, L)
            blocks(mS, SEQ, L)
            blocks(mI, SEQ, L)
            made(pool.tensor_tensor(mF[:], mS[:], mD[:], ALU.subtract))
            made(pool.memset(keep[:], 1.0))
            made(pool.memset(keep[:, 0:SEQ].rearrange("p (c l) -> p c l", l=L)[:, :, 0:1], 0.0))
            made(pool.memset(keep[:, SEQ:TOK].rearrange("p (c l) -> p c l", l=TS)[:, :, 0:1], 0.0))
            made(pool.memset(mB[:], 0.0))
            for b in range(NB):
                made(pool.memset(mB[:, b, TS * b:TS * b + TS], 1.0))
            made(pool.memset(mJ[:], 1.0))
            for h in range(2):
                view = mJ[64 * h:64 * h + 64, :]
                made(pool.affine_select(out=view, in_=view, compare_op=ALU.is_ge, fill=0.0, base=0,
                                        pattern=[[-TS, NB]], channel_multiplier=1))
                made(pool.affine_select(out=view, in_=view, compare_op=ALU.is_ge, fill=0.0,
                                        base=TS - 1, pattern=[[TS, NB]], channel_multiplier=-1))
            c_.n_masks = n[0]

            def prepare(l, i):
                T, v, s, g = l.T, l.v, l.a, l.g

                def tt(name, out, x, y, op):
                    g.done(pool.tensor_tensor(out, x, y, op), name)

                yield AT["g.csm"]
                v.wait(pool, "cs", i)
                tt("csm", T["csm"][:], T["cs"][:], l.ins["s"][:], ALU.subtract)
                yield AT["g.Rz"]
                s.wait(pool, "Pc", i)
                pool.wait_ge(l.s_in["r"], 16 * i + 16)
                tt("Rz", T["Rz"][:], l.ins["r"][:], T["Pc"][:], ALU.mult)
                for x, d in (("", "D"), ("t", "Dt")):
                    yield AT["g.ID" + x]
                    v.wait(pool, d, i)
                    tt("ID" + x, T["W1" + x][:].rearrange("p (c l) -> p c l", l=L),
                       T[d][:].rearrange("p (c l) -> p c l", l=L),
                       I2[:].unsqueeze(1).to_broadcast([P, CH, HS]), ALU.add)

                def kept(x, z):
                    yield AT[f"g.{x}P"]
                    v.wait(pool, z, i)
                    tt(x + "P", prompt_chunks(T[x]), prompt_chunks(T[z]),
                       prompt_chunks(T["Pc"])[:, :, L - 1:L].to_broadcast([P, NCH, L]), ALU.mult)
                    yield AT[f"g.{x}S"]
                    tt(x + "S", sample_blocks(T[x]), sample_blocks(T[z]),
                       sample_blocks(T["Pc"])[:, :, TS - 1:TS].to_broadcast([P, NB, TS]), ALU.mult)

                yield from kept("Bp", "Bz")
                for x in ("", "t"):
                    yield AT["g.W1" + x]
                    s.wait(pool, "D2" + x, i)
                    g.wait(pool, "ID" + x, i)
                    tt("W1" + x, T["W1" + x][:], T["W1" + x][:], T["D2" + x][:], ALU.add)
                yield from kept("Kp", "Kz")
                yield AT["g.AzM"]
                if not isinstance(i, int) or i > 0:
                    pool.wait_ge(l.wkv_stored, 16 * i)
                tt("AzM", l.AzM[:], T["Az"][:, SEQ:TOK].unsqueeze(1).to_broadcast([P, NB, HS]), mB[:], ALU.mult)
                yield AT["g.dP"]
                tt("dP", l.dP[:], sample_blocks(T["Pc"])[:, :, TS - 1:TS].to_broadcast([P, NB, HS]),
                   I2[:].unsqueeze(1).to_broadcast([P, NB, HS]), ALU.mult)

            def run(l, i):
                mj = mJ[:].unsqueeze(2).to_broadcast([P, NB, HS])
                for name, out, src in (("Bx", l.Bx, "Bn"), ("Kx", l.Kx, "Kn")):
                    yield AT["g." + name]
                    l.a.wait(pool, src, i)
                    l.g.done(pool.tensor_tensor(out[:], l.T[src][:, SEQ:TOK].unsqueeze(1)
                                                .to_broadcast([P, NB, HS]), mj, ALU.mult), name)

            two_lanes(pool, lanes, prepare, run)

        @block.scalar
        def _(act):
            act.preload_act_table_set("natural_log_exp_and_others")
            act.wait_ge(masks, c_.n_masks)

            def af(l, name, out, in_, fn=ACT.Copy, **kw):
                l.a.done(act.activation(out, in_, fn, **kw), name)

            def take(l, name, i, n=CH):
                l.t.wait(act, name, i)
                af(l, name, l.T[name][:, 0:n * L], l.bank(name)[:, 0:n * L])

            def prepare(l, i):
                T, v, s, g, t = l.T, l.v, l.a, l.g, l.t
                yield AT["a.Pc"]
                v.wait(act, "cs", i)
                af(l, "Pc", T["Pc"][:], T["cs"][:], ACT.Exp, scale=-DECAY)
                yield AT["a.sq"]
                v.wait(act, "kk0", i)
                af(l, "sq", T["sq"][:], T["kk0"][:], ACT.Square)
                yield AT["a.Pi"]
                af(l, "Pi", T["Pi"][:], T["cs"][:], ACT.Exp, scale=DECAY)
                yield AT["a.Pm"]
                g.wait(act, "csm", i)
                af(l, "Pm", T["Pm"][:], T["csm"][:], ACT.Exp, scale=-DECAY)
                yield AT["a.ln"]
                v.wait(act, "ssm", i)
                af(l, "ln", T["rn"][:], T["rn"][:], ACT.Ln, scale=float(2 ** 20))
                yield AT["a.rn"]
                s.wait(act, "ln", i)
                af(l, "rn", T["rn"][:], T["rn"][:], ACT.Exp, scale=-0.5, bias=c_.consts[:, 2:3])
                for name in ("Vn", "D2", "D2t", "D4", "D4t"):
                    yield AT["a." + name]
                    take(l, name, i)
                for name in ("E", "Et", "E2", "E2t"):
                    yield AT["a." + name]
                    take(l, name, i, NCH)
                yield AT["a.Bn"]
                take(l, "Bn", i)
                yield AT["a.E4t"]
                take(l, "E4t", i, NCH)
                yield AT["a.Kn"]
                take(l, "Kn", i)
                yield AT["a.S0T"]
                t.wait(act, "S0T", i)
                af(l, "S0T", wide(l.S0T), l.bank("S0T")[:])

            def run(l, i):
                T, v, s, t = l.T, l.v, l.a, l.t
                for name in ("O0", "O4", "O1", "SN", "O2", "O3"):
                    yield AT["a." + name]
                    t.wait(act, name, i)
                    if name == "SN":
                        af(l, name, wide(l.SN), l.bank(name)[:])
                    else:
                        c = int(name[1])
                        af(l, name, T["OT"][:, c * L:(c + 1) * L], l.bank(name)[:, 0:L])
                yield AT["a.SF"]
                t.wait(act, "SF", i)
                if not isinstance(i, int) :
                    pass
                af(l, "SF", l.SF[:], l.bank("SF")[:, 0:HS])
                yield AT["a.csq"]
                v.wait(act, "cen", i)
                af(l, "csq", T["sq"][:], T["cs"][:], ACT.Square)
                yield AT["a.lnv"]
                t.wait(act, "var", i)
                af(l, "lnv", T["rn"][:], l.bank("var")[:, 0:TOK], ACT.Ln, bias=c_.consts[:, 1:2])
                yield AT["a.rstd"]
                s.wait(act, "lnv", i)
                af(l, "rstd", T["rn"][:], T["rn"][:], ACT.Exp, scale=-0.5)
                yield AT["a.xh"]
                v.wait(act, "y", i)
                af(l, "xh", c_.xhi[:, bass.ds(l.tile(i), 1), :].rearrange("p m t -> p (m t)"), T["kk"][:])

            two_lanes(act, lanes, prepare, run)

        @block.vector
        def _(dve):
            dve.wait_ge(masks, c_.n_masks)

            def tt(l, name, out, x, y, op=ALU.mult):
                l.v.done(dve.tensor_tensor(out, x, y, op), name)

            def stt(l, name, out, x, scalar_, y, op0, op1):
                l.v.done(dve.scalar_tensor_tensor(out=out, in0=x, scalar=scalar_, in1=y, op0=op0, op1=op1), name)

            def ts(l, name, out, x, s1, s2, op0, op1=None):
                if op1 is None:
                    l.v.done(dve.tensor_scalar(out, x, s1, None, op0), name)
                else:
                    l.v.done(dve.tensor_scalar(out, x, s1, s2, op0, op1), name)

            def prepare(l, i):
                T, v, s, g, t = l.T, l.v, l.a, l.g, l.t

                def masked(name, step, mask):
                    t.wait(dve, step, i)
                    tt(l, name, T[name][:], l.bank(step)[:, 0:TOK], mask[:])

                def plus(name, base, n=CH, step=None):
                    step = step or name
                    t.wait(dve, step, i)
                    tt(l, name, T[name][:, 0:n * L], l.bank(step)[:, 0:n * L], T[base][:, 0:n * L], ALU.add)

                yield AT["v.cs"]
                dve.wait_ge(l.s_in["s"], 16 * i + 16)
                v.done(dve.tensor_tensor_scan(out=T["cs"][:], data0=keep[:], data1=l.ins["s"][:],
                                              initial=0.0, op0=ALU.mult, op1=ALU.add), "cs")
                yield AT["v.kk0"]
                dve.wait_ge(l.s_in["k"], 16 * i + 16)
                ts(l, "kk0", T["kk0"][:], l.ins["k"][:], scalar("k_k", l.tile(i)), None, ALU.mult)
                yield AT["v.ssm"]
                t.wait(dve, "ss", i)
                ts(l, "ssm", T["rn"][:], l.bank("ss")[:, 0:TOK], 1e-24, None, ALU.max)
                yield AT["v.ka1"]
                dve.wait_ge(l.s_in["a"], 16 * i + 16)
                ts(l, "ka1", T["k2"][:], l.ins["a"][:], -1.0, scalar("k_a", l.tile(i)), ALU.add, ALU.mult)
                yield AT["v.k2"]
                v.wait(dve, "ka1", i)
                stt(l, "k2", T["k2"][:], T["k2"][:], 1.0, l.ins["k"][:], ALU.add, ALU.mult)
                yield AT["v.rk"]
                v.wait(dve, "k2", i)
                dve.wait_ge(l.s_in["r"], 16 * i + 16)
                stt(l, "rk", T["rk"][:], l.ins["r"][:], scalar("r_k", l.tile(i)), T["k2"][:], ALU.mult, ALU.mult)
                yield AT["v.Kz"]
                s.wait(dve, "Pi", i)
                tt(l, "Kz", T["Kz"][:], T["k2"][:], T["Pi"][:])
                yield AT["v.kk"]
                s.wait(dve, "rn", i)
                tt(l, "kk", T["kk"][:], T["kk0"][:], T["rn"][:])
                yield AT["v.Az"]
                v.wait(dve, "kk", i)
                stt(l, "Az", T["Az"][:], T["kk"][:], -1.0, T["Pm"][:], ALU.mult, ALU.mult)
                yield AT["v.ka"]
                tt(l, "ka", T["kk0"][:], T["kk"][:], l.ins["a"][:])
                yield AT["v.Bz"]
                v.wait(dve, "ka", i)
                tt(l, "Bz", T["Bz"][:], T["kk0"][:], T["Pi"][:])
                yield AT["v.D"]
                masked("D", "abT", mD)
                yield AT["v.F"]
                tt(l, "F", T["F"][:], l.bank("abT")[:, 0:TOK], mF[:])
                yield AT["v.Dt"]
                masked("Dt", "ab", mDt)
                yield AT["v.AK"]
                masked("AK", "akT", mS)
                yield AT["v.W"]
                g.wait(dve, "W1", i)
                plus("W", "W1", step="D3")
                yield AT["v.Wt"]
                g.wait(dve, "W1t", i)
                plus("Wt", "W1t", step="D3t")
                yield AT["v.Y"]
                plus("Y", "W")
                yield AT["v.Yt"]
                plus("Yt", "Wt")
                yield AT["v.RB"]
                masked("RB", "rbT", mI)
                yield AT["v.RK"]
                masked("RK", "rkT", mI)
                yield AT["v.Z1"]
                plus("Z1", "Y", NCH)
                yield AT["v.Z2"]
                v.wait(dve, "Z1", i)
                plus("Z2", "Z1", NCH)
                yield AT["v.X"]
                v.wait(dve, "Z2", i)
                plus("X", "Z2", NCH)

            def run(l, i):
                T, v, s, g, t = l.T, l.v, l.a, l.g, l.t
                small = {"U4": l.U4, "SA4": l.SA4, "ST0": l.ST[0]}
                for c in range(NCH):
                    small |= {f"U{c}": l.U, f"SA{c}": l.SA[c % 2]}
                order = [x[2:] for x in RUN if x[0] == "v"]
                for name in order[:order.index("cen")]:
                    yield AT["v." + name]
                    if name in small:
                        step = {"ST0": "S0"}.get(name, name)
                        t.wait(dve, step, i)
                        v.done(dve.tensor_copy(small[name][:], l.bank(step)[:, 0:HS]), name)
                    elif name == "bonus":
                        t.wait(dve, "bon", i)
                        dve.wait_ge(l.s_in["v"], 16 * i + 16)
                        tt(l, name, T["k2"][:], l.psB[:, 0:TOK], l.ins["v"][:])
                    elif name[:2] == "SP":
                        c = int(name[2])
                        v.wait(dve, f"ST{c - 1}", i)
                        ts(l, name, l.SPr[:], l.ST[(c - 1) % 2][:], T["Pc"][:, c * L + L - 1:c * L + L],
                           None, ALU.mult)
                    else:
                        c = int(name[2])
                        t.wait(dve, f"S{c}", i)
                        v.wait(dve, f"SP{c}", i)
                        tt(l, name, l.ST[c % 2][:], l.bank(f"S{c}")[:, 0:HS], l.SPr[:], ALU.add)
                yield AT["v.cen"]
                t.wait(dve, "mean", i)
                tt(l, "cen", T["cs"][:], T["OT"][:], l.bank("mean")[:, 0:TOK], ALU.subtract)
                yield AT["v.on"]
                s.wait(dve, "rstd", i)
                tt(l, "on", T["OT"][:], T["cs"][:], T["rn"][:])
                yield AT["v.ong"]
                v.wait(dve, "on", i)
                ts(l, "ong", T["OT"][:], T["OT"][:], scalar("lnx_g", l.tile(i)), scalar("lnx_b", l.tile(i)),
                   ALU.mult, ALU.add)
                yield AT["v.oy"]
                v.wait(dve, "ong", i)
                tt(l, "oy", T["OT"][:], T["OT"][:], T["k2"][:], ALU.add)
                yield AT["v.y"]
                v.wait(dve, "oy", i)
                dve.wait_ge(l.s_in["g"], 16 * i + 16)
                tt(l, "y", T["kk"][:], T["OT"][:], l.ins["g"][:])
                yield AT["v.xl"]
                s.wait(dve, "xh", i)
                m = bass.ds(l.tile(i), 1)
                tt(l, "xl", c_.xlo[:, m, :].rearrange("p m t -> p (m t)"), T["kk"][:],
                   c_.xhi[:, m, :].rearrange("p m t -> p (m t)"), ALU.subtract)

            two_lanes(dve, lanes, prepare, run)

        @block.tensor
        def _(pe):
            pe.wait_ge(masks, c_.n_masks)
            halves = [slice(64 * h, 64 * h + 64) for h in range(2)]

            def need(marks, name, i):
                marks.wait(pe, name, i)
                pass_point(pe, "pe")

            def begin(l, name, i):
                if name != "bon":
                    k = TURNS.index(name)
                    if k >= SETS:
                        eng, mark = TAKEN[TURNS[k - SETS]]
                        l.who[eng].wait(pe, mark, i)
                pass_point(pe, "pe")
                return l.bank(name)

            def products(l, name, lhs, rhs, i, n=CH):
                out = begin(l, name, i)
                for c in range(n):
                    for r in halves:
                        cc = slice(c * L, c * L + L)
                        last = pe.matmul(out[r, cc], lhs[r, cc], I2[r, :] if rhs is None else rhs[r, cc],
                                         start=True, stop=True)
                l.t.done(last, name)

            def heads(l, name, i, groups):
                out = begin(l, name, i)
                for j, (lhs, rhs, c0, w) in enumerate(groups):
                    for r in halves:
                        last = pe.matmul(out[r, c0:c0 + w], lhs[r], rhs[r], start=(j == 0),
                                         stop=(j == len(groups) - 1))
                l.t.done(last, name)

            def at(x, c):
                return x[:, c * L:(c + 1) * L]

            def over_channels(l, name, mat, x, i):
                out = begin(l, name, i)
                l.t.done(pe.matmul(out[:, 0:TOK], mat[:], x[:], start=True, stop=True), name)

            PRODUCTS = {"abT": ("Bz", "Az", ("v", "Bz")), "ab": ("Az", "Bz", None), "akT": ("Kz", "Az", None),
                        "D2": ("Dt", "D", ("v", "Dt")), "D2t": ("D", "Dt", None), "Bn": ("Bp", None, ("g", "BpS")),
                        "Kn": ("Kp", None, ("g", "KpS")), "D3": ("D2t", "D", ("a", "D2t")),
                        "D3t": ("D2", "Dt", None), "D4": ("D2t", "D2", None), "D4t": ("D2", "D2t", None),
                        "rbT": ("Bz", "Rz", ("g", "Rz")), "rkT": ("Kz", "Rz", ("v", "Kz")),
                        "Y": ("D4t", "W", ("v", "Wt")), "Yt": ("D4", "Wt", None)}
            PROMPT_PRODUCTS = {"E": ("Yt", "F", ("v", "Yt")), "Et": ("F", "Yt", None),
                               "Z1": ("Et", "Y", None), "E2": ("Et", "E", ("a", "Et")), "E2t": ("E", "Et", None),
                               "E4t": ("E2", "E2t", ("a", "E2t")), "Z2": ("E2t", "Z1", ("v", "Z1")),
                               "X": ("E4t", "Z2", ("v", "Z2"))}

            def prepare(l, i):
                T, marks = l.T, {"v": l.v, "a": l.a, "g": l.g}
                for name in [x[2:] for x in PREPARE if x[0] == "t"]:
                    yield AT["t." + name]
                    if name == "ss":
                        need(l.a, "sq", i)
                        over_channels(l, name, blk, T["sq"], i)
                    elif name == "bon":
                        need(l.v, "rk", i)
                        over_channels(l, name, blk, T["rk"], i)
                    elif name == "Vn":
                        pe.wait_ge(l.s_in["v"], 16 * i + 16)
                        pass_point(pe, "pe")
                        products(l, name, l.ins["v"], None, i)
                    elif name == "S0T":
                        pe.wait_ge(l.s0_in, 16 * i + 16)
                        pass_point(pe, "pe")
                        out = begin(l, name, i)
                        for b in range(NB):
                            for r in halves:
                                last = pe.matmul(out[r, b * HS:(b + 1) * HS], l.S0n[r, b], I2[r, :],
                                                 start=True, stop=True)
                        l.t.done(last, name)
                    else:
                        lhs, rhs, ready = (PRODUCTS | PROMPT_PRODUCTS)[name]
                        if ready is not None:
                            need(marks[ready[0]], ready[1], i)
                        if name == "Y":
                            need(l.a, "D4t", i)
                        if name == "X":
                            need(l.a, "E4t", i)
                        products(l, name, T[lhs], None if rhs is None else T[rhs], i,
                                 NCH if name in PROMPT_PRODUCTS else CH)

            def run(l, i):
                T, ST, SA = l.T, l.ST, l.SA
                for name in [x[2:] for x in RUN if x[0] == "t"]:
                    yield AT["t." + name]
                    if name == "U0":
                        need(l.a, "Kn", i)
                        need(l.v, "AK", i)
                    if name == "U4":
                        need(l.g, "AzM", i)
                        need(l.a, "S0T", i)
                        heads(l, name, i, [(at(T["AK"], 4), at(T["Vn"], 4), 0, HS)]
                              + [(l.AzM[:, b], l.S0T[:, b], 0, HS) for b in range(NB)])
                    elif name == "SA4":
                        need(l.v, "U4", i)
                        heads(l, name, i, [(at(T["Y"], 4), l.U4[:], 0, HS)])
                    elif name == "O4":
                        need(l.v, "SA4", i)
                        heads(l, name, i, [(l.SA4[:], at(T["RB"], 4), 0, L), (at(T["Vn"], 4), at(T["RK"], 4), 0, L)]
                              + [(l.S0T[:, b], T["Rz"][:, SEQ + TS * b:SEQ + TS * b + TS], TS * b, TS)
                                 for b in range(NB)])
                    elif name == "SN":
                        need(l.g, "Kx", i)
                        heads(l, name, i, [(l.SA4[:], wide(l.Bx), 0, NB * HS), (at(T["Vn"], 4), wide(l.Kx), 0, NB * HS)]
                              + [(l.S0T[:, b], l.dP[:, b], b * HS, HS) for b in range(NB)])
                    elif name == "SF":
                        need(l.v, "ST3", i)
                        heads(l, name, i, [(ST[1][:], I2[:], 0, HS)])
                    elif name == "mean":
                        need(l.a, "O3", i)
                        over_channels(l, name, blkm, T["OT"], i)
                    elif name == "var":
                        need(l.a, "csq", i)
                        over_channels(l, name, blkm, T["sq"], i)
                    else:
                        step, c = name[:-1], int(name[-1])
                        old, new = ST[(c - 1) % 2], SA[c % 2]
                        if step == "U":
                            if c > 0:
                                need(l.v, f"ST{c - 1}", i)
                            heads(l, name, i, ([(at(T["Az"], c), old[:], 0, HS)] if c else [])
                                  + [(at(T["AK"], c), at(T["Vn"], c), 0, HS)])
                        elif step == "SA":
                            need(l.v, f"U{c}", i)
                            heads(l, name, i, [(at(T["X"], c), l.U[:], 0, HS)])
                        elif step == "S":
                            need(l.v, f"SA{c}", i)
                            heads(l, name, i, [(at(T["Bn"], c), new[:], 0, HS),
                                               (at(T["Kn"], c), at(T["Vn"], c), 0, HS)])
                        else:
                            heads(l, name, i, ([(old[:], at(T["Rz"], c), 0, L)] if c else [])
                                  + [(new[:], at(T["RB"], c), 0, L), (at(T["Vn"], c), at(T["RK"], c), 0, L)])

            two_lanes(pe, lanes, prepare, run)


def middle(nc, c_, a):
    with ExitStack() as ctx:
        split_buffers(nc, ctx, c_)
        c_.psN = ctx.enter_context(nc.psum_tensor(c_.name("psN"), [P, 512], F32))
        res_stored = ctx.enter_context(nc.semaphore("res_stored"))
        wo, kk, kv, q, g2 = (PB[x] for x in ("wo", "kk", "kv", "q", "g2"))
        block = ctx.enter_context(nc.Block())

        @block.sync
        def _(sp):
            load_group(c_, sp, wo, 0, None)
            for n in (wo, kk, kv, q, g2):
                sp_projection(c_, sp, n, n + 1 if n < g2 else None, first_store=(n == wo))
                if n == kk:
                    sp.dma_start(c_.res_spill.rearrange("m p t -> p m t"), c_.resT[:]).then_inc(res_stored, 16)
            store_group(c_, sp, g2, 3, 4 * g2 + 3, None)
            sp.wait_ge(res_stored, 16)
            sp.wait_ge(c_.stored, 16 * 32 + 1)

        @block.tensor
        def _(pe):
            pe_projection(c_, pe, wo, 12)
            norm_sum_pe(c_, pe, 1)
            pe_projection(c_, pe, kk, 16)
            pe_projection(c_, pe, kv, 16)
            pe_projection(c_, pe, q, 20)
            pe_projection(c_, pe, g2, 20)

        @block.scalar
        def _(act):
            act_projection(c_, act, wo, None)
            act.wait_ge(c_.evacuated, 4 * (4 * wo + 4) + LEAD)
            norm_squares_act(c_, act, 1)
            norm_rsqrt_act(c_, act, 1)
            for x in range(4):
                act_x_quarter(c_, act, 16 + x, x)
            act.preload_act_table(ACT.Sigmoid)
            act_projection(c_, act, kk, None)
            act_projection(c_, act, kv, kk, roll=20)
            act_projection(c_, act, q, kv, rolled=20)
            act_projection(c_, act, g2, q)
            act_gate(c_, act, g2, 4 * g2 + 3)

        @block.vector
        def _(dve):
            dve_projection(c_, dve, wo, None)
            dve_evacuate(c_, dve, wo, 4 * wo + 3, 3)
            dve.wait_ge(c_.rs_ready, 2)
            for x in range(4):
                dve_x_quarter(c_, dve, 16 + x, x, normed(c_, "kv_norm"))
            dve_projection(c_, dve, kk, None)
            dve_projection(c_, dve, kv, kk, roll=20, source=normed(c_, "b_norm"))
            dve_projection(c_, dve, q, kv, rolled=20, source_now=normed(c_, "b_norm"))
            dve_projection(c_, dve, g2, q)
            dve_evacuate(c_, dve, g2, 4 * g2 + 3, 3)


MASKED = -1e30
HG = 4
ZW = P + SEQ

DVE_P = ["z", "sp", "rc", "arg", "y", "qs", "knl"]
ACT_P = ["abs", "exp", "ln", "kn", "vn", "att", "attT", "gs", "knh"]
PE_P = ["z", "kn", "vn", "attT", "o"]


def prompt_attention(nc, c_, a):
    with ExitStack() as ctx:
        def sb(name, shape, dt=F32):
            return ctx.enter_context(nc.sbuf_tensor("pa_" + name, shape, dt))

        def sem(name):
            return ctx.enter_context(nc.semaphore("pa_" + name))

        ins = {x: sb("in_" + x, [P, HG, TOK]) for x in ("q", "kk", "kv", "g2")}
        Q, K, V, G = (ins[x] for x in ("q", "kk", "kv", "g2"))
        kn, vn = sb("kn", [P, HG, 3, P]), sb("vn", [P, HG, 3, P])
        z, w, sp_, rc, att, attT = (sb(x, [P, HG, ZW]) for x in ("z", "w", "sp", "rc", "att", "attT"))
        mask, onesz = sb("mask", [P, ZW]), sb("onesz", [P, SEQ])
        zadd = sb("zadd", [P, HG, ZW])
        bcol, bdiag, brow = sb("bcol", [NHB, 1]), sb("bdiag", [NHB, NHB]), sb("brow", [P, NHB])
        spread = sb("spread", [NHB, P])
        psA = ctx.enter_context(nc.psum_tensor("pa_psA", [P, HG, 512], F32))
        psB = ctx.enter_context(nc.psum_tensor("pa_psB", [P, HG, 512], F32))
        s_in = {x: sem("in_" + x) for x in ins}
        b_in, made, bias_made, kv_stored, b_mm = (sem("b_in"), sem("made"), sem("bias_made"),
                                                  sem("kv_stored"), sem("b_mm"))
        v, t, s = (Marks(sem(x), y) for x, y in (("vector", DVE_P), ("tensor", PE_P), ("scalar", ACT_P)))
        passed, zadd_ready = sem("passed"), sem("zadd_ready")
        n_made = [0]

        block = ctx.enter_context(nc.Block())

        @block.sync
        def _(sp):
            sp.dma_start(bcol[:], a["b_logit_bias"][0].rearrange("(h o) -> h o", o=1)).then_inc(b_in, 16)

            def load(i, prior):
                for x, (m, last) in (("q", (v, "qs")), ("kk", (v, "knl")), ("kv", (t, "vn")), ("g2", (v, "y"))):
                    if prior is not None:
                        if x == "g2":
                            s.wait(sp, "gs", prior)
                            sp.sem_inc(passed, 1)
                        m.wait(sp, last, prior)
                        sp.sem_inc(passed, 1)
                    sp.dma_start(ins[x][:], c_.spill[SP_I[x]].rearrange("m p t -> p m t")
                                 [:, bass.ds(HG * i, HG), :]).then_inc(s_in[x], 16)

            def store(i):
                for x, buf, mark in (("k", kn, "kn"), ("v", vn, "vn")):
                    s.wait(sp, mark, i)
                    sp.sem_inc(passed, 1)
                    for tt in range(2):
                        dst = a[f"o_{x}_p"][0, tt * P:(tt + 1) * P]
                        sp.dma_start(dst[:, bass.ds(HG * i, HG), :], buf[:, :, tt]).then_inc(kv_stored, 16)
                    dst = a[f"o_{x}_s"].rearrange("b t h d -> (b t) h d")
                    sp.dma_start(dst[:, bass.ds(HG * i, HG), :], buf[0:NB * TS, :, 2]).then_inc(kv_stored, 16)

            sp.sem_inc(kv_stored, 1)
            load(0, None)
            with sp.Fori(0, NHB // HG - 1) as i:
                store(i)
                load(i + 1, i)
            store(NHB // HG - 1)
            sp.wait_ge(kv_stored, 16 * 6 * (NHB // HG) + 1)

        @block.gpsimd
        def _(pool):
            def step(ins_):
                n_made[0] += 1
                ins_.then_inc(made, 1)
                pool.wait_ge(made, n_made[0])

            step(pool.memset(mask[:], 0.0))
            step(pool.memset(onesz[:], 1.0))
            step(pool.memset(spread[:], 1.0))
            step(pool.affine_select(out=mask[:, 0:P], in_=mask[:, 0:P], compare_op=ALU.is_gt, fill=MASKED,
                                    base=0, pattern=[[-1, P]], channel_multiplier=1))
            step(pool.affine_select(out=mask[:, P:ZW], in_=mask[:, P:ZW], compare_op=ALU.is_gt, fill=MASKED,
                                    base=P, pattern=[[-1, SEQ]], channel_multiplier=1))
            step(pool.affine_select(out=spread[:], in_=spread[:], compare_op=ALU.is_ge, fill=0.0,
                                    base=0, pattern=[[1, P]], channel_multiplier=-TS))
            step(pool.affine_select(out=spread[:], in_=spread[:], compare_op=ALU.is_ge, fill=0.0,
                                    base=TS - 1, pattern=[[-1, P]], channel_multiplier=TS))

            pool.wait_ge(bias_made, 3)
            def add_mask(i):
                pool.tensor_tensor(zadd[:], mask[:].unsqueeze(1).to_broadcast([P, HG, ZW]),
                                   brow[:, bass.ds(HG * i, HG)].unsqueeze(2).to_broadcast([P, HG, ZW]),
                                   ALU.add).then_inc(zadd_ready, 1)

            add_mask(0)
            with pool.Fori(1, NHB // HG) as i:
                v.wait(pool, "z", i - 1)
                add_mask(i)

        @block.scalar
        def _(act):
            act.preload_act_table_set("natural_log_exp_and_others")
            with act.Fori(0, NHB // HG) as i:
                v.wait(act, "z", i)
                s.done(act.activation(w[:], z[:], ACT.Abs), "abs")
                s.wait(act, "abs", i)
                s.done(act.activation(w[:], w[:], ACT.Exp, scale=-1.0), "exp")
                s.wait(act, "exp", i)
                s.done(act.activation(w[:], w[:], ACT.Ln, bias=c_.ones[:, 0:1]), "ln")
                for x, buf in (("kn", kn), ("vn", vn)):
                    t.wait(act, x, i)
                    act.wait_ge(kv_stored, 16 * 6 * i + 1)
                    for tt in range(3):
                        n = P if tt < 2 else NB * TS
                        last = act.activation(buf[0:n, :, tt], psB[0:n, :, tt * P:(tt + 1) * P], ACT.Copy)
                    s.done(last, x)
                v.wait(act, "arg", i)
                s.done(act.activation(att[:], z[:], ACT.Exp), "att")
                t.wait(act, "attT", i)
                s.done(act.activation(attT[:], psA[:, :, 0:ZW], ACT.Copy), "attT")
                act.wait_ge(s_in["g2"], 16 * i + 16)
                s.done(act.activation(c_.gS[:, bass.ds(HG * i, HG), :], G[:, :, SEQ:TOK], ACT.Copy), "gs")
                act.wait_ge(s_in["kk"], 16 * i + 16)
                s.done(act.activation(c_.kNh[:, bass.ds(HG * i, HG), :], K[:, :, SEQ:TOK], ACT.Copy), "knh")

        @block.vector
        def _(dve):
            dve.wait_ge(b_in, 16)
            dve.tensor_scalar(bdiag[:], c_.ident[0:NHB, 0:NHB], bcol[:, 0:1], None, ALU.mult).then_inc(bias_made, 1)
            dve.wait_ge(b_mm, 1)
            dve.tensor_copy(brow[:], psA[:, 0, 0:NHB]).then_inc(bias_made, 1)
            dve.tensor_copy(c_.biasQ[:], psA[:, 0, NHB:NHB + 1]).then_inc(bias_made, 1)
            dve.wait_ge(made, n_made[0])
            with dve.Fori(0, NHB // HG) as i:
                t.wait(dve, "z", i)
                dve.wait_ge(zadd_ready, i + 1)
                v.done(dve.scalar_tensor_tensor(out=z[:], in0=psA[:, :, 0:ZW], scalar=SCALE, in1=zadd[:],
                                                op0=ALU.mult, op1=ALU.add), "z")
                s.wait(dve, "ln", i)
                v.done(dve.scalar_tensor_tensor(out=sp_[:], in0=z[:], scalar=0.0, in1=w[:], op0=ALU.max,
                                                op1=ALU.add), "sp")
                v.wait(dve, "sp", i)
                for h in range(HG):
                    dve.tensor_tensor_scan(out=rc[:, h, P - 1::-1], data0=onesz[:, 0:P],
                                           data1=sp_[:, h, P - 1::-1], initial=0.0, op0=ALU.mult, op1=ALU.add)
                    last = dve.tensor_tensor_scan(out=rc[:, h, ZW - 1:P - 1:-1], data0=onesz[:],
                                                  data1=sp_[:, h, ZW - 1:P - 1:-1], initial=0.0,
                                                  op0=ALU.mult, op1=ALU.add)
                v.done(last, "rc")
                v.wait(dve, "rc", i)
                v.done(dve.tensor_tensor(z[:], z[:], rc[:], ALU.subtract), "arg")
                t.wait(dve, "o", i)
                dve.wait_ge(s_in["g2"], 16 * i + 16)
                v.done(dve.tensor_tensor(c_.yT[:, bass.ds(HG * i, HG), 0:SEQ], psB[:, :, 0:SEQ],
                                         G[:, :, 0:SEQ], ALU.mult), "y")
                dve.wait_ge(s_in["q"], 16 * i + 16)
                v.done(dve.tensor_scalar(c_.qS[:, bass.ds(HG * i, HG), :], Q[:, :, SEQ:TOK], SCALE, None,
                                         ALU.mult), "qs")
                s.wait(dve, "knh", i)
                v.done(dve.tensor_tensor(c_.kNl[:, bass.ds(HG * i, HG), :], K[:, :, SEQ:TOK],
                                         c_.kNh[:, bass.ds(HG * i, HG), :], ALU.subtract), "knl")

        @block.tensor
        def _(pe):
            pe.wait_ge(made, n_made[0])
            pe.wait_ge(bias_made, 1)
            pe.matmul(psA[:, 0, 0:NHB], c_.ones[0:NHB, :], bdiag[:], start=True, stop=True)
            pe.matmul(psA[:, 0, NHB:NHB + 1], spread[:], bcol[:], start=True, stop=True).then_inc(b_mm, 1)
            pe.wait_ge(bias_made, 3)

            def rows(name, src, i):
                for h in range(HG):
                    for tt in range(3):
                        n = P if tt < 2 else NB * TS
                        last = pe.transpose(psB[0:n, h, tt * P:(tt + 1) * P], src[:, h, tt * P:tt * P + n],
                                            c_.ident[:])
                t.done(last, name)

            with pe.Fori(0, NHB // HG) as i:
                pe.wait_ge(s_in["q"], 16 * i + 16)
                pe.wait_ge(s_in["kk"], 16 * i + 16)
                for h in range(HG):
                    pe.matmul(psA[:, h, 0:P], Q[:, h, 0:P], K[:, h, 0:P], start=True, stop=True)
                    last = pe.matmul(psA[:, h, P:ZW], Q[:, h, P:SEQ], K[:, h, 0:SEQ], start=True, stop=True)
                t.done(last, "z")
                rows("kn", K, i)
                pe.wait_ge(s_in["kv"], 16 * i + 16)
                s.wait(pe, "kn", i)
                rows("vn", V, i)
                s.wait(pe, "att", i)
                for h in range(HG):
                    for j, c0 in enumerate((0, P, 2 * P)):
                        last = pe.transpose(psA[:, h, c0:c0 + P], att[:, h, c0:c0 + P], c_.ident[:])
                t.done(last, "attT")
                s.wait(pe, "vn", i)
                s.wait(pe, "attT", i)
                for h in range(HG):
                    pe.matmul(psB[:, h, 0:P], vn[:, h, 0], attT[:, h, 0:P], start=True, stop=True)
                    pe.matmul(psB[:, h, P:SEQ], vn[:, h, 0], attT[:, h, P:2 * P], start=True, stop=False)
                    last = pe.matmul(psB[:, h, P:SEQ], vn[:, h, 1], attT[:, h, 2 * P:ZW], start=False, stop=True)
                t.done(last, "o")


def closing(nc, c_, a):
    with ExitStack() as ctx:
        weight_buffers(nc, ctx, c_)
        split_buffers(nc, ctx, c_)
        yn = ctx.enter_context(nc.sbuf_tensor("yn", [P, 3, D], F32))
        c_.psN = ctx.enter_context(nc.psum_tensor(c_.name("psN"), [P, 512], F32))
        psT = ctx.enter_context(nc.psum_tensor("out_ps", [P, 3, 512], F32))
        res_in, turned, out_ready, y_stored = (ctx.enter_context(nc.semaphore(x)) for x in
                                               ("res_in", "turned", "out_ready", "y_stored"))
        y_ready = ctx.enter_context(nc.semaphore("y_ready"))
        bo = PB["bo"]
        block = ctx.enter_context(nc.Block())

        @block.sync
        def _(sp):
            load_group(c_, sp, bo, 0, None)
            sp.wait_ge(c_.x_ready, 28)
            sp.dma_start(c_.resT[:], c_.res_spill.rearrange("m p t -> p m t")).then_inc(res_in, 16)
            sp_projection(c_, sp, bo, None, first_store=True)
            sp.wait_ge(out_ready, NM)
            for tt in range(2):
                sp.dma_start(a["o_y_p"][0, tt * P:(tt + 1) * P], yn[:, tt]).then_inc(y_stored, 16)
            sp.dma_start(a["o_y_s"].rearrange("b t d -> (b t) d"), yn[0:NB * TS, 2]).then_inc(y_stored, 16)
            sp.wait_ge(y_stored, 48)

        @block.tensor
        def _(pe):
            pe_projection(c_, pe, bo, 24)
            norm_sum_pe(c_, pe, 2)
            for m in range(NM):
                pe.wait_ge(y_ready, m + 1)
                if m >= 3:
                    pe.wait_ge(out_ready, m - 2)
                for tt in range(3):
                    n = P if tt < 2 else NB * TS
                    last = pe.transpose(psT[0:n, m % 3, tt * P:(tt + 1) * P], c_.yT[:, m, tt * P:tt * P + n],
                                        c_.ident[:])
                last.then_inc(turned, 1)

        @block.scalar
        def _(act):
            for q in range(4):
                act.activation(c_.xhi[:, 4 * q:4 * q + 4], c_.yT[:, 4 * q:4 * q + 4], ACT.Copy).then_inc(c_.xhi_ready, 1)
            act_projection(c_, act, bo, None)
            act.wait_ge(c_.evacuated, 4 * (4 * bo + 4) + LEAD)
            norm_squares_act(c_, act, 2)
            norm_rsqrt_act(c_, act, 2)
            for m in range(NM):
                act.wait_ge(turned, m + 1)
                act.activation(yn[:, 0:2, m * P:(m + 1) * P],
                               psT[:, m % 3, 0:2 * P].rearrange("p (t c) -> p t c", t=2), ACT.Copy)
                act.activation(yn[0:64, 2, m * P:(m + 1) * P], psT[0:64, m % 3, 2 * P:3 * P],
                               ACT.Copy).then_inc(out_ready, 1)

        @block.vector
        def _(dve):
            for q in range(4):
                dve.wait_ge(c_.xhi_ready, 24 + q + 1)
                dve.tensor_tensor(c_.xlo[:, 4 * q:4 * q + 4], c_.yT[:, 4 * q:4 * q + 4],
                                  c_.xhi[:, 4 * q:4 * q + 4], ALU.subtract).then_inc(c_.x_ready, 1)
            dve.wait_ge(res_in, 16)
            dve_projection(c_, dve, bo, None)
            dve_evacuate(c_, dve, bo, 4 * bo + 3, 3)
            dve.wait_ge(c_.rs_ready, 3)
            src = normed(c_, "final_norm")
            for m in range(NM):
                src(dve, c_.yT[:, m], m).then_inc(y_ready, 1)


KB = 4
NBLK = NPAGE // KB
BK = KB * PAGE
NQ = NBLK * 4
NEW = NB * TS
LAG = 6
LAST = NQ + LAG + 1


def sample_attention(nc, c_, a):
    with ExitStack() as ctx:
        def sb(name, shape, dt=F32):
            return ctx.enter_context(nc.sbuf_tensor("sa_" + name, shape, dt))

        def sem(name):
            return ctx.enter_context(nc.semaphore("sa_" + name))

        kraw, vraw = sb("kraw", [P, 4, KB, 512]), sb("vraw", [P, 4, KB, 512])
        vhi, vlo = sb("vhi", [P, 2, KB, 512], F32R), sb("vlo", [P, 2, KB, 512], F32R)
        khi, klo = sb("khi", [P, 2, BK], F32R), sb("klo", [P, 2, BK], F32R)
        qp = sb("qp", [P, 2, 8 * 136], F32R)
        z, w, sps, rc, att = (sb(x, [P, BK]) for x in ("z", "w", "sps", "rc", "att"))
        moved = sb("moved", [P, BK])
        carry, onesz = sb("carry", [P, 1]), sb("onesz", [P, BK])
        st, st_new = sb("st", [P, 2, KB, 2, P], F32R), sb("st_new", [NEW, 2, P], F32R)
        osb = sb("osb", [P, 4, 512])
        vn_raw = osb[0:NEW].rearrange("k g c -> k (g c)")
        vn_hi, vn_lo = sb("vn_hi", [NEW, D], F32R), sb("vn_lo", [NEW, D], F32R)
        mask, mask8 = sb("mask", [P, NB, NEW]), sb("mask8", [P, TS])
        spread, tri = sb("spread", [TS, P]), sb("tri", [TS, TS])
        I2 = sb("I2", [P, 64])
        pt = sb("pt", [1, NB * NPAGE], I32)
        psO = ctx.enter_context(nc.psum_tensor("sa_psO", [P, 4, 512], F32))
        psS = ctx.enter_context(nc.psum_tensor("sa_psS", [P, 2, 512], F32))
        psT = ctx.enter_context(nc.psum_tensor("sa_psT", [P, 2, 512], F32))

        k_in, v_in = [sem(f"k_in{q}") for q in range(4)], [sem(f"v_in{q}") for q in range(4)]
        pt_in, vn_in, made, mask_mm, mask_out = (sem(x) for x in ("pt_in", "vn_in", "made", "mask_mm", "mask_out"))
        vn_hi_ready, vn_lo_ready = sem("vn_hi_ready"), sem("vn_lo_ready")
        keys_turned, keys_hi, keys_lo, keys_scored = (sem(x) for x in ("keys_turned", "keys_hi", "keys_lo", "keys_scored"))
        qp_hi, qp_lo = sem("qp_hi"), sem("qp_lo")
        new_scored = sem("new_scored")
        half_moved, z_ready = sem("half_moved"), sem("z_ready")
        abs_ready, exp_ready, ln_ready, sp_ready = (sem(x) for x in ("abs", "exp", "ln", "sp"))
        rc_ready, carry_ready, arg_ready, att_ready = (sem(x) for x in ("rc", "carry", "arg", "att"))
        new_z = sem("new_z")
        att_turned, st_hi, st_lo = sem("att_turned"), sem("st_hi"), sem("st_lo")
        v_hi, v_lo, values_used = sem("v_hi"), sem("v_lo"), sem("values_used")
        o_copied, final_summed, final_out = sem("o_copied"), sem("final_summed"), sem("final_out")
        passed_sp, passed_pe = sem("passed_sp"), sem("passed_pe")
        n_made = [0]

        def chain(b, c, k=1):
            return 5 * k * b + k * c

        def clocks(b, n, old):
            return ([(old, n + NQ)] if old is not None and n + NQ <= LAST else []) + ([(b, n)] if b is not None else [])

        def sequence(slot):
            def run(eng):
                for n in range(NQ):
                    slot(0, n, None)
                with eng.Fori(1, NB) as b:
                    for n in range(NQ):
                        slot(b, n, b - 1)
                for n in range(LAST - NQ + 1):
                    slot(None, n, NB - 1)
            return run

        def step_kind(m):
            out = set()
            if m == 2:
                out |= {"new_scores"}
            if m == 3:
                out |= {"att0"}
            for s in range(NBLK):
                if m == 4 * s + 3:
                    out |= {f"zA{s + 1}"}
                if m == 4 * s + 4:
                    out |= {f"zB{s + 1}"}
                if m == 4 * s + 5:
                    out |= {f"att{s + 1}"}
            if LAST - 1 <= m <= LAST:
                out |= {f"final{m - (LAST - 1)}"}
            if LAST - 4 <= m < LAST:
                out |= {f"copy{m - (LAST - 4)}"}
            return out

        def split_of(b, n, old):
            return (b, n - LAG + 1) if n >= LAG - 1 else (old, n + NQ - LAG + 1)

        block = ctx.enter_context(nc.Block())

        @block.sync
        def _(sp):
            sp.dma_start(pt[:], a["page_table"].rearrange("(o b) n -> o (b n)", o=1)).then_inc(pt_in, 16)
            sp.dma_start(vn_raw, a["o_v_s"].rearrange("b t h d -> (b t) (h d)")).then_inc(vn_in, 16)
            sp.wait_ge(pt_in, 16)

            def load(ring, name, arrived, b, n):
                s, gg = n // 4, n % 4
                sp.sem_inc(passed_sp, 1)
                for pg in range(KB):
                    col = KB * (NBLK - 1 - s) + pg
                    page = sp.value_load(pt[0:1, bass.ds(NPAGE * b + col, 1)])
                    src = a[name][bass.ds(page, 1), :, 4 * gg:4 * gg + 4, :].rearrange("o s h d -> (o s) (h d)")
                    sp.dma_start(ring[:, gg, pg], src).then_inc(arrived[gg], 16)

            def slot(b, n, old):
                if b is not None:
                    if not (isinstance(b, int) and 4 * n < 16):
                        sp.wait_ge(keys_turned, 64 * b + 4 * n - 12)
                    load(kraw, "cache_k", k_in, b, n)
                vb, p = (b, n - 4) if n >= 4 else (old, n + 12)
                if vb is not None:
                    if not (isinstance(vb, int) and vb == 0 and p < 4):
                        sp.wait_ge(v_lo, 32 * vb + 2 * p - 6)
                    load(vraw, "cache_v", v_in, vb, p)

            for n in range(NQ):
                slot(0, n, None)
            with sp.Fori(1, NB) as b:
                for n in range(NQ):
                    slot(b, n, b - 1)
            for n in range(4):
                slot(None, n, NB - 1)

        @block.gpsimd
        def _(pool):
            def step(ins_):
                n_made[0] += 1
                ins_.then_inc(made, 1)
                pool.wait_ge(made, n_made[0])

            step(pool.memset(onesz[:], 1.0))
            for g in range(2):
                step(pool.memset(qp[:, g].bitcast(F32), 0.0))
                step(pool.tensor_copy(I2[64 * g:64 * g + 64, :], c_.ident[64 * g:64 * g + 64, 64 * g:64 * g + 64]))
            step(pool.memset(tri[:], 0.0))
            step(pool.affine_select(out=tri[:], in_=tri[:], compare_op=ALU.is_gt, fill=MASKED, base=0,
                                    pattern=[[-1, TS]], channel_multiplier=1))
            step(pool.memset(spread[:], 0.0))
            step(pool.affine_select(out=spread[:].rearrange("q (h r) -> q h r", r=TS),
                                    in_=spread[:].rearrange("q (h r) -> q h r", r=TS),
                                    compare_op=ALU.not_equal, fill=1.0, base=0,
                                    pattern=[[0, NHB], [1, TS]], channel_multiplier=-1))
            step(pool.memset(mask[:], MASKED))
            pool.wait_ge(mask_out, 1)
            for b in range(NB):
                step(pool.tensor_copy(mask[:, b, TS * b:TS * b + TS], mask8[:]))

            def slot(b, n, old):
                vb, p = split_of(b, n, old)
                if vb is None:
                    return
                for hf in range(2):
                    pool.wait_ge(v_hi, 64 * vb + 4 * p + 2 * hf + 2)
                    r = slice(2 * hf, 2 * hf + 2)
                    pool.tensor_tensor(vlo[:, p % 2, r], vraw[:, p % 4, r], vhi[:, p % 2, r],
                                       ALU.subtract).then_inc(v_lo, 1)

            sequence(slot)(pool)

        def half_source(b, c, half, rows):
            if c == 0:
                return psT[rows, plan[window_of(b)]["new_scores"], NEW * half:NEW * half + NEW]
            return psS[rows, half, :]

        def width(c):
            return NEW if c == 0 else BK

        plan = turn_plan(step_kind)

        def bank(b, x):
            return plan[window_of(b)]["key", x]

        def turned_weights(b, x):
            c, bank_ = int(x[3]), plan[window_of(b)][x]
            if c == 0:
                out = st_new[:, :, 0:64], st_new[:, :, 64:128]
                return out, psT[0:NEW, bank_, 0:P].rearrange("k (g r) -> k g r", g=2)
            out = st[:, c % 2, :, :, 0:64], st[:, c % 2, :, :, 64:128]
            return out, psT[:, bank_, :].rearrange("k (t g r) -> k t g r", t=KB, g=2)

        def qp_view(g, part):
            return qp[:, g].rearrange("p (i x) -> p i x", x=136)[:, :, 64 * part:64 * part + TS]

        @block.scalar
        def _(act):
            act.preload_act_table_set("natural_log_exp_and_others")
            act.wait_ge(vn_in, 16)
            act.activation(vn_hi[:], vn_raw, ACT.Copy).then_inc(vn_hi_ready, 1)
            act.wait_ge(made, 5)

            def keys(b, x):
                act.wait_ge(keys_turned, 64 * b + x + 1)
                if not (isinstance(b, int) and x < 2):
                    act.wait_ge(keys_scored, 64 * b + x - 1)
                act.activation(khi[:, x % 2], psT[:, bank(b, x)], ACT.Copy).then_inc(keys_hi, 1)

            def move(b, c, half):
                if c == 0:
                    act.wait_ge(new_scored, b + 1)
                else:
                    act.wait_ge(keys_scored, 64 * b + 16 * (c - 1) + 8 * half + 8)
                if c > 0 or not (isinstance(b, int) and b == 0):
                    act.wait_ge(z_ready, chain(b, c, 2) - 1 + half)
                dst, src = (slice(0, 64), slice(64, 128)) if half == 0 else (slice(64, 128), slice(0, 64))
                act.activation(moved[dst, 0:width(c)], half_source(b, c, half, src),
                               ACT.Copy).then_inc(half_moved, 1)

            def chain_step(b, c, name):
                n = slice(0, width(c))
                if name == "abs":
                    act.wait_ge(z_ready if c else new_z, chain(b, c, 2) + 2 if c else b + 1)
                    act.activation(w[:, n], z[:, n], ACT.Abs).then_inc(abs_ready, 1)
                elif name == "exp":
                    act.wait_ge(abs_ready, chain(b, c) + 1)
                    act.activation(w[:, n], w[:, n], ACT.Exp, scale=-1.0).then_inc(exp_ready, 1)
                elif name == "ln":
                    act.wait_ge(exp_ready, chain(b, c) + 1)
                    act.activation(w[:, n], w[:, n], ACT.Ln, bias=c_.ones[:, 0:1]).then_inc(ln_ready, 1)

            def weights(bb, c):
                act.wait_ge(arg_ready, chain(bb, c) + 1)
                if c or not (isinstance(bb, int) and bb == 0):
                    act.wait_ge(att_turned, chain(bb, c))
                act.activation(att[:, 0:width(c)], z[:, 0:width(c)], ACT.Exp).then_inc(att_ready, 1)

            def weights_high(b, bb, x):
                c = int(x[3])
                act.wait_ge(att_turned, chain(bb, c) + 1)
                if c == 0:
                    if not isinstance(bb, int):
                        act.wait_ge(values_used, 16 * bb - 12)
                elif c > 2 or not isinstance(bb, int):
                    act.wait_ge(values_used, 16 * bb + 4 * c - 8)
                out, src = turned_weights(b, x)
                act.activation(out[0], src, ACT.Copy).then_inc(st_hi, 1)

            def queries(b, old):
                if old is not None:
                    act.wait_ge(keys_scored, 64 * b)
                for g in range(2):
                    ins_ = act.activation(qp_view(g, 0), c_.qS[:, 8 * g:8 * g + 8, bass.ds(TS * b, TS)], ACT.Copy)
                ins_.then_inc(qp_hi, 1)

            def slot(b, n, old):
                steps = [(bb, x) for bb, m in clocks(b, n, old) for x in sorted(step_kind(m))]
                chains = [(bb, int(x[2])) for bb, x in steps if x[:2] == "zB"]
                new = [bb for bb, x in steps if x == "new_scores"]
                vb, p = split_of(b, n, old)
                if vb is not None:
                    act.wait_ge(v_in[p % 4], 64 * (4 * vb + p // 4 + 1))
                for j in range(4):
                    if b is not None:
                        keys(b, 4 * n + j)
                    if j == 0:
                        for bb, x in steps:
                            if x[:3] == "att":
                                weights(bb, int(x[3]))
                        if b is not None and n == 0:
                            queries(b, old)
                        for bb, x in steps:
                            if x[0] == "z":
                                move(bb, int(x[2]), 0 if x[1] == "A" else 1)
                    if j == 1:
                        for bb, x in steps:
                            if x[:3] == "att":
                                weights_high(b, bb, x)
                    for bb, c in chains:
                        if j >= 1:
                            chain_step(bb, c, ("abs", "exp", "ln")[j - 1])
                    for bb in new:
                        if j == 1:
                            move(bb, 0, 0)
                            move(bb, 0, 1)
                        if j == 2:
                            chain_step(bb, 0, "abs")
                        if j == 3:
                            chain_step(bb, 0, "exp")
                            chain_step(bb, 0, "ln")
                    if vb is not None:
                        if j == 0 and not (isinstance(vb, int) and vb == 0 and p < 2):
                            act.wait_ge(values_used, 16 * vb + p - 1)
                        act.activation(vhi[:, p % 2, j], vraw[:, p % 4, j], ACT.Copy).then_inc(v_hi, 1)

            sequence(slot)(act)

        @block.vector
        def _(dve):
            dve.wait_ge(mask_mm, 1)
            dve.tensor_copy(mask8[:], psT[:, 0, 0:TS]).then_inc(mask_out, 1)
            dve.wait_ge(vn_hi_ready, 1)
            dve.tensor_tensor(vn_lo[:], vn_raw, vn_hi[:], ALU.subtract).then_inc(vn_lo_ready, 1)
            dve.wait_ge(made, n_made[0])

            def keys(b, x):
                dve.wait_ge(keys_hi, 64 * b + x + 1)
                dve.tensor_tensor(klo[:, x % 2], psT[:, bank(b, x)], khi[:, x % 2],
                                  ALU.subtract).then_inc(keys_lo, 1)

            def z_half(b, c, half):
                dve.wait_ge(half_moved, chain(b, c, 2) + (half + 1 if c else 2))
                if c > 0 or not (isinstance(b, int) and b == 0):
                    dve.wait_ge(att_ready, chain(b, c))
                r = slice(64 * half, 64 * half + 64)
                dve.scalar_tensor_tensor(out=z[r, 0:width(c)], in0=half_source(b, c, half, r),
                                         scalar=c_.biasQ[r, 0:1], in1=moved[r, 0:width(c)], op0=ALU.add,
                                         op1=ALU.add).then_inc(z_ready, 1)

            def chain_rest(b, c):
                n = slice(0, width(c))
                dve.wait_ge(ln_ready, chain(b, c) + 1)
                dve.scalar_tensor_tensor(out=sps[:, n], in0=z[:, n], scalar=0.0, in1=w[:, n], op0=ALU.max,
                                         op1=ALU.add).then_inc(sp_ready, 1)
                dve.wait_ge(sp_ready, chain(b, c) + 1)
                last = width(c) - 1
                if c:
                    dve.wait_ge(carry_ready, chain(b, c))
                dve.tensor_tensor_scan(out=rc[:, last::-1], data0=onesz[:, n], data1=sps[:, last::-1],
                                       initial=0.0 if c == 0 else carry[:, 0:1], op0=ALU.mult,
                                       op1=ALU.add).then_inc(rc_ready, 1)
                dve.wait_ge(rc_ready, chain(b, c) + 1)
                dve.tensor_copy(carry[:], rc[:, 0:1]).then_inc(carry_ready, 1)
                dve.tensor_tensor(z[:, n], z[:, n], rc[:, n], ALU.subtract).then_inc(arg_ready, 1)

            def slot(b, n, old):
                steps = [(bb, x) for bb, m in clocks(b, n, old) for x in sorted(step_kind(m))]
                for bb, x in steps:
                    if x[:4] == "copy":
                        gg = int(x[4])
                        dve.wait_ge(values_used, 16 * bb + 12 + gg + 1)
                        dve.tensor_copy(osb[:, gg], psO[:, gg]).then_inc(o_copied, 1)
                for j in range(4):
                    if b is not None:
                        keys(b, 4 * n + j)
                    if j == 0:
                        if b is not None and n == 0:
                            dve.wait_ge(qp_hi, b + 1)
                            for g in range(2):
                                ins_ = dve.tensor_tensor(qp_view(g, 1), c_.qS[:, 8 * g:8 * g + 8, bass.ds(TS * b, TS)],
                                                         qp_view(g, 0), ALU.subtract)
                            ins_.then_inc(qp_lo, 1)
                        for bb, x in steps:
                            if x[0] == "z":
                                z_half(bb, int(x[2]), 0 if x[1] == "A" else 1)
                    if j != 1:
                        continue
                    for bb, x in steps:
                        if x == "new_scores":
                            z_half(bb, 0, 0)
                            z_half(bb, 0, 1)
                            dve.wait_ge(z_ready, chain(bb, 0, 2) + 2)
                            dve.tensor_tensor(z[:, 0:NEW], z[:, 0:NEW],
                                              mask[:, bass.ds(bb, 1), :].rearrange("p o k -> p (o k)"),
                                              ALU.add).then_inc(new_z, 1)
                        if x[:3] == "att":
                            dve.wait_ge(st_hi, chain(bb, int(x[3])) + 1)
                            out, src = turned_weights(b, x)
                            dve.tensor_tensor(out[1], src, out[0], ALU.subtract).then_inc(st_lo, 1)
                        if x[:5] == "final":
                            f = int(x[5])
                            dve.wait_ge(final_summed, 2 * bb + f + 1)
                            h = slice(8 * f, 8 * f + 8)
                            dve.tensor_tensor(c_.yT[:, h, bass.ds(SEQ + TS * bb, TS)],
                                              psT[:, plan[window_of(b)][x], 0:64].rearrange("p (h q) -> p h q", h=8),
                                              c_.gS[:, h, bass.ds(TS * bb, TS)], ALU.mult).then_inc(final_out, 1)
                for bb, x in steps:
                    if x == "new_scores":
                        chain_rest(bb, 0)
                    if x[:2] == "zB":
                        chain_rest(bb, int(x[2]))

            sequence(slot)(dve)

        @block.tensor
        def _(pe):
            pe.wait_ge(made, 9)
            pe.matmul(psT[:, 0, 0:TS], spread[:], tri[:], start=True, stop=True).then_inc(mask_mm, 1)
            pe.wait_ge(mask_out, 1)
            pe.wait_ge(made, n_made[0])
            pe.wait_ge(vn_lo_ready, 1)
            user = [None, None]
            turn = [1]

            def take_bank(sem_, per, k, b):
                t = turn[0] % 2
                turn[0] += 1
                if user[t] is not None:
                    s_, per_, k_, b_ = user[t]
                    pe.wait_ge(s_, per_ * b_ + k_)
                user[t] = (sem_, per, k, b)
                return t

            def turn_keys(b, x):
                gg, j = (x // 4) % 4, x % 4
                if j == 0:
                    pe.wait_ge(k_in[gg], 64 * (4 * b + x // 16 + 1))
                t = take_bank(keys_lo, 64, x + 1, b)
                assert t == bank(b, x)
                for pg in range(KB):
                    last = pe.transpose(psT[:, t, pg * P:(pg + 1) * P], kraw[:, gg, pg, j * P:(j + 1) * P],
                                        c_.ident[:])
                last.then_inc(keys_turned, 1)

            def score(b, x):
                s, gg, j = x // 16, (x // 4) % 4, x % 4
                half, i = gg // 2, 4 * (gg % 2) + j
                pe.wait_ge(keys_lo, 64 * b + x + 1)
                if x == 0:
                    pe.wait_ge(qp_lo, b + 1)
                if i == 0:
                    c = s + 1
                    if s > 0 or not (isinstance(b, int) and b == 0):
                        pe.wait_ge(z_ready, chain(b, c, 2) + half - 1 if s > 0 else 10 * b - 1 + half)
                lhs = qp[:, half, i * P:(i + 1) * P]
                pe.matmul(psS[:, half, :], lhs, khi[:, x % 2], start=(i == 0), stop=False)
                pe.matmul(psS[:, half, :], lhs, klo[:, x % 2], start=False, stop=(i == 7)).then_inc(keys_scored, 1)

            def extra(b, bb, x):
                if x == "new_scores":
                    t = take_bank(new_z, 1, 1, bb)
                    assert t == plan[window_of(b)][x]
                    for half in range(2):
                        for i in range(8):
                            lhs = qp[:, half, i * P:(i + 1) * P]
                            out = psT[:, t, NEW * half:NEW * half + NEW]
                            pe.matmul(out, lhs, c_.kNh[:, 8 * half + i], start=(i == 0), stop=False)
                            last = pe.matmul(out, lhs, c_.kNl[:, 8 * half + i], start=False, stop=(i == 7))
                    last.then_inc(new_scored, 1)
                elif x[:3] == "att":
                    c = int(x[3])
                    t = take_bank(st_lo, 5, c + 1, bb)
                    assert t == plan[window_of(b)][x]
                    pe.wait_ge(att_ready, chain(bb, c) + 1)
                    if c == 0:
                        pe.sem_inc(passed_pe, 1)
                        last = pe.transpose(psT[0:NEW, t, 0:P], att[:, 0:NEW], c_.ident[:])
                    else:
                        for pg in range(KB):
                            last = pe.transpose(psT[:, t, pg * P:(pg + 1) * P], att[:, pg * P:(pg + 1) * P],
                                                c_.ident[:])
                    last.then_inc(att_turned, 1)
                elif x[:5] == "final":
                    f = int(x[5])
                    t = take_bank(final_out, 2, f + 1, bb)
                    assert t == plan[window_of(b)][x]
                    pe.wait_ge(o_copied, 4 * bb + 2 * f + 2)
                    for i in range(8):
                        h = 8 * f + i
                        last = pe.matmul(psT[:, t, i * TS:(i + 1) * TS], osb[:, h // 4, (h % 4) * P:(h % 4 + 1) * P],
                                         I2[:, i * TS:(i + 1) * TS], start=True, stop=True)
                    last.then_inc(final_summed, 1)

            def values(b, p, pg):
                gg, c = p % 4, p // 4 + 1
                half = gg // 2
                if p < 4 and pg == 0:
                    pe.wait_ge(st_lo, chain(b, 0) + 1)
                    if not (isinstance(b, int) and b == 0):
                        pe.wait_ge(o_copied, 4 * b - 3 + gg)
                    for j, x in enumerate((vn_hi, vn_lo)):
                        pe.matmul(psO[:, gg], st_new[:, half, :], x[:, 512 * gg:512 * gg + 512],
                                  start=(j == 0), stop=False)
                if pg == 0:
                    pe.wait_ge(st_lo, chain(b, c) + 1)
                if pg % 2 == 0:
                    pe.wait_ge(v_lo, 32 * b + 2 * p + 1 + pg // 2)
                for j, x in enumerate((vhi, vlo)):
                    last = pe.matmul(psO[:, gg], st[:, c % 2, pg, half, :], x[:, p % 2, pg], start=False,
                                     stop=(p >= 12 and pg == KB - 1 and j == 1))
                if pg == KB - 1:
                    last.then_inc(values_used, 1)

            def slot(b, n, old):
                steps = [(bb, x) for bb, m in clocks(b, n, old) for x in sorted(step_kind(m))]
                vb, p = (b, n - LAG) if n >= LAG else (old, n + NQ - LAG)
                for j in range(4):
                    if b is not None:
                        turn_keys(b, 4 * n + j)
                    if vb is not None:
                        values(vb, p, j)
                    x = 4 * n + j - 1
                    if x >= 0:
                        if b is not None:
                            score(b, x)
                    elif old is not None:
                        score(old, x + 64)
                    if j == 1:
                        for bb, x in steps:
                            extra(b, bb, x)

            for n in range(NQ):
                slot(0, n, None)
            with pe.Fori(1, NB) as b:
                user[:] = [(s_, per, k, b - 1) for s_, per, k, _ in user]
                for n in range(NQ):
                    slot(b, n, b - 1)
            user[:] = [(s_, per, k, NB - 1) for s_, per, k, _ in user]
            for n in range(LAST - NQ + 1):
                slot(None, n, NB - 1)


def turn_plan(step_kind):
    plans = {}
    for window, start in (("first", 1), ("loop", 0), ("rest", 0)):
        plan, t = {}, start
        for n in range(NQ):
            if window != "rest":
                plan["key", 4 * n], plan["key", 4 * n + 1] = t % 2, (t + 1) % 2
                t += 2
            for m in {"first": (n,), "loop": (n + NQ, n), "rest": (n + NQ,)}[window]:
                for x in sorted(step_kind(m)):
                    if x == "new_scores" or x[:3] == "att" or x[:5] == "final":
                        plan[x] = t % 2
                        t += 1
            if window != "rest":
                plan["key", 4 * n + 2], plan["key", 4 * n + 3] = t % 2, (t + 1) % 2
                t += 2
        assert window == "rest" or t % 2 == 0
        plans[window] = plan
    return plans


def window_of(b):
    return "rest" if b is None else "first" if isinstance(b, int) else "loop"


def program(nc, a):
    c_ = Core()
    with ExitStack() as ctx:
        def sb(name, shape, dt=F32):
            return ctx.enter_context(nc.sbuf_tensor(name, shape, dt))

        def sem(name):
            return ctx.enter_context(nc.semaphore(name))

        used = set()

        def name(x):
            while x in used:
                x += "_"
            used.add(x)
            return x

        c_.name = name
        c_.W = {"r": a["a_w_rkvg"][0, 0], "k": a["a_w_rkvg"][0, 1], "v": a["a_w_rkvg"][0, 2],
                "g": a["a_w_rkvg"][0, 3], "wo": a["a_w_o"][0], "kk": a["w_kv"][:, 0:D],
                "kv": a["w_kv"][:, D:2 * D], "q": a["b_w_qg"][0][:, 0:D],
                "g2": a["b_w_qg"][0][:, D:2 * D], "bo": a["b_w_o"][0]}
        c_.spill = nc.dram_tensor("spill", [len(SPILL), NM, P, TOK], F32, kind="Internal").ap()
        c_.res_spill = nc.dram_tensor("res_spill", [NM, P, TOK], F32, kind="Internal").ap()
        c_.ident = sb("ident", [P, P])
        c_.ones = sb("ones", [P, P])
        c_.consts = sb("consts", [P, 4])
        c_.vec = sb("vec", [P, 3 * P])
        c_.resT = sb("resT", [P, NM, TOK])
        c_.wlo_ready = sem("wlo_ready")
        c_.whi_ready = sem("whi_ready")
        c_.evacuated = sem("evacuated")
        c_.stored = sem("stored")
        c_.bank_full = sem("bank_full")
        c_.chunk_used = sem("chunk_used")
        c_.sig_ready = sem("sig_ready")
        c_.xtmp_ready = sem("xtmp_ready")
        c_.xhi_ready = sem("xhi_ready")
        c_.x_ready = sem("x_ready")
        c_.sq_ready = sem("sq_ready")
        c_.sq_summed = sem("sq_summed")
        c_.ln_ready = sem("ln_ready")
        c_.rs_ready = sem("rs_ready")
        c_.w_in = [sem(f"w_in{q}") for q in range(4)]
        with ExitStack() as ch:
            weight_buffers(nc, ch, c_)
            c_.hT = ch.enter_context(nc.sbuf_tensor("hT", [P, NM, TOK], F32))
            c_.delta = ch.enter_context(nc.sbuf_tensor("delta", [P, NM, TOK], F32))
            opening(nc, c_, a)
            x_buffers(nc, ch, c_)
            mixing_projections(nc, c_, a)
        with ExitStack() as cx:
            x_buffers(nc, cx, c_)
            recurrence(nc, c_, a)
            weight_buffers(nc, cx, c_)
            middle(nc, c_, a)
        c_.yT = c_.resT
        with ExitStack() as ca:
            c_.qS = ca.enter_context(nc.sbuf_tensor("qS", [P, NHB, NB * TS], F32))
            c_.gS = ca.enter_context(nc.sbuf_tensor("gS", [P, NHB, NB * TS], F32))
            c_.kNh = ca.enter_context(nc.sbuf_tensor("kNh", [P, NHB, NB * TS], F32R))
            c_.kNl = ca.enter_context(nc.sbuf_tensor("kNl", [P, NHB, NB * TS], F32R))
            c_.biasQ = ca.enter_context(nc.sbuf_tensor("biasQ", [P, 1], F32))
            prompt_attention(nc, c_, a)
            sample_attention(nc, c_, a)
        x_buffers(nc, ctx, c_)
        closing(nc, c_, a)


OUTS = (("o_y_p", (1, SEQ, D)), ("o_y_s", (NB, TS, D)), ("o_shift_p", (1, 1, D)),
        ("o_wkv_p", (1, 1, D // HS, HS, HS)), ("o_k_p", (1, SEQ, NHB, DH)), ("o_v_p", (1, SEQ, NHB, DH)),
        ("o_shift_s", (1, NB, D)), ("o_wkv_s", (1, NB, D // HS, HS, HS)),
        ("o_k_s", (NB, TS, NHB, DH)), ("o_v_s", (NB, TS, NHB, DH)))


def vector_views(a):
    for i in range(6):
        a[f"mu{i}"] = a["a_mu"][0, i]
    for x in ("w0", "a0", "k_k", "k_a", "lnx_g", "lnx_b"):
        a[x] = a["a_" + x][0]
    for x in ("a_norm", "b_norm"):
        a[x] = a[x][0]
    a["r_k"] = a["a_r_k"][0].rearrange("h n -> (h n)")


def kernel(**inputs):
    import numpy as np
    import concourse.bacc as bacc
    from concourse.bass_utils import run_bass_kernel_spmd

    nc = bacc.Bacc("TRN2", target_bir_lowering=False, num_devices=1)
    a, arrays = {}, {}
    for name, value in inputs.items():
        arrays["in_" + name] = np.ascontiguousarray(value)
        a[name] = nc.dram_tensor("in_" + name, arrays["in_" + name].shape,
                                 mybir.dt.from_np(arrays["in_" + name].dtype), kind="ExternalInput").ap()
    for name, shape in OUTS:
        a[name] = nc.dram_tensor(name, shape, F32, kind="ExternalOutput").ap()
    vector_views(a)
    program(nc, a)
    r = run_bass_kernel_spmd(nc, [arrays], core_ids=[0])
    return tuple(r.results[0][name] for name, _ in OUTS)
```
